# Optimizing a Trainium2 kernel written in Bass

```python
import math
import jax, jax.numpy as jnp
from jax import lax
import numpy as np

D_MODEL = 1024
BATCH = 1
SEQ = 256
DEPTH = 2

N_MIXERS = 3
D_FF = 2816
RMS_EPS = 1e-6
S5_WIDTH = D_MODEL
S5_GROUP = 16
S5_GROUPS = S5_WIDTH // S5_GROUP
S5_STATE = 64
S5_CHUNK = 128
S5_DT_MIN = 1e-3
S5_DT_MAX = 1e-1
SB_HEAD_DIM = 64
SB_HEADS = D_MODEL // SB_HEAD_DIM
SB_BLOCK = 128
LRU_WIDTH = D_MODEL
LRU_BLOCK_WIDTH = 256
LRU_BLOCKS = LRU_WIDTH // LRU_BLOCK_WIDTH
LRU_CONV = 4
LRU_C = 8.0
N_S5 = len(range(0, DEPTH, N_MIXERS))
N_SB = len(range(1, DEPTH, N_MIXERS))
N_LRU = len(range(2, DEPTH, N_MIXERS))

kernel_name = "hybrid_s5_stickbreak_rglru_macaron"

def rms_norm(x, g):
    xf = x.astype(jnp.float32)
    y = xf * lax.rsqrt(jnp.mean(xf * xf, axis=-1, keepdims=True) + RMS_EPS)
    return (y * g.astype(jnp.float32)).astype(x.dtype)

def swiglu_ffn(h, w_in, w_out):
    gate, up = jnp.split(h @ w_in, 2, axis=-1)
    return (jax.nn.silu(gate) * up) @ w_out

def _linear_recurrence_op(left, right):
    a_l, b_l = left
    a_r, b_r = right
    return a_r * a_l, a_r * b_l + b_r

def s5_mixer(h, w_in, lam_re, lam_im, log_dt, b_re, b_im, c_re, c_im, d_skip, w_out):
    f32 = jnp.float32
    bsz, seq, _ = h.shape
    u = (h @ w_in).astype(f32)
    lam = lax.complex(lam_re.astype(f32), lam_im.astype(f32))
    lam_dt = lam * jnp.exp(log_dt.astype(f32))[:, None]
    lam_bar = jnp.exp(lam_dt)
    b_bar = ((lam_bar - 1.0) / lam)[:, :, None] * lax.complex(b_re.astype(f32), b_im.astype(f32))
    c = lax.complex(c_re.astype(f32), c_im.astype(f32))
    decay_pow = jnp.exp(lam_dt[None] * jnp.arange(1, S5_CHUNK + 1, dtype=f32)[:, None, None])
    n_chunks = seq // S5_CHUNK
    u_blocks = u.reshape(bsz, n_chunks, S5_CHUNK, S5_GROUPS, S5_GROUP).transpose(1, 0, 2, 3, 4)
    a_elems = jnp.broadcast_to(lam_bar, (bsz, S5_CHUNK, S5_GROUPS, S5_STATE))

    def chunk_step(state, u_blk):
        bu = jnp.einsum('gph,btgh->btgp', b_bar, u_blk.astype(jnp.complex64))
        _, s = lax.associative_scan(_linear_recurrence_op, (a_elems, bu), axis=1)
        s = s + decay_pow[None] * state[:, None]
        y_blk = jnp.einsum('ghp,btgp->btgh', c, s).real
        return s[:, -1], y_blk

    state0 = jnp.zeros((bsz, S5_GROUPS, S5_STATE), jnp.complex64)
    _, y = lax.scan(chunk_step, state0, u_blocks)
    y = y.transpose(1, 0, 2, 3, 4).reshape(bsz, seq, S5_WIDTH) + d_skip.astype(f32) * u
    z = jax.nn.gelu(y).astype(h.dtype)
    val, gate = jnp.split(z @ w_out, 2, axis=-1)
    return val * jax.nn.sigmoid(gate)

def stick_breaking_mixer(h, w_qkv, w_out):
    f32 = jnp.float32
    bsz, seq, _ = h.shape
    qkv = (h @ w_qkv).reshape(bsz, seq, 3, SB_HEADS, SB_HEAD_DIM)
    q = qkv[:, :, 0].astype(f32) * (SB_HEAD_DIM ** -0.5)
    k = qkv[:, :, 1].astype(f32)
    v = qkv[:, :, 2].astype(f32)
    n_blocks = seq // SB_BLOCK
    q_blocks = q.reshape(bsz, n_blocks, SB_BLOCK, SB_HEADS, SB_HEAD_DIM).transpose(1, 0, 2, 3, 4)
    key_pos = jnp.arange(seq)

    def attend(args):
        q_blk, blk = args
        logits = jnp.einsum('bqhd,bkhd->bhqk', q_blk, k)
        query_pos = blk * SB_BLOCK + jnp.arange(SB_BLOCK)
        causal = key_pos[None, :] < query_pos[:, None]
        log_keep = jnp.where(causal, jax.nn.log_sigmoid(-logits), 0.0)
        log_remaining = lax.cumsum(log_keep, axis=3, reverse=True) - log_keep
        weights = jnp.where(causal, jnp.exp(jax.nn.log_sigmoid(logits) + log_remaining), 0.0)
        return jnp.einsum('bhqk,bkhd->bqhd', weights, v)

    o = lax.map(attend, (q_blocks, jnp.arange(n_blocks)))
    o = o.transpose(1, 0, 2, 3, 4).reshape(bsz, seq, D_MODEL).astype(h.dtype)
    return o @ w_out

def rglru_mixer(h, w_in, conv_w, conv_b, w_a, b_a, w_x, b_x, lam, w_out):
    f32 = jnp.float32
    bsz, seq, _ = h.shape
    branch_gelu, branch_rnn = jnp.split(h @ w_in, 2, axis=-1)
    xc = lax.conv_general_dilated(
        branch_rnn, conv_w[:, None, :], window_strides=(1,), padding=[(LRU_CONV - 1, 0)],
        dimension_numbers=('NWC', 'WIO', 'NWC'), feature_group_count=LRU_WIDTH) + conv_b
    xb = xc.reshape(bsz, seq, LRU_BLOCKS, LRU_BLOCK_WIDTH)
    r = jax.nn.sigmoid(jnp.einsum('blnc,ncd->blnd', xb, w_a) + b_a).reshape(bsz, seq, LRU_WIDTH)
    i = jax.nn.sigmoid(jnp.einsum('blnc,ncd->blnd', xb, w_x) + b_x).reshape(bsz, seq, LRU_WIDTH)
    log_a = (-LRU_C * r.astype(f32)) * jax.nn.softplus(-lam.astype(f32))
    a = jnp.exp(log_a)
    gated_x = (i * xc).astype(f32) * jnp.sqrt(-jnp.expm1(2.0 * log_a))
    _, hseq = lax.associative_scan(_linear_recurrence_op, (a, gated_x), axis=1)
    y = (jax.nn.gelu(branch_gelu.astype(f32)) * hseq).astype(h.dtype)
    return y @ w_out

def setup_inputs(seed: int = 0) -> dict:
    key = jax.random.key(seed)
    ks = iter(jax.random.split(key, 40))

    def dense(shape, fan_in):
        return jax.random.normal(next(ks), shape, jnp.float32) * (fan_in ** -0.5)

    def gain(shape):
        return 1.0 + 0.02 * jax.random.normal(next(ks), shape, jnp.float32)

    def small(shape):
        return 0.01 * jax.random.normal(next(ks), shape, jnp.float32)

    x = jax.random.normal(next(ks), (BATCH, SEQ, D_MODEL), jnp.float32)
    inp = {"x": x}
    inp["ffn1_norm"] = gain((DEPTH, D_MODEL))
    inp["ffn1_w_in"] = dense((DEPTH, D_MODEL, 2 * D_FF), D_MODEL)
    inp["ffn1_w_out"] = dense((DEPTH, D_FF, D_MODEL), D_FF)
    inp["mix_norm"] = gain((DEPTH, D_MODEL))
    inp["ffn2_norm"] = gain((DEPTH, D_MODEL))
    inp["ffn2_w_in"] = dense((DEPTH, D_MODEL, 2 * D_FF), D_MODEL)
    inp["ffn2_w_out"] = dense((DEPTH, D_FF, D_MODEL), D_FF)
    inp["final_norm"] = gain((D_MODEL,))
    inp["s5_w_in"] = dense((N_S5, D_MODEL, S5_WIDTH), D_MODEL)
    inp["s5_lam_re"] = -0.5 + small((N_S5, S5_GROUPS, S5_STATE))
    inp["s5_lam_im"] = (math.pi * jnp.arange(S5_STATE, dtype=jnp.float32))[None, None, :] + small((N_S5, S5_GROUPS, S5_STATE))
    inp["s5_log_dt"] = jax.random.uniform(next(ks), (N_S5, S5_GROUPS), jnp.float32,
                                          math.log(S5_DT_MIN), math.log(S5_DT_MAX))
    inp["s5_b_re"] = dense((N_S5, S5_GROUPS, S5_STATE, S5_GROUP), 2 * S5_GROUP)
    inp["s5_b_im"] = dense((N_S5, S5_GROUPS, S5_STATE, S5_GROUP), 2 * S5_GROUP)
    inp["s5_c_re"] = dense((N_S5, S5_GROUPS, S5_GROUP, S5_STATE), S5_STATE)
    inp["s5_c_im"] = dense((N_S5, S5_GROUPS, S5_GROUP, S5_STATE), S5_STATE)
    inp["s5_d"] = jax.random.normal(next(ks), (N_S5, S5_WIDTH), jnp.float32)
    inp["s5_w_out"] = dense((N_S5, S5_WIDTH, 2 * D_MODEL), S5_WIDTH)
    inp["sb_w_qkv"] = dense((N_SB, D_MODEL, 3 * D_MODEL), D_MODEL)
    inp["sb_w_out"] = dense((N_SB, D_MODEL, D_MODEL), D_MODEL)
    inp["lru_w_in"] = dense((N_LRU, D_MODEL, 2 * LRU_WIDTH), D_MODEL)
    inp["lru_conv_w"] = dense((N_LRU, LRU_CONV, LRU_WIDTH), LRU_CONV)
    inp["lru_conv_b"] = small((N_LRU, LRU_WIDTH))
    inp["lru_w_a"] = dense((N_LRU, LRU_BLOCKS, LRU_BLOCK_WIDTH, LRU_BLOCK_WIDTH), LRU_BLOCK_WIDTH)
    inp["lru_b_a"] = small((N_LRU, LRU_BLOCKS, LRU_BLOCK_WIDTH))
    inp["lru_w_x"] = dense((N_LRU, LRU_BLOCKS, LRU_BLOCK_WIDTH, LRU_BLOCK_WIDTH), LRU_BLOCK_WIDTH)
    inp["lru_b_x"] = small((N_LRU, LRU_BLOCKS, LRU_BLOCK_WIDTH))
    a0 = jax.random.uniform(next(ks), (N_LRU, LRU_WIDTH), jnp.float32, 0.9, 0.999)
    p = jnp.exp(jnp.log(a0) / LRU_C)
    inp["lru_lambda"] = jnp.log(p) - jnp.log1p(-p)
    inp["lru_w_out"] = dense((N_LRU, LRU_WIDTH, D_MODEL), LRU_WIDTH)
    return inp

def reference(x, ffn1_norm, ffn1_w_in, ffn1_w_out, mix_norm, ffn2_norm, ffn2_w_in, ffn2_w_out, final_norm,
              s5_w_in, s5_lam_re, s5_lam_im, s5_log_dt, s5_b_re, s5_b_im, s5_c_re, s5_c_im, s5_d, s5_w_out,
              sb_w_qkv, sb_w_out,
              lru_w_in, lru_conv_w, lru_conv_b, lru_w_a, lru_b_a, lru_w_x, lru_b_x, lru_lambda, lru_w_out):
    h = x
    for layer in range(DEPTH):
        h = h + 0.5 * swiglu_ffn(rms_norm(h, ffn1_norm[layer]), ffn1_w_in[layer], ffn1_w_out[layer])
        hn = rms_norm(h, mix_norm[layer])
        kind = layer % N_MIXERS
        j = layer // N_MIXERS
        if kind == 0:
            mixed = s5_mixer(hn, s5_w_in[j], s5_lam_re[j], s5_lam_im[j], s5_log_dt[j], s5_b_re[j], s5_b_im[j],
                             s5_c_re[j], s5_c_im[j], s5_d[j], s5_w_out[j])
        elif kind == 1:
            mixed = stick_breaking_mixer(hn, sb_w_qkv[j], sb_w_out[j])
        else:
            mixed = rglru_mixer(hn, lru_w_in[j], lru_conv_w[j], lru_conv_b[j], lru_w_a[j], lru_b_a[j],
                                lru_w_x[j], lru_b_x[j], lru_lambda[j], lru_w_out[j])
        h = h + mixed
        h = h + 0.5 * swiglu_ffn(rms_norm(h, ffn2_norm[layer]), ffn2_w_in[layer], ffn2_w_out[layer])
    return rms_norm(h, final_norm)


_drawn_inputs = setup_inputs


def setup_inputs(seed=0):
    import zlib

    import numpy as np

    out = dict(_drawn_inputs(seed))
    spreads = {}
    factors = {'ffn1_norm': 4.456,
     'mix_norm': 4.109,
     'ffn2_norm': 5.24,
     'final_norm': 2.991,
     's5_lam_re': 8.0,
     's5_b_re': 2.69,
     's5_b_im': 2.746,
     's5_c_re': 2.687,
     's5_c_im': 2.71}
    for name, (base, spread) in spreads.items():
        noise = np.random.default_rng([zlib.crc32(name.encode()), seed]).standard_normal(out[name].shape)
        drawn = base * np.exp(spread * noise) if base else spread * noise
        out[name] = __import__('jax').numpy.asarray(drawn.astype(out[name].dtype))
    for name, factor in factors.items():
        out[name] = (out[name] * factor).astype(out[name].dtype)
    return out
```

```python
import math
from contextlib import ExitStack

import concourse.bass as bass
from concourse import mybir

F32, F32R, BF16, I32 = mybir.dt.float32, mybir.dt.float32r, mybir.dt.bfloat16, mybir.dt.int32
ALU = mybir.AluOpType
ACT = mybir.ActivationFunctionType

P = 128
SEQ = 256
D = 1024
DF = 2816
KB = D // P
NF = DF // P
EPS = 1e-6

RAW = 3
RING = 4
FFN_UNITS = 3 * NF
S5_IN, S5_OUT = KB, 2 * KB
FFN_BASE = [0, FFN_UNITS + S5_IN + S5_OUT]
S5_BASE = FFN_UNITS
FFN_BASE += [FFN_BASE[1] + FFN_UNITS]
ATT_BASE = FFN_BASE[2] + FFN_UNITS
FFN_BASE += [ATT_BASE + 4 * KB]
UNITS = FFN_BASE[3] + FFN_UNITS
BODY = 4
TURNS = (NF - 2) // BODY
assert (NF - 2) % BODY == 0 and (3 * BODY) % RAW == 0 and (3 * BODY) % RING == 0

GROUP, STATE = 16, 64
PAIRS = 32
CH = 2 * GROUP
STEPS = 4
CHUNKS = SEQ // STEPS
QUARTERS = 4
QP = PAIRS // QUARTERS
HEAD = 64
NEG = -1e30

TWO_PI = 2 * math.pi
C1 = 6.28125
C2 = 2029 / 1048576
C3 = TWO_PI - C1 - C2


def gate_unit(base, f):
    return base + 3 * f - 1


def trunk(nc, x_in, gains, wstream, lam_re, lam_im, log_dt, b_re, b_im, c_re, c_im, skip, out):
    with ExitStack() as ctx:
        def sb(name, shape, dt=F32):
            return ctx.enter_context(nc.sbuf_tensor(name, shape, dt))

        def sem(name):
            return ctx.enter_context(nc.semaphore(name))

        raw = sb("raw", [P, RAW, D])
        w_hi = sb("w_hi", [P, RING, D], F32R)
        w_lo = sb("w_lo", [P, RING, D], F32R)
        x = sb("x", [P, KB, SEQ])
        g_hi = sb("g_hi", [P, KB, SEQ], F32R)
        g_lo = sb("g_lo", [P, KB, SEQ], F32R)
        h_hi = sb("h_hi", [P, 2, SEQ], F32R)
        h_lo = sb("h_lo", [P, 2, SEQ], F32R)
        tmp = sb("tmp", [P, 2, 4, SEQ])
        rstd = sb("rstd", [P, SEQ])
        ssq = sb("ssq", [P, SEQ])
        sq = sb("sq", [P, SEQ])
        gain = sb("gain", [P, 7, KB])
        ones = sb("ones", [P, P])
        eps = sb("eps", [P, 1])
        ident = sb("ident", [P, P])
        par = sb("par", [P, 20, PAIRS])
        par_i = sb("par_i", [P, PAIRS], I32)
        skip_col = sb("skip_col", [P, PAIRS])
        arena = sb("arena", [P, 30 * 1024])

        state_in = arena[:, 0:8192].rearrange("p (r a s) -> p r a s", r=2, a=PAIRS)
        toep = arena[:, 8192:12288].rearrange("p (a s) -> p a s", a=PAIRS)
        state_out = arena[:, 12288:20480].rearrange("p (r a s) -> p r a s", r=2, a=PAIRS)
        b_pow = arena[:, 20480:28672].rearrange("p (r a s) -> p r a s", r=2, a=PAIRS)
        c_zero = arena[:, 28672:30720].rearrange("p (r a s) -> p r a s", r=2, a=PAIRS)
        b_raw = arena[:, 0:1024].rearrange("p (r a h) -> p r a h", r=2, a=PAIRS)
        c_raw = arena[:, 1024:2048].rearrange("p (r a h) -> p r a h", r=2, a=PAIRS)
        prep_tmp = arena[:, 2048:4096].rearrange("p (r a s) -> p r a s", r=2, a=PAIRS)
        rot = arena[:, 20480:24576].rearrange("p (r a c) -> p r a c", r=2, a=PAIRS)
        rho = arena[:, 24576:26624].rearrange("p (a c) -> p a c", a=PAIRS)
        u = arena[:, 26624:28672].rearrange("p (a c) -> p a c", a=PAIRS)
        rot_tmp = arena[:, 28672:30720].rearrange("p (r a c) -> p r a c", r=2, a=PAIRS)
        skip_tmp = arena[:, 20480:24576].rearrange("p (a s) -> p a s", a=PAIRS)
        prod = arena[:, 28672:30720].rearrange("p (k a c) -> p k a c", k=4, a=QP)
        mod = tmp[:, :, :, :].rearrange("p a b t -> p (a b t)").rearrange("p (k n) -> p k n", k=4)
        z = arena[:, 0:2048].rearrange("p (k t) -> p k t", k=KB)

        v = arena[:, 0:2048].rearrange("p (t n) -> p t n", t=2)
        qk = arena[:, 2048:3072].rearrange("p (b r t) -> p b r t", b=2, r=2)
        az = arena[:, 3072:3840].rearrange("p (h n) -> p h n", h=2)
        ez = arena[:, 3840:4608].rearrange("p (h n) -> p h n", h=2)
        sp_ = arena[:, 4608:5376].rearrange("p (h n) -> p h n", h=2)
        wts = arena[:, 5376:6144].rearrange("p (h n) -> p h n", h=2)
        o = arena[:, 6144:8192].rearrange("p (k t) -> p k t", k=KB)
        ntri = arena[:, 20480:20608]
        nones = arena[:, 20608:20736]
        keep = arena[:, 20736:20864]
        big = arena[:, 20864:20992]
        r_col = arena[:, 20992:20994]
        ident_b = arena[:, 20996:21060].bitcast(BF16)
        big_b = arena[:, 21060:21124].bitcast(BF16)

        acc = ctx.enter_context(nc.psum_tensor("acc", [P, 4, 512], F32))
        gu = ctx.enter_context(nc.psum_tensor("gu", [P, 2, 512], F32))
        mx = ctx.enter_context(nc.psum_tensor("mx", [P, 2, 512], F32))

        raw_in = [sem(f"raw_in{s}") for s in range(RAW)]
        hi_ready, lo_ready, unit_done = sem("hi_ready"), sem("lo_ready"), sem("unit_done")
        x_loaded, gain_loaded, s5_loaded = sem("x_loaded"), sem("gain_loaded"), sem("s5_loaded")
        x_ready, ghi_ready, g_ready = sem("x_ready"), sem("ghi_ready"), sem("g_ready")
        ssq_ready, sum_ready, rstd_ready = sem("ssq_ready"), sem("sum_ready"), sem("rstd_ready")
        root_ready = sem("root_ready")
        acc_ready = sem("acc_ready")
        gu_scaled, silu_ready, h_ready = sem("gu_scaled"), sem("silu_ready"), sem("h_ready")
        hhi_ready, hlo_ready = sem("hhi_ready"), sem("hlo_ready")
        const_ready, eps_ready = sem("const_ready"), sem("eps_ready")
        par_dve, par_act = sem("par_dve"), sem("par_act")
        matrices_ready, turned, kernels_done = sem("matrices_ready"), sem("turned"), sem("kernels_done")
        prep_dve, prep_act = sem("prep_dve"), sem("prep_act")
        rot_ready = sem("rot_ready")
        u_ready, inflow_done, inflow_read = sem("u_ready"), sem("inflow_done"), sem("inflow_read")
        v_scanned, prod_dve, prod_pool, y_done = sem("v_scanned"), sem("prod_dve"), sem("prod_pool"), sem("y_done")
        z_act, z_dve, z_pool = sem("z_act"), sem("z_dve"), sem("z_pool")
        sg_ready, mix_read = sem("sg_ready"), sem("mix_read")
        rcol_done, rcol_ready, v_ready = sem("rcol_done"), sem("rcol_ready"), sem("v_ready")
        att_const, qk_ready, logits_done = sem("att_const"), sem("qk_ready"), sem("logits_done")
        az_ready, ez_ready, ln_ready = sem("az_ready"), sem("ez_ready"), sem("ln_ready")
        sp_ready, arg_done = sem("sp_ready"), sem("arg_done")
        wts_ready, o_done, o_ready = sem("wts_ready"), sem("o_done"), sem("o_ready")
        out_read = sem("out_read")
        dve_step, pool_step = sem("dve_step"), sem("pool_step")
        y_ready, stored = sem("y_ready"), sem("stored")

        g_out = arena[:, 0:2048].rearrange("p (k t) -> p k t", k=KB)

        def z_move(q, i, j):
            dst = z[CH * i:CH * (i + 1), 2 * q:2 * q + 2, :].rearrange("p t (c j) -> p t c j", j=STEPS)[:, :, :, j]
            src = u[CH * j:CH * (j + 1), QP * q:QP * (q + 1), :].rearrange("p (t i) c -> p t i c", t=2)[:, :, i, :]
            return dst, src

        def diagonal(t):
            return bass.AP(t.tensor, t.offset, [list(t.ap[0]), [256, 2], [1, P]])

        block = ctx.enter_context(nc.Block())

        def slot(ring, unit):
            return unit % ring

        @block.sync
        def _(sp):
            def load(unit, s, turn):
                if turn is not None:
                    sp.wait_ge(lo_ready, turn)
                sp.dma_start(raw[:, s, :], wstream[unit] if isinstance(unit, int)
                             else wstream[bass.ds(unit, 1)].rearrange("a p n -> (a p) n")).then_inc(raw_in[s], 16)

            for s in range(RAW):
                load(s, s, None)
            turns = UNITS // RAW
            with sp.Fori(1, turns) as i:
                for s in range(RAW):
                    load(RAW * i + s, s, RAW * i + (s - RAW + 1))
            for unit in range(RAW * turns, UNITS):
                load(unit, slot(RAW, unit), unit - RAW + 1)
            for d in range(KB):
                sp.wait_ge(y_ready, d + 1)
                sp.dma_start(out[:, d, :], g_out[:, d, :]).then_inc(stored, 16)
            sp.wait_ge(stored, 16 * KB)

        @block.scalar
        def _(act):
            def split_hi(unit, s_raw, s_ring, known=None):
                act.wait_ge(raw_in[s_raw], 16 * (known if known is not None else unit // RAW + 1))
                if not isinstance(unit, int) or unit >= RING:
                    act.wait_ge(unit_done, unit - RING + 1)
                act.activation(w_hi[:, s_ring, :], raw[:, s_raw, :], ACT.Copy).then_inc(hi_ready, 1)

            def split_after(done):
                if done + RING < UNITS:
                    n = done + RING
                    split_hi(n, n % RAW, n % RING)

            def silu(n, f):
                act.wait_ge(gu_scaled, NF * n + f + 1)
                act.activation(tmp[:, f % 2, 2, :], tmp[:, f % 2, 0, :], ACT.Silu).then_inc(silu_ready, 1)

            def round_h(n, f):
                act.wait_ge(h_ready, NF * n + f + 1)
                act.activation(h_hi[:, f % 2, :], tmp[:, f % 2, 3, :], ACT.Copy).then_inc(hhi_ready, 1)

            def root(n):
                act.wait_ge(sum_ready, n + 1)
                if n == 0:
                    act.wait_ge(eps_ready, 1)
                else:
                    act.wait_ge(rstd_ready, n)
                act.activation(rstd[:, :], mx[:, 1, 0:SEQ], ACT.Sqrt, scale=1.0 / D,
                               bias=eps[:, :]).then_inc(root_ready, 1)

            def ffn_head(n, f, norm_index=None):
                g = FFN_BASE[n] if f == 0 else gate_unit(FFN_BASE[n], f)
                split_after(g)
                if norm_index is not None:
                    root(norm_index)
                silu(n, f)
                split_after(g + 1)
                round_h(n, f)
                if f:
                    split_after(g + 2)

            def ffn_turn(n, i):
                base = FFN_BASE[n]
                for m in range(BODY):
                    g0 = gate_unit(base, 2 + m)
                    f0 = NF * n + 2 + m
                    for k in range(3):
                        if k == 1:
                            act.wait_ge(gu_scaled, BODY * i + (f0 + 1))
                            act.activation(tmp[:, m % 2, 2, :], tmp[:, m % 2, 0, :],
                                           ACT.Silu).then_inc(silu_ready, 1)
                        if k == 2:
                            act.wait_ge(h_ready, BODY * i + (f0 + 1))
                            act.activation(h_hi[:, m % 2, :], tmp[:, m % 2, 3, :],
                                           ACT.Copy).then_inc(hhi_ready, 1)
                        n0 = g0 + k + RING
                        if isinstance(i, int) and n0 + 3 * BODY * i >= UNITS:
                            continue
                        act.wait_ge(raw_in[n0 % RAW], (16 * 3 * BODY // RAW) * i + 16 * (n0 // RAW + 1))
                        act.wait_ge(unit_done, 3 * BODY * i + (g0 + k + 1))
                        act.activation(w_hi[:, n0 % RING, :], raw[:, n0 % RAW, :],
                                       ACT.Copy).then_inc(hi_ready, 1)

            def ffn_loop(n, first, last):
                with act.Fori(first, last) as i:
                    ffn_turn(n, i)

            def norm(n):
                for d in range(KB):
                    if n == 0:
                        act.wait_ge(x_loaded, 16)
                        act.wait_ge(gain_loaded, 16)
                    else:
                        act.wait_ge(x_ready, KB * (n - 1) + d + 1)
                    act.activation(g_hi[:, d, :], x[:, d, :], ACT.Copy,
                                   scale=gain[:, n, d:d + 1]).then_inc(ghi_ready, 1)

            def s5_parameters():
                pr = lambda k: par[:, k, :]
                act.wait_ge(s5_loaded, 16 * 9)
                act.activation(pr(3), pr(2), ACT.Exp).then_inc(par_act, 1)
                act.wait_ge(par_dve, 1)
                act.activation(pr(6), pr(4), ACT.Exp).then_inc(par_act, 1)
                act.wait_ge(par_dve, 2)
                act.activation(pr(9), pr(7), ACT.Sin).then_inc(par_act, 1)
                act.activation(pr(10), pr(8), ACT.Sin).then_inc(par_act, 1)

            def s5_prepare():
                for k in range(1, 16, 2):
                    act.wait_ge(turned, k + 1)
                    act.activation(state_in[:, k // 8, 4 * (k % 8):4 * (k % 8) + 4, :],
                                   mx[:, 1, :].rearrange("p (a s) -> p a s", a=4), ACT.Copy).then_inc(prep_act, 1)

            def s5_mixer():
                b = S5_BASE
                split_after(b)
                root(1)
                for k in range(1, S5_IN):
                    split_after(b + k)
                for q in range(QUARTERS):
                    act.wait_ge(y_done, q + 1)
                    act.activation(u[:, QP * q:QP * (q + 1), :], acc[:, q, :].rearrange("p (a c) -> p a c", a=QP),
                                   ACT.Gelu_apprx_tanh).then_inc(z_act, 1)
                    if q:
                        round_z(q - 1)
                round_z(QUARTERS - 1)
                for cb in range(KB):
                    split_after(b + KB + 2 * cb)
                    act.wait_ge(unit_done, b + KB + 2 * cb + 2)
                    act.activation(tmp[:, cb % 2, 2, :], gu[:, cb % 2, SEQ:2 * SEQ],
                                   ACT.Sigmoid).then_inc(sg_ready, 1)
                    split_after(b + KB + 2 * cb + 1)

            def round_z(q):
                act.wait_ge(z_dve, q + 1)
                act.wait_ge(z_pool, q + 1)
                act.activation(g_hi[:, 2 * q:2 * q + 2, :], z[:, 2 * q:2 * q + 2, :], ACT.Copy).then_inc(ghi_ready, 2)

            def attention():
                b = ATT_BASE
                split_after(b)
                root(4)
                for k in range(1, KB):
                    split_after(b + k)
                act.wait_ge(rcol_ready, 1)
                for t in range(2):
                    for half in range(2):
                        act.activation(v[:, t, 512 * half:512 * half + 512], acc[:, 2 * t + half, :], ACT.Copy,
                                       scale=r_col[:, t:t + 1]).then_inc(v_ready, 1)
                split_after(b + KB)
                split_after(b + KB + 1)
                for cb in range(KB):
                    for hh in range(2):
                        act.wait_ge(logits_done, 2 * cb + hh + 1)
                        if cb:
                            act.wait_ge(sp_ready, 2 * cb)
                        act.activation(az[:, hh, :], mx[:, hh, 0:384], ACT.Abs).then_inc(az_ready, 1)
                        act.wait_ge(az_ready, 2 * cb + hh + 1)
                        act.activation(ez[:, hh, :], az[:, hh, :], ACT.Exp, scale=-1.0).then_inc(ez_ready, 1)
                        act.wait_ge(ez_ready, 2 * cb + hh + 1)
                        act.activation(az[:, hh, :], ez[:, hh, :], ACT.Ln, bias=1.0).then_inc(ln_ready, 1)
                    if cb + 1 < KB:
                        split_after(b + KB + 2 * cb + 2)
                    for hh in range(2):
                        act.wait_ge(arg_done, 2 * cb + hh + 1)
                        if cb:
                            act.wait_ge(o_done, 2 * cb)
                        act.activation(wts[:, hh, :], mx[:, hh, 0:384], ACT.Exp).then_inc(wts_ready, 1)
                    if cb + 1 < KB:
                        split_after(b + KB + 2 * cb + 3)
                for d in range(KB):
                    act.wait_ge(o_ready, d + 1)
                    act.activation(g_hi[:, d, :], o[:, d, :], ACT.Copy).then_inc(ghi_ready, 1)
                for cb in range(KB):
                    split_after(b + 3 * KB + cb)

            act.dma_start(gain[:, :, :], gains).then_inc(gain_loaded, 16)
            act.dma_start(x[:, :, :], x_in).then_inc(x_loaded, 16)
            for unit in range(RAW):
                split_hi(unit, unit % RAW, unit % RING)
            norm(0)
            split_hi(3, 3 % RAW, 3 % RING)
            ffn_head(0, 0, 0)
            s5_parameters()
            ffn_head(0, 1)
            ffn_loop(0, 0, PREP_TURN)
            s5_prepare()
            ffn_loop(0, PREP_TURN, TURNS)
            norm(1)
            split_after(FFN_BASE[0] + FFN_UNITS - 1)
            s5_mixer()
            norm(2)
            for n in (1, 2, 3):
                ffn_head(n, 0, (2, 3, 5)[n - 1])
                ffn_head(n, 1)
                ffn_loop(n, 0, TURNS - (n == 3))
                if n == 3:
                    ffn_turn(n, TURNS - 1)
                if n < 3:
                    norm((0, 3, 4)[n])
                split_after(FFN_BASE[n] + FFN_UNITS - 1)
                if n == 2:
                    attention()
                    norm(5)
            root(6)

        @block.vector
        def _(dve):
            count = [0]

            def step(ins):
                count[0] += 1
                ins.then_inc(dve_step, 1)
                dve.wait_ge(dve_step, count[0])

            def split_lo(n):
                dve.wait_ge(hi_ready, n + 1)
                dve.tensor_tensor(w_lo[:, n % RING, :], raw[:, n % RAW, :], w_hi[:, n % RING, :].bitcast(F32),
                                  ALU.subtract).then_inc(lo_ready, 1)

            def split_after(done):
                if done + RING < UNITS:
                    split_lo(done + RING)

            def scale_gu(m, wait_units):
                dve.wait_ge(unit_done, wait_units)
                dve.tensor_tensor(tmp[:, m, 0:2, :], gu[:, m, :].rearrange("p (r t) -> p r t", r=2),
                                  rstd[:, :].unsqueeze(1).broadcast_to([P, 2, SEQ]), ALU.mult).then_inc(gu_scaled, 1)

            def hidden(m, n_f):
                dve.wait_ge(gu_scaled, n_f)
                dve.wait_ge(silu_ready, n_f)
                dve.tensor_tensor(tmp[:, m, 3, :], tmp[:, m, 2, :], tmp[:, m, 1, :], ALU.mult).then_inc(h_ready, 1)
                dve.wait_ge(h_ready, n_f)
                dve.wait_ge(hhi_ready, n_f)
                dve.tensor_tensor(h_lo[:, m, :], tmp[:, m, 3, :], h_hi[:, m, :].bitcast(F32),
                                  ALU.subtract).then_inc(hlo_ready, 1)

            def ffn_head(n, f, before=None):
                g = FFN_BASE[n] if f == 0 else gate_unit(FFN_BASE[n], f)
                split_after(g)
                if before:
                    before()
                scale_gu(f % 2, g + 2)
                split_after(g + 1)
                hidden(f % 2, NF * n + f + 1)
                if f:
                    split_after(g + 2)

            def ffn_turn(n, i):
                base = FFN_BASE[n]
                for m in range(BODY):
                    g0 = gate_unit(base, 2 + m)
                    f1 = BODY * i + (NF * n + 2 + m + 1)
                    for k in range(3):
                        if k == 1:
                            scale_gu(m % 2, 3 * BODY * i + (g0 + 2))
                        if k == 2:
                            hidden(m % 2, f1)
                        n0 = g0 + k + RING
                        if isinstance(i, int) and n0 + 3 * BODY * i >= UNITS:
                            continue
                        dve.wait_ge(hi_ready, 3 * BODY * i + (n0 + 1))
                        dve.tensor_tensor(w_lo[:, n0 % RING, :], raw[:, n0 % RAW, :],
                                          w_hi[:, n0 % RING, :].bitcast(F32),
                                          ALU.subtract).then_inc(lo_ready, 1)

            def ffn_loop(n, first, last):
                with dve.Fori(first, last) as i:
                    ffn_turn(n, i)

            def root(n):
                dve.wait_ge(root_ready, n + 1)
                dve.reciprocal(rstd[:, :], rstd[:, :]).then_inc(rstd_ready, 1)
                dve.wait_ge(rstd_ready, n + 1)

            def low_part(src, d, count_hi, gain_col=None):
                dve.wait_ge(ghi_ready, count_hi)
                if gain_col is None:
                    dve.tensor_tensor(g_lo[:, d, :], src[:, d, :], g_hi[:, d, :].bitcast(F32),
                                      ALU.subtract).then_inc(g_ready, 1)
                else:
                    dve.scalar_tensor_tensor(g_lo[:, d, :], src[:, d, :], gain_col, g_hi[:, d, :].bitcast(F32),
                                             ALU.mult, ALU.subtract).then_inc(g_ready, 1)

            def norm(n, base, update=None):
                for d in range(KB + 1):
                    if d < KB and update:
                        update(d)
                    if d:
                        if n:
                            dve.wait_ge(x_ready, KB * (n - 1) + d)
                        low_part(x, d - 1, base + d, gain[:, n, d - 1:d])

            def ffn_update(n):
                def update(d):
                    if d < KB - 2:
                        dve.wait_ge(acc_ready, 3 * n + d // 2 + 1)
                    else:
                        dve.wait_ge(unit_done, FFN_BASE[n] + FFN_UNITS)
                    dve.scalar_tensor_tensor(x[:, d, :], acc[:, d // 2, SEQ * (d % 2):SEQ * (d % 2 + 1)], 0.5,
                                             x[:, d, :], ALU.mult, ALU.add).then_inc(x_ready, 1)
                return update

            def s5_parameters():
                pr = lambda k: par[:, k, :]
                tt_ = lambda a, b_, c, op: dve.tensor_tensor(pr(a), pr(b_), pr(c), op)
                tt = lambda *o: step(tt_(*o))
                dve.wait_ge(par_act, 1)
                tt(4, 0, 3, ALU.mult)
                tt_(5, 1, 3, ALU.mult).then_inc(par_dve, 1)
                dve.wait_ge(par_dve, 1)
                step(dve.tensor_scalar(par_i[:, :], pr(5), 1 / TWO_PI, None, ALU.mult))
                step(dve.tensor_copy(pr(11), par_i[:, :]))
                step(dve.scalar_tensor_tensor(pr(7), pr(11), -C1, pr(5), ALU.mult, ALU.add))
                step(dve.scalar_tensor_tensor(pr(7), pr(11), -C2, pr(7), ALU.mult, ALU.add))
                step(dve.scalar_tensor_tensor(pr(7), pr(11), -C3, pr(7), ALU.mult, ALU.add))
                step(dve.tensor_scalar(pr(7), pr(7), 0.5, None, ALU.mult))
                step(dve.scalar_tensor_tensor(pr(8), pr(7), -1.0, pr(7), ALU.mult, ALU.max))
                dve.tensor_scalar(pr(8), pr(8), -1.0, math.pi / 2, ALU.mult, ALU.add).then_inc(par_dve, 1)
                dve.wait_ge(par_dve, 2)
                dve.wait_ge(par_act, 4)
                step(dve.scalar_tensor_tensor(pr(13), pr(9), 2.0, pr(10), ALU.mult, ALU.mult))
                tt(11, 9, 9, ALU.mult)
                step(dve.tensor_scalar(pr(12), pr(11), -2.0, 1.0, ALU.mult, ALU.add))
                tt(14, 6, 12, ALU.mult)
                tt(15, 6, 13, ALU.mult)
                tt(3, 0, 0, ALU.mult)
                tt(4, 1, 1, ALU.mult)
                tt(3, 3, 4, ALU.add)
                step(dve.reciprocal(pr(3), pr(3)))
                step(dve.tensor_scalar(pr(5), pr(14), -1.0, None, ALU.add))
                tt(7, 5, 0, ALU.mult)
                tt(8, 15, 1, ALU.mult)
                tt(9, 15, 0, ALU.mult)
                tt(10, 5, 1, ALU.mult)
                tt(7, 7, 8, ALU.add)
                tt(9, 9, 10, ALU.subtract)
                tt(16, 7, 3, ALU.mult)
                tt(17, 9, 3, ALU.mult)
                for _ in range(2):
                    tt(7, 12, 12, ALU.mult)
                    tt(8, 13, 13, ALU.mult)
                    step(dve.scalar_tensor_tensor(pr(9), pr(12), 2.0, pr(13), ALU.mult, ALU.mult))
                    tt(12, 7, 8, ALU.subtract)
                    step(dve.tensor_copy(pr(13), pr(9)))
                tt(18, 6, 6, ALU.mult)
                tt_(19, 18, 18, ALU.mult).then_inc(par_dve, 1)

            def s5_prepare():
                for k in range(0, 16, 2):
                    dve.wait_ge(turned, k + 1)
                    dve.tensor_copy(state_in[:, k // 8, 4 * (k % 8):4 * (k % 8) + 4, :],
                                    mx[:, 0, :].rearrange("p (a s) -> p a s", a=4)).then_inc(prep_dve, 1)
                for k in range(8):
                    dve.wait_ge(kernels_done, k + 1)
                    src = mx[0:CH, k % 2, :].rearrange("p (a s) -> p a s", a=4)
                    for j in range(STEPS):
                        last = dve.tensor_copy(toep[CH * j:CH * (j + 1), 4 * k:4 * k + 4, CH * j:P],
                                               src[:, :, 0:P - CH * j])
                    last.then_inc(prep_dve, 1)

            def s5_scale_u(q):
                dve.wait_ge(unit_done, S5_BASE + 2 * q + 2)
                if q == 0:
                    dve.wait_ge(rot_ready, 1)
                for j in range(STEPS):
                    for i in range(4):
                        src = acc[CH * i:CH * (i + 1), q, :].rearrange("p (t c j) -> p t c j", t=2, j=STEPS)[:, :, :, j]
                        r = rstd[CH * i:CH * (i + 1), :].rearrange("p (c j) -> p c j", j=STEPS)[:, :, j]
                        dst = u[CH * j:CH * (j + 1), QP * q:QP * (q + 1), :].rearrange(
                            "p (t i) c -> p t i c", t=2)[:, :, i, :]
                        last = dve.tensor_tensor(dst, src, r.unsqueeze(1).broadcast_to([CH, 2, CHUNKS]), ALU.mult)
                last.then_inc(u_ready, 1)

            def s5_scan(q):
                dve.wait_ge(inflow_done, q + 1)
                if q:
                    dve.wait_ge(prod_pool, q)
                    dve.wait_ge(prod_dve, q)
                else:
                    dve.wait_ge(hlo_ready, NF)
                re, im = ((gu, mx)[q % 2][:, r, :] for r in range(2))
                cos, sin = (rot[:, r, QP * q:QP * (q + 1), :].rearrange("p a c -> p (a c)") for r in range(2))
                dve.tensor_tensor(mod[:, 0, :], re, cos, ALU.mult)
                dve.tensor_tensor(mod[:, 1, :], im, sin, ALU.mult)
                dve.tensor_tensor(mod[:, 2, :], im, cos, ALU.mult)
                step(dve.tensor_tensor(mod[:, 3, :], re, sin, ALU.mult))
                dve.tensor_tensor(mod[:, 0, :], mod[:, 0, :], mod[:, 1, :], ALU.add).then_inc(inflow_read, 1)
                step(dve.tensor_tensor(mod[:, 2, :], mod[:, 2, :], mod[:, 3, :], ALU.subtract))
                decay = rho[:, QP * q:QP * (q + 1), :].rearrange("p a c -> p (a c)")
                dve.tensor_tensor_scan(mod[:, 1, :], decay, mod[:, 0, :], 0.0, ALU.mult, ALU.add)
                dve.tensor_tensor_scan(mod[:, 3, :], decay, mod[:, 2, :], 0.0, ALU.mult, ALU.add).then_inc(v_scanned, 1)

            def s5_products(q):
                dve.wait_ge(v_scanned, q + 1)
                if q:
                    dve.wait_ge(y_done, q)
                cos, sin = (rot[:, r, QP * q:QP * (q + 1), :] for r in range(2))
                vr, vi = (mod[:, k, :].rearrange("p (a c) -> p a c", a=QP) for k in (1, 3))
                dve.tensor_tensor(prod[:, 0], vr, cos, ALU.mult)
                dve.scalar_tensor_tensor(prod[:, 1].rearrange("p a c -> p (a c)"), mod[:, 3, :], -1.0,
                                         sin.rearrange("p a c -> p (a c)"), ALU.mult, ALU.mult).then_inc(prod_dve, 1)

            def s5_shuffle(q):
                dve.wait_ge(z_act, q + 1)
                for j in (0, 1):
                    for i in range(4):
                        last = dve.tensor_copy(*z_move(q, i, j))
                last.then_inc(z_dve, 1)

            def s5_low(q):
                dve.wait_ge(ghi_ready, 16 + 2 * q + 2)
                dve.tensor_tensor(g_lo[:, 2 * q:2 * q + 2, :], z[:, 2 * q:2 * q + 2, :],
                                  g_hi[:, 2 * q:2 * q + 2, :].bitcast(F32), ALU.subtract).then_inc(g_ready, 2)

            def s5_mixer():
                b = S5_BASE
                split_after(b)
                root(1)
                split_after(b + 1)
                s5_scale_u(0)
                split_after(b + 2)
                split_after(b + 3)
                s5_scale_u(1)
                s5_scan(0)
                s5_products(0)
                split_after(b + 4)
                split_after(b + 5)
                s5_scale_u(2)
                s5_scan(1)
                split_after(b + 6)
                split_after(b + 7)
                s5_scale_u(3)
                s5_products(1)
                s5_scan(2)
                s5_products(2)
                s5_shuffle(0)
                s5_scan(3)
                s5_products(3)
                s5_low(0)
                for q in range(1, QUARTERS):
                    s5_shuffle(q)
                    s5_low(q)
                for cb in range(KB):
                    split_after(b + KB + 2 * cb)
                    dve.wait_ge(sg_ready, cb + 1)
                    if cb >= 2:
                        dve.wait_ge(x_ready, KB + cb - 1)
                    dve.tensor_tensor(tmp[:, cb % 2, 3, :], gu[:, cb % 2, 0:SEQ], tmp[:, cb % 2, 2, :],
                                      ALU.mult).then_inc(mix_read, 1)
                    dve.wait_ge(mix_read, cb + 1)
                    dve.tensor_tensor(x[:, cb, :], x[:, cb, :], tmp[:, cb % 2, 3, :], ALU.add).then_inc(x_ready, 1)
                    split_after(b + KB + 2 * cb + 1)

            def attention():
                b = ATT_BASE
                split_after(b)
                root(4)
                for k in range(1, KB):
                    split_after(b + k)
                dve.wait_ge(rcol_done, 1)
                dve.tensor_copy(r_col, mx[:, 0, 0:2]).then_inc(rcol_ready, 1)

                def scale_qk(cb):
                    dve.wait_ge(unit_done, b + KB + 2 * cb + 2)
                    dve.scalar_tensor_tensor(qk[:, cb % 2, 0, :], gu[:, cb % 2, 0:SEQ], HEAD ** -0.5, rstd[:, :],
                                             ALU.mult, ALU.mult)
                    dve.tensor_tensor(qk[:, cb % 2, 1, :], gu[:, cb % 2, SEQ:2 * SEQ], rstd[:, :],
                                      ALU.mult).then_inc(qk_ready, 1)

                split_after(b + KB)
                scale_qk(0)
                split_after(b + KB + 1)
                for cb in range(KB):
                    for hh in range(2):
                        n = 2 * cb + hh + 1
                        dve.wait_ge(ln_ready, n)
                        if cb:
                            dve.wait_ge(arg_done, 2 * cb)
                        step(dve.scalar_tensor_tensor(sp_[:, hh, :], mx[:, hh, 0:384], 0.0, az[:, hh, :],
                                                      ALU.max, ALU.add))
                        diag = diagonal(sp_[:, hh, :])
                        dve.tensor_tensor(diag, diag, keep.unsqueeze(1).broadcast_to([P, 2, P]),
                                          ALU.mult).then_inc(sp_ready, 1)
                    if cb + 1 < KB:
                        split_after(b + KB + 2 * cb + 2)
                        scale_qk(cb + 1)
                        split_after(b + KB + 2 * cb + 3)
                    dve.wait_ge(o_done, 2 * cb + 2)
                    dve.tensor_copy(o[:, cb, :], acc[:, cb % 4, 0:SEQ]).then_inc(o_ready, 1)
                dve.wait_ge(o_ready, KB)
                for d in range(KB):
                    low_part(o, d, 48 + d + 1)
                for cb in range(KB):
                    dve.wait_ge(unit_done, b + 3 * KB + cb + 1)
                    dve.tensor_tensor(x[:, cb, :], x[:, cb, :], gu[:, cb % 2, 0:SEQ], ALU.add).then_inc(x_ready, 1)
                    split_after(b + 3 * KB + cb)

            dve.memset(eps[:, :], EPS).then_inc(eps_ready, 1)
            for unit in range(RAW):
                split_lo(unit)
            norm(0, 0)
            split_lo(3)
            ffn_head(0, 0, lambda: root(0))
            s5_parameters()
            ffn_head(0, 1)
            ffn_loop(0, 0, PREP_TURN)
            s5_prepare()
            ffn_loop(0, PREP_TURN, TURNS)
            norm(1, 8, ffn_update(0))
            split_after(FFN_BASE[0] + FFN_UNITS - 1)
            s5_mixer()
            norm(2, 24)
            for n in (1, 2, 3):
                ffn_head(n, 0, lambda: root((2, 3, 5)[n - 1]))
                ffn_head(n, 1)
                ffn_loop(n, 0, TURNS - (n == 3))
                if n == 3:
                    ffn_turn(n, TURNS - 1)
                if n == 1:
                    norm(3, 32, ffn_update(n))
                if n == 2:
                    norm(4, 40, ffn_update(n))
                split_after(FFN_BASE[n] + FFN_UNITS - 1)
                if n == 2:
                    attention()
                    norm(5, 56)
            for d in range(KB):
                ffn_update(3)(d)
            root(6)
            dve.wait_ge(x_ready, 6 * KB)
            for d in range(KB):
                dve.scalar_tensor_tensor(g_out[:, d, :], x[:, d, :], gain[:, 6, d:d + 1], rstd[:, :],
                                         ALU.mult, ALU.mult).then_inc(y_ready, 1)

        @block.tensor
        def _(pe):
            def three(dst, unit_slot, cols, hi, lo, start, stop, check=False):
                a, b_ = w_hi[:, unit_slot, cols], w_lo[:, unit_slot, cols]
                pe.matmul(dst, a, hi, start=start, stop=False, skip_group_check=check)
                pe.matmul(dst, a, lo, start=False, stop=False, skip_group_check=check)
                return pe.matmul(dst, b_, hi, start=False, stop=stop, skip_group_check=check)

            def column_unit(dst, s, g_base=None):
                for kb in range(KB):
                    if g_base is not None:
                        pe.wait_ge(g_ready, g_base + kb + 1)
                    last = three(dst, s, slice(P * kb, P * kb + P), g_hi[:, kb, :], g_lo[:, kb, :],
                                 kb == 0, kb == KB - 1)
                last.then_inc(unit_done, 1)

            def down_unit(s, m, first=False, last_block=False):
                for d in range(KB):
                    mm = three(acc[:, d // 2, SEQ * (d % 2):SEQ * (d % 2 + 1)], s, slice(P * d, P * d + P),
                               h_hi[:, m, :], h_lo[:, m, :], first and d % 2 == 0, last_block, check=True)
                    if last_block and d % 2 and d < KB - 1:
                        mm.then_inc(acc_ready, 1)
                mm.then_inc(unit_done, 1)

            def squares(n):
                pe.wait_ge(ssq_ready, n + 1)
                if n == 0:
                    pe.wait_ge(const_ready, 1)
                pe.matmul(mx[:, 1, 0:SEQ], ones[:, :], ssq[:, :], start=True, stop=True).then_inc(sum_ready, 1)

            def ffn_head(n, f, g_base=None, norm_index=None):
                g = FFN_BASE[n] if f == 0 else gate_unit(FFN_BASE[n], f)
                if NF * n + f >= 2:
                    pe.wait_ge(gu_scaled, NF * n + f - 1)
                pe.wait_ge(lo_ready, g + 1)
                column_unit(gu[:, f % 2, 0:SEQ], g % RING, g_base)
                if norm_index is not None:
                    squares(norm_index)
                pe.wait_ge(lo_ready, g + 2)
                column_unit(gu[:, f % 2, SEQ:2 * SEQ], (g + 1) % RING)
                if f:
                    pe.wait_ge(lo_ready, g + 3)
                    pe.wait_ge(hlo_ready, NF * n + f)
                    down_unit((g + 2) % RING, (f - 1) % 2, first=f == 1)

            def ffn_loop(n, first, last):
                base = FFN_BASE[n]
                with pe.Fori(first, last) as i:
                    for m in range(BODY):
                        g0 = gate_unit(base, 2 + m)
                        f0 = NF * n + 2 + m
                        pe.wait_ge(gu_scaled, BODY * i + (f0 - 1))
                        pe.wait_ge(lo_ready, 3 * BODY * i + (g0 + 1))
                        column_unit(gu[:, m % 2, 0:SEQ], g0 % RING)
                        pe.wait_ge(lo_ready, 3 * BODY * i + (g0 + 2))
                        column_unit(gu[:, m % 2, SEQ:2 * SEQ], (g0 + 1) % RING)
                        pe.wait_ge(lo_ready, 3 * BODY * i + (g0 + 3))
                        pe.wait_ge(hlo_ready, BODY * i + f0)
                        down_unit((g0 + 2) % RING, (m + 1) % 2)

            def ffn_tail(n):
                g = gate_unit(FFN_BASE[n], NF - 1)
                pe.wait_ge(lo_ready, g + 4)
                pe.wait_ge(hlo_ready, NF * n + NF)
                down_unit((g + 3) % RING, (NF - 1) % 2, last_block=True)

            def s5_prepare():
                pe.wait_ge(matrices_ready, 1)
                pe.wait_ge(const_ready, 1)
                for k in range(16):
                    if k >= 2:
                        pe.wait_ge((prep_dve, prep_act)[k % 2], k // 2)
                    for a in range(4):
                        mm = pe.transpose(mx[:, k % 2, P * a:P * (a + 1)], b_pow[:, k // 8, 4 * (k % 8) + a, :],
                                          ident[:, :])
                    mm.then_inc(turned, 1)
                for k in range(8):
                    if k == 0:
                        pe.wait_ge(prep_dve, 8)
                    elif k == 1:
                        pe.wait_ge(prep_act, 8)
                    else:
                        pe.wait_ge(prep_dve, 8 + k - 1)
                    for a in range(4):
                        pair = 4 * k + a
                        for r in range(2):
                            pe.matmul(mx[0:CH, k % 2, P * a:P * a + CH], b_pow[:, r, pair, 3 * CH:4 * CH],
                                      c_zero[:, r, pair, :], start=r == 0, stop=r == 1)
                        for r in range(2):
                            mm = pe.matmul(mx[0:CH, k % 2, P * a + CH:P * (a + 1)], b_pow[:, r, pair, 3 * CH:4 * CH],
                                           state_out[:, r, pair, 0:3 * CH], start=r == 0, stop=r == 1)
                    mm.then_inc(kernels_done, 1)

            def s5_inflow(q):
                pe.wait_ge(u_ready, q + 1)
                if q >= 2:
                    pe.wait_ge(inflow_read, q - 1)
                bank = (gu, mx)[q % 2]
                for a in range(QP):
                    for r in range(2):
                        mm = pe.matmul(bank[:, r, CHUNKS * a:CHUNKS * (a + 1)], state_in[:, r, QP * q + a, :],
                                       u[:, QP * q + a, :], start=True, stop=True)
                mm.then_inc(inflow_done, 1)
                for a in range(QP):
                    mm = pe.matmul(acc[:, q, CHUNKS * a:CHUNKS * (a + 1)], toep[:, QP * q + a, :],
                                   u[:, QP * q + a, :], start=a == 0, stop=False, skip_group_check=True)

            def s5_mixer():
                b = S5_BASE

                def project(k, g_base=None):
                    pe.wait_ge(lo_ready, b + k + 1)
                    column_unit(acc[:, k // 2, SEQ * (k % 2):SEQ * (k % 2 + 1)], (b + k) % RING, g_base)

                project(0, 8)
                squares(1)
                for k in range(1, 4):
                    project(k)
                s5_inflow(0)
                project(4)
                project(5)
                s5_inflow(1)
                project(6)
                project(7)
                s5_inflow(2)
                s5_inflow(3)
                for q in range(QUARTERS):
                    pe.wait_ge(prod_dve, q + 1)
                    pe.wait_ge(prod_pool, q + 1)
                    for a in range(QP):
                        for k in range(4):
                            mm = pe.matmul(acc[:, q, CHUNKS * a + 1:CHUNKS * (a + 1)],
                                           state_out[:, k // 2, QP * q + a, :], prod[:, k, a, 0:CHUNKS - 1],
                                           start=False, stop=k == 3, skip_group_check=True)
                    mm.then_inc(y_done, 1)
                for cb in range(KB):
                    n = b + KB + 2 * cb
                    if cb >= 2:
                        pe.wait_ge(mix_read, cb - 1)
                    pe.wait_ge(lo_ready, n + 1)
                    column_unit(gu[:, cb % 2, 0:SEQ], n % RING, 16 if cb == 0 else None)
                    pe.wait_ge(lo_ready, n + 2)
                    column_unit(gu[:, cb % 2, SEQ:2 * SEQ], (n + 1) % RING)

            def attention():
                b = ATT_BASE
                for kb in range(KB):
                    pe.wait_ge(lo_ready, b + kb + 1)
                    pe.wait_ge(g_ready, 40 + kb + 1)
                    if kb == 0:
                        pe.wait_ge(x_ready, 4 * KB)
                    s = (b + kb) % RING
                    for t in range(2):
                        gh, gl = g_hi[:, kb, P * t:P * (t + 1)], g_lo[:, kb, P * t:P * (t + 1)]
                        for half in range(2):
                            cols = slice(512 * half, 512 * half + 512)
                            dst = acc[:, 2 * t + half, :]
                            pe.matmul(dst, gh, w_hi[:, s, cols], start=kb == 0, stop=False)
                            pe.matmul(dst, gh, w_lo[:, s, cols], start=False, stop=False)
                            mm = pe.matmul(dst, gl, w_hi[:, s, cols], start=False, stop=kb == KB - 1)
                    mm.then_inc(unit_done, 1)
                    if kb == 0:
                        squares(4)
                pe.wait_ge(rstd_ready, 5)
                for t in range(2):
                    mm = pe.matmul(mx[:, 0, t:t + 1], rstd[0:1, P * t:P * (t + 1)], ones[0:1, 0:1],
                                   start=True, stop=True)
                mm.then_inc(rcol_done, 1)

                def project(cb, r):
                    n = b + KB + 2 * cb + r
                    pe.wait_ge(lo_ready, n + 1)
                    if cb >= 2:
                        pe.wait_ge(qk_ready, cb - 1)
                    column_unit(gu[:, cb % 2, SEQ * r:SEQ * (r + 1)], n % RING)

                project(0, 0)
                project(0, 1)
                pe.wait_ge(att_const, 1)
                pe.wait_ge(rcol_ready, 1)
                for cb in range(KB):
                    pe.wait_ge(qk_ready, cb + 1)
                    for hh in range(2):
                        rows = slice(HEAD * hh, HEAD * (hh + 1))
                        if cb:
                            pe.wait_ge(wts_ready, 2 * cb)
                        q_, k_ = qk[rows, cb % 2, 0, :], qk[rows, cb % 2, 1, :]
                        pe.matmul(mx[:, hh, 0:SEQ], k_[:, 0:P], q_, start=True, stop=False, skip_group_check=True)
                        pe.matmul(mx[:, hh, SEQ:384], k_[:, P:SEQ], q_[:, P:SEQ], start=False, stop=False,
                                  skip_group_check=True).then_inc(logits_done, 1)
                    if cb + 1 < KB:
                        project(cb + 1, 0)
                    for hh in range(2):
                        pe.wait_ge(sp_ready, 2 * cb + hh + 1)
                        s_ = sp_[:, hh, :]
                        args = [(mx[:, hh, 0:SEQ], ntri, s_[:, 0:SEQ]), (mx[:, hh, P:SEQ], nones, s_[:, SEQ:384]),
                                (mx[:, hh, SEQ:384], ntri, s_[:, SEQ:384]),
                                (mx[:, hh, 0:P], ident_b, big_b), (mx[:, hh, SEQ:384], ident_b, big_b)]
                        for k, (dst, a, m_) in enumerate(args):
                            mm = pe.matmul(dst, a, m_, start=False, stop=k == 4, skip_group_check=True)
                        mm.then_inc(arg_done, 1)
                    if cb + 1 < KB:
                        project(cb + 1, 1)
                    pe.wait_ge(v_ready, 4)
                    if cb >= 4:
                        pe.wait_ge(o_ready, cb - 3)
                    for hh in range(2):
                        pe.wait_ge(wts_ready, 2 * cb + hh + 1)
                        c0 = P * cb + HEAD * hh
                        dst = acc[HEAD * hh:HEAD * (hh + 1), cb % 4, 0:SEQ]
                        pe.matmul(dst, v[:, 0, c0:c0 + HEAD], wts[:, hh, 0:SEQ], start=True, stop=False,
                                  skip_group_check=True)
                        pe.matmul(dst[:, P:SEQ], v[:, 1, c0:c0 + HEAD], wts[:, hh, SEQ:384], start=False, stop=True,
                                  skip_group_check=True).then_inc(o_done, 1)
                for cb in range(KB):
                    n = b + 3 * KB + cb
                    pe.wait_ge(lo_ready, n + 1)
                    if cb >= 2:
                        pe.wait_ge(x_ready, 4 * KB + cb - 1)
                    column_unit(gu[:, cb % 2, 0:SEQ], n % RING, 48 if cb == 0 else None)

            ffn_head(0, 0, 0, 0)
            ffn_head(0, 1)
            ffn_loop(0, 0, PREP_TURN)
            s5_prepare()
            ffn_loop(0, PREP_TURN, TURNS)
            ffn_tail(0)
            s5_mixer()
            for n in (1, 2, 3):
                ffn_head(n, 0, (24, 32, 56)[n - 1], (2, 3, 5)[n - 1])
                ffn_head(n, 1)
                ffn_loop(n, 0, TURNS)
                ffn_tail(n)
                if n == 2:
                    attention()
            squares(6)

        @block.gpsimd
        def _(pool):
            count = [0]

            def step(ins):
                count[0] += 1
                ins.then_inc(pool_step, 1)
                pool.wait_ge(pool_step, count[0])

            def norm(n):
                for d in range(KB):
                    if n == 0:
                        pool.wait_ge(x_loaded, 16)
                    else:
                        pool.wait_ge(x_ready, KB * (n - 1) + d + 1)
                    if d == 0:
                        if n:
                            pool.wait_ge(sum_ready, n)
                        step(pool.tensor_tensor(ssq[:, :], x[:, 0, :], x[:, 0, :], ALU.mult))
                        continue
                    step(pool.tensor_tensor(sq[:, :], x[:, d, :], x[:, d, :], ALU.mult))
                    add = pool.tensor_tensor(ssq[:, :], ssq[:, :], sq[:, :], ALU.add)
                    if d < KB - 1:
                        step(add)
                add.then_inc(ssq_ready, 1)

            def halves(fn):
                for g2 in range(2):
                    fn(slice(STATE * g2, STATE * (g2 + 1)), slice(GROUP * g2, GROUP * (g2 + 1)))

            def times(dst_re, dst_im, re, im, l_re, l_im, t, conj):
                tt = pool.tensor_tensor
                step(tt(t[0], re, l_re, ALU.mult))
                step(tt(t[1], im, l_im, ALU.mult))
                step(tt(dst_re, t[0], t[1], ALU.add if conj else ALU.subtract))
                step(tt(t[0], im, l_re, ALU.mult))
                step(tt(t[1], re, l_im, ALU.mult))
                step(tt(dst_im, t[0], t[1], ALU.subtract if conj else ALU.add))

            def s5_matrices():
                pool.wait_ge(s5_loaded, 16 * 9)
                pool.wait_ge(par_dve, 3)
                wide = lambda k, n: par[:, k, :].unsqueeze(2).broadcast_to([P, PAIRS, n])
                t = [prep_tmp[:, r, :, 0:GROUP] for r in range(2)]
                base_b = [b_pow[:, r, :, 3 * CH:4 * CH] for r in range(2)]
                for r in range(2):
                    step(pool.tensor_tensor(t[0], b_raw[:, r], wide(16, GROUP), ALU.mult))
                    step(pool.tensor_tensor(t[1], b_raw[:, 1 - r], wide(17, GROUP), ALU.mult))
                    halves(lambda rows, cols: step(pool.tensor_tensor(
                        base_b[r][rows, :, cols], t[0][rows], t[1][rows], (ALU.subtract, ALU.add)[r])))
                    halves(lambda rows, cols: step(pool.tensor_scalar(
                        c_zero[rows, r, :, cols], c_raw[rows, r], (1.0, -1.0)[r], None, ALU.mult)))
                t = [prep_tmp[:, r] for r in range(2)]
                l_re, l_im = wide(14, CH), wide(15, CH)
                for j in (2, 1, 0):
                    blk = [[b_pow[:, r, :, CH * k:CH * (k + 1)] for r in range(2)] for k in (j, j + 1)]
                    times(*blk[0], *blk[1], l_re, l_im, t, False)
                for j in range(STEPS):
                    dst = [state_out[:, r, :, CH * j:CH * (j + 1)] for r in range(2)]
                    src = [state_out[:, r, :, CH * (j - 1):CH * j] if j else c_zero[:, r] for r in range(2)]
                    times(*dst, *src, l_re, l_im, t, True)

            def s5_tables():
                pool.wait_ge(prep_dve, 16)
                pool.wait_ge(prep_act, 8)
                wide = lambda k, n: par[:, k, :].unsqueeze(2).broadcast_to([P, PAIRS, n])
                step(pool.tensor_tensor(skip_tmp, ident[:, :].unsqueeze(1).broadcast_to([P, PAIRS, P]),
                                        skip_col[:, :].unsqueeze(2).broadcast_to([P, PAIRS, P]), ALU.mult))
                step(pool.tensor_tensor(toep, toep, skip_tmp, ALU.add))
                step(pool.memset(rot[:, 0, :, 0:1], 1.0))
                step(pool.memset(rot[:, 1, :, 0:1], 0.0))
                step(pool.tensor_scalar(rho, par[:, 19, :].unsqueeze(2).broadcast_to([P, PAIRS, CHUNKS]), 1.0, None,
                                        ALU.mult))
                step(pool.memset(rho[:, :, 0:1], 0.0))
                n = 1
                while n < CHUNKS:
                    t = [rot_tmp[:, r, :, 0:n] for r in range(2)]
                    times(rot[:, 0, :, n:2 * n], rot[:, 1, :, n:2 * n], rot[:, 0, :, 0:n], rot[:, 1, :, 0:n],
                          wide(12, n), wide(13, n), t, False)
                    n *= 2
                    if n < CHUNKS:
                        t = [rot_tmp[:, r, :, 0] for r in range(2)]
                        s_ = rot_tmp[:, 0, :, 1]
                        step(pool.tensor_tensor(t[0], par[:, 12, :], par[:, 12, :], ALU.mult))
                        step(pool.tensor_tensor(t[1], par[:, 13, :], par[:, 13, :], ALU.mult))
                        step(pool.tensor_tensor(s_, par[:, 12, :], par[:, 13, :], ALU.mult))
                        step(pool.tensor_tensor(par[:, 12, :], t[0], t[1], ALU.subtract))
                        step(pool.tensor_scalar(par[:, 13, :], s_, 2.0, None, ALU.mult))

            def s5_products(q):
                pool.wait_ge(v_scanned, q + 1)
                if q:
                    pool.wait_ge(y_done, q)
                cos, sin = (rot[:, r, QP * q:QP * (q + 1), :] for r in range(2))
                vr, vi = (mod[:, k, :].rearrange("p (a c) -> p a c", a=QP) for k in (1, 3))
                pool.tensor_tensor(prod[:, 2], vr, sin, ALU.mult)
                pool.tensor_tensor(prod[:, 3], vi, cos, ALU.mult).then_inc(prod_pool, 1)

            def s5_shuffle(q):
                pool.wait_ge(z_act, q + 1)
                pool.wait_ge(prod_pool, min(q + 3, QUARTERS))
                for j in (2, 3):
                    for i in range(4):
                        step(pool.tensor_copy(*z_move(q, i, j)))
                pool.sem_inc(z_pool, 1)

            def attention_masks():
                pool.wait_ge(x_ready, 2 * KB)
                step(pool.memset(nones, -1.0))
                step(pool.memset(keep, 1.0))
                step(pool.memset(big, 0.0))
                step(pool.affine_select(out=ntri, in_=nones, compare_op=ALU.is_ge, fill=0.0, base=0,
                                        pattern=[[-1, P]], channel_multiplier=1))
                step(pool.affine_select(out=keep, in_=keep, compare_op=ALU.is_gt, fill=0.0, base=0,
                                        pattern=[[1, P]], channel_multiplier=-1))
                step(pool.affine_select(out=big, in_=big, compare_op=ALU.is_gt, fill=NEG, base=0,
                                        pattern=[[1, P]], channel_multiplier=-1))
                step(pool.tensor_copy(ident_b, ident[:, :]))
                pool.tensor_copy(big_b, big).then_inc(att_const, 1)

            norm(0)
            step(pool.memset(ident[:, :], 0.0))
            step(pool.affine_select(out=ident[:, :], in_=ident[:, :], compare_op=ALU.not_equal, fill=1.0, base=0,
                                    pattern=[[-1, P]], channel_multiplier=1))
            pool.memset(ones[:, :], 1.0).then_inc(const_ready, 1)
            for dst, src in ((par[:, 0, :], lam_re), (par[:, 1, :], lam_im),
                             (par[0:STATE, 2, :], log_dt[0:1, :].broadcast_to([STATE, PAIRS])),
                             (par[STATE:P, 2, :], log_dt[1:2, :].broadcast_to([STATE, PAIRS])),
                             (b_raw[:, 0], b_re), (b_raw[:, 1], b_im), (c_raw[:, 0], c_re), (c_raw[:, 1], c_im),
                             (skip_col[:, :], skip)):
                pool.dma_start(dst, src).then_inc(s5_loaded, 16)
            step(pool.memset(b_pow[:, :, :, 3 * CH:4 * CH], 0.0))
            step(pool.memset(c_zero, 0.0))
            step(pool.memset(toep, 0.0))
            s5_matrices()
            pool.sem_inc(matrices_ready, 1)
            s5_tables()
            pool.sem_inc(rot_ready, 1)
            norm(1)
            for q in range(QUARTERS):
                s5_products(q)
                if q >= 2:
                    s5_shuffle(q - 2)
            s5_shuffle(2)
            s5_shuffle(3)
            norm(2)
            attention_masks()
            for n in (3, 4, 5, 6):
                norm(n)


PREP_TURN = 3


def lay_out(a):
    import numpy as np

    stream = np.empty((UNITS, P, D), np.float32)
    at = [0]

    def put(block):
        stream[at[0]] = block
        at[0] += 1

    def columns(w, c):
        put(w[:, P * c:P * (c + 1)].reshape(KB, P, P).transpose(1, 0, 2).reshape(P, D))

    def ffn(w_in, w_out):
        for f in range(NF):
            columns(w_in, f)
            columns(w_in, NF + f)
            if f:
                put(w_out[P * (f - 1):P * f])
        put(w_out[P * (NF - 1):])

    ffn(a["ffn1_w_in"][0], a["ffn1_w_out"][0])
    for c in range(KB):
        columns(a["s5_w_in"][0], c)
    for c in range(KB):
        columns(a["s5_w_out"][0], c)
        columns(a["s5_w_out"][0], KB + c)
    ffn(a["ffn2_w_in"][0], a["ffn2_w_out"][0])
    ffn(a["ffn1_w_in"][1], a["ffn1_w_out"][1])
    qkv = a["sb_w_qkv"][0]
    for k in range(KB):
        put(qkv[P * k:P * (k + 1), 2 * D:])
    for c in range(KB):
        columns(qkv, c)
        columns(qkv, KB + c)
    for c in range(KB):
        columns(a["sb_w_out"][0], c)
    ffn(a["ffn2_w_in"][1], a["ffn2_w_out"][1])

    def block_vector(g):
        return g.reshape(KB, P).T

    def states(m):
        m = m.reshape(PAIRS, 2, STATE, *m.shape[2:])
        return m.transpose(1, 2, 0, *range(3, m.ndim)).reshape(P, PAIRS, *m.shape[3:])

    gains = np.stack([block_vector(g) for g in (
        a["ffn1_norm"][0], a["mix_norm"][0], a["ffn2_norm"][0], a["ffn1_norm"][1], a["mix_norm"][1],
        a["ffn2_norm"][1], a["final_norm"])], axis=1)
    return {
        "x_in": a["x"][0].T.reshape(KB, P, SEQ).transpose(1, 0, 2),
        "gains": gains,
        "wstream": stream,
        "lam_re": states(a["s5_lam_re"][0]),
        "lam_im": states(a["s5_lam_im"][0]),
        "log_dt": a["s5_log_dt"][0].reshape(PAIRS, 2).T,
        "b_re": states(a["s5_b_re"][0]),
        "b_im": states(a["s5_b_im"][0]),
        "c_re": states(a["s5_c_re"][0].transpose(0, 2, 1)),
        "c_im": states(a["s5_c_im"][0].transpose(0, 2, 1)),
        "skip": np.concatenate([a["s5_d"][0].reshape(PAIRS, CH).T] * STEPS),
    }


def kernel(**inputs):
    import numpy as np
    import concourse.bacc as bacc
    from concourse.bass_utils import run_bass_kernel_spmd as run

    nc = bacc.Bacc("TRN2", target_bir_lowering=False, num_devices=1)
    arrays, args = {}, []
    for name, a in lay_out({k: np.asarray(v) for k, v in inputs.items()}).items():
        a = np.ascontiguousarray(a)
        arrays[f"{name}_dram"] = a
        args.append(nc.dram_tensor(f"{name}_dram", a.shape, mybir.dt.from_np(a.dtype), kind="ExternalInput").ap())
    out = nc.dram_tensor("out_dram", (P, KB, SEQ), F32, kind="ExternalOutput").ap()
    trunk(nc, *args, out)
    result = run(nc, [arrays], core_ids=[0]).results[0]["out_dram"]
    return result.transpose(1, 0, 2).reshape(1, D, SEQ).transpose(0, 2, 1)
```

```python
import math
from contextlib import ExitStack

import concourse.bass as bass
from concourse import mybir

F32, F32R, BF16, I32 = mybir.dt.float32, mybir.dt.float32r, mybir.dt.bfloat16, mybir.dt.int32
ALU = mybir.AluOpType
ACT = mybir.ActivationFunctionType

P = 128
SEQ = 256
D = 1024
DF = 2816
KB = D // P
NF = DF // P
EPS = 1e-6

RAW = 3
RING = 4
FFN_UNITS = 3 * NF
S5_IN, S5_OUT = KB, 2 * KB
FFN_BASE = [0, FFN_UNITS + S5_IN + S5_OUT]
S5_BASE = FFN_UNITS
FFN_BASE += [FFN_BASE[1] + FFN_UNITS]
ATT_BASE = FFN_BASE[2] + FFN_UNITS
FFN_BASE += [ATT_BASE + 4 * KB]
UNITS = FFN_BASE[3] + FFN_UNITS
BODY = 4
TURNS = (NF - 2) // BODY
assert (NF - 2) % BODY == 0 and (3 * BODY) % RAW == 0 and (3 * BODY) % RING == 0

GROUP, STATE = 16, 64
PAIRS = 32
CH = 2 * GROUP
STEPS = 4
CHUNKS = SEQ // STEPS
QUARTERS = 4
QP = PAIRS // QUARTERS
ROTATIONS = [(0, 1), (2, 3), (4, 5), (6, 7), (8, 9), (10, 11)]
assert 2 ** len(ROTATIONS) == CHUNKS
HEAD = 64
NEG = -1e30

TWO_PI = 2 * math.pi
C1 = 6.28125
C2 = 2029 / 1048576
C3 = TWO_PI - C1 - C2


def gate_unit(base, f):
    return base + 3 * f - 1


def trunk(nc, x_in, gains, wstream, lam_re, lam_im, log_dt, b_re, b_im, c_re, c_im, skip, out):
    with ExitStack() as ctx:
        def sb(name, shape, dt=F32):
            return ctx.enter_context(nc.sbuf_tensor(name, shape, dt))

        def sem(name):
            return ctx.enter_context(nc.semaphore(name))

        raw = sb("raw", [P, RAW, D])
        w_hi = sb("w_hi", [P, RING, D], F32R)
        w_lo = sb("w_lo", [P, RING, D], F32R)
        x = sb("x", [P, KB, SEQ])
        g_hi = sb("g_hi", [P, KB, SEQ], F32R)
        g_lo = sb("g_lo", [P, KB, SEQ], F32R)
        h_hi = sb("h_hi", [P, 2, SEQ], F32R)
        h_lo = sb("h_lo", [P, 2, SEQ], F32R)
        tmp = sb("tmp", [P, 2, 4, SEQ])
        rstd = sb("rstd", [P, SEQ])
        ssq = sb("ssq", [P, SEQ])
        gain = sb("gain", [P, 7, KB])
        ones = sb("ones", [P, P])
        eps = sb("eps", [P, 1])
        ident = sb("ident", [P, P])
        par = sb("par", [P, 20, PAIRS])
        par_i = sb("par_i", [P, PAIRS], I32)
        skip_col = sb("skip_col", [P, PAIRS])
        arena = sb("arena", [P, 26 * 1024])

        with nc.sbuf_tensor("low_part", [P, 4096], F32) as low:
            state_in = [low[:, :].rearrange("p (a s) -> p a s", a=PAIRS),
                        arena[:, 0:4096].rearrange("p (a s) -> p a s", a=PAIRS)]
        m_hi = sb("m_hi", [P, KB, SEQ], F32R)
        m_lo = sb("m_lo", [P, KB, SEQ], F32R)
        toep = arena[:, 4096:8192].rearrange("p (a s) -> p a s", a=PAIRS)
        state_out = arena[:, 8192:16384].rearrange("p (r a s) -> p r a s", r=2, a=PAIRS)
        b_pow = arena[:, 16384:24576].rearrange("p (r a s) -> p r a s", r=2, a=PAIRS)
        c_zero = arena[:, 24576:26624].rearrange("p (r a s) -> p r a s", r=2, a=PAIRS)
        b_raw = arena[:, 0:1024].rearrange("p (r a h) -> p r a h", r=2, a=PAIRS)
        c_raw = arena[:, 1024:2048].rearrange("p (r a h) -> p r a h", r=2, a=PAIRS)
        prep_tmp = [low[:, 2048 * k:2048 * k + 2048].rearrange("p (a j h) -> p a j h", a=PAIRS, j=STEPS)
                    for k in range(2)]
        powers = arena[:, 2048:2560].rearrange("p (w r a k) -> p w r a k", w=2, r=2, a=PAIRS)
        skip_diag = arena[0:CH, 2560:3584].rearrange("p (a c) -> p a c", a=PAIRS)
        rot = arena[:, 16384:20480].rearrange("p (r a c) -> p r a c", r=2, a=PAIRS)
        rho = arena[:, 20480:22528].rearrange("p (a c) -> p a c", a=PAIRS)
        u = arena[:, 22528:24576].rearrange("p (a c) -> p a c", a=PAIRS)
        rot_tmp = arena[:, 24576:26624].rearrange("p (r a c) -> p r a c", r=2, a=PAIRS)
        state_im = arena[:, 24576:25600].rearrange("p (k a c) -> p k a c", k=2, a=QP)
        pool_tmp = arena[:, 25600:26624].rearrange("p (k a c) -> p k a c", k=2, a=QP)
        mod = tmp[:, :, :, :].rearrange("p a b t -> p (a b t)").rearrange("p (k n) -> p k n", k=4)

        v = arena[:, 0:2048].rearrange("p (t n) -> p t n", t=2)
        qk = arena[:, 2048:3072].rearrange("p (b r t) -> p b r t", b=2, r=2)
        az = arena[:, 3072:3840].rearrange("p (h n) -> p h n", h=2)
        ez = arena[:, 3840:4608].rearrange("p (h n) -> p h n", h=2)
        sp_ = arena[:, 4608:5376].rearrange("p (h n) -> p h n", h=2)
        wts = arena[:, 5376:6144].rearrange("p (h n) -> p h n", h=2)
        ntri = arena[:, 8192:8320]
        nones = arena[:, 8320:8448]
        keep = arena[:, 8448:8576]
        big = arena[:, 8576:8704]
        r_col = arena[:, 8704:8706]
        ident_b = arena[:, 8708:8772].bitcast(BF16)
        big_b = arena[:, 8772:8836].bitcast(BF16)
        squares_out = arena[:, 10240:12288].rearrange("p (k t) -> p k t", k=KB)
        g_out = arena[:, 12288:14336].rearrange("p (k t) -> p k t", k=KB)

        acc = ctx.enter_context(nc.psum_tensor("acc", [P, 4, 512], F32))
        gu = ctx.enter_context(nc.psum_tensor("gu", [P, 2, 512], F32))
        mx = ctx.enter_context(nc.psum_tensor("mx", [P, 2, 512], F32))

        raw_in = [sem(f"raw_in{s}") for s in range(RAW)]
        hi_ready, lo_ready, unit_done = sem("hi_ready"), sem("lo_ready"), sem("unit_done")
        x_loaded = [sem("x_loaded0"), sem("x_loaded1")]
        gain_loaded, s5_loaded = sem("gain_loaded"), sem("s5_loaded")
        x_ready, ghi_ready, g_ready = sem("x_ready"), sem("ghi_ready"), sem("g_ready")
        sq_ready, sq_added = sem("sq_ready"), sem("sq_added")
        ssq_ready, sum_ready, rstd_ready = sem("ssq_ready"), sem("sum_ready"), sem("rstd_ready")
        root_ready = sem("root_ready")
        acc_ready = sem("acc_ready")
        gu_scaled, silu_ready, h_ready = sem("gu_scaled"), sem("silu_ready"), sem("h_ready")
        hhi_ready, hlo_ready = sem("hhi_ready"), sem("hlo_ready")
        const_ready, eps_ready = sem("const_ready"), sem("eps_ready")
        par_ready, par_act, par_dve = sem("par_ready"), sem("par_act"), sem("par_dve")
        matrices_ready, turned, kernels_done = sem("matrices_ready"), sem("turned"), sem("kernels_done")
        prep_dve, prep_act = sem("prep_dve"), sem("prep_act")
        rot_ready = sem("rot_ready")
        zeroed, own_done = sem("zeroed"), sem("own_done")
        u_ready, inflow_done, inflow_read = sem("u_ready"), sem("inflow_done"), sem("inflow_read")
        v_scanned, scan_read = sem("v_scanned"), sem("scan_read")
        real_ready, imag_ready = sem("real_ready"), sem("imag_ready")
        y_done, z_ready, z_turned = sem("y_done"), sem("z_ready"), sem("z_turned")
        m_hi_ready, m_ready = sem("m_hi_ready"), sem("m_ready")
        sg_ready, mix_read = sem("sg_ready"), sem("mix_read")
        rcol_done, rcol_ready, v_ready = sem("rcol_done"), sem("rcol_ready"), sem("v_ready")
        att_const, qk_ready, logits_done = sem("att_const"), sem("qk_ready"), sem("logits_done")
        az_ready, ez_ready, ln_ready = sem("az_ready"), sem("ez_ready"), sem("ln_ready")
        sp_ready, arg_done = sem("sp_ready"), sem("arg_done")
        wts_ready, o_done = sem("wts_ready"), sem("o_done")
        out_read = sem("out_read")
        dve_step, pool_step = sem("dve_step"), sem("pool_step")
        y_ready, stored = sem("y_ready"), sem("stored")

        def z_of(q):
            return u[:, QP * q:QP * (q + 1), :].rearrange("p a c -> p (a c)").rearrange(
                "p (j i h) -> p j i h", j=STEPS, i=4)

        def turned_z(q):
            return (gu, mx)[q // 2][:, q % 2, :].rearrange("p (j t c) -> p t c j", j=STEPS, t=2)

        def diagonal(t):
            return bass.AP(t.tensor, t.offset, [list(t.ap[0]), [384, 2], [256, 2], [1, P]])

        def z_banks(cb):
            return acc[:, 2:4, 0:384] if cb % 2 else mx[:, :, 0:384]

        block = ctx.enter_context(nc.Block())

        def slot(ring, unit):
            return unit % ring

        @block.sync
        def _(sp):
            def load(unit, s, turn):
                if turn is not None:
                    sp.wait_ge(lo_ready, turn)
                sp.dma_start(raw[:, s, :], wstream[unit] if isinstance(unit, int)
                             else wstream[bass.ds(unit, 1)].rearrange("a p n -> (a p) n")).then_inc(raw_in[s], 16)

            for s in range(RAW):
                load(s, s, None)
                if s == 0:
                    for h in range(2):
                        sp.dma_start(x[:, 4 * h:4 * h + 4, :], x_in[:, 4 * h:4 * h + 4, :]).then_inc(x_loaded[h], 16)
            for dst, src in ((par[:, 0, :], lam_re), (par[:, 1, :], lam_im),
                             (par[0:STATE, 2, :], log_dt[0:1, :].broadcast_to([STATE, PAIRS])),
                             (par[STATE:P, 2, :], log_dt[1:2, :].broadcast_to([STATE, PAIRS])),
                             (b_raw[:, 0], b_re), (b_raw[:, 1], b_im), (c_raw[:, 0], c_re), (c_raw[:, 1], c_im),
                             (skip_col[:, :], skip)):
                sp.dma_start(dst, src).then_inc(s5_loaded, 16)
            turns = UNITS // RAW
            with sp.Fori(1, turns) as i:
                for s in range(RAW):
                    load(RAW * i + s, s, RAW * i + (s - RAW + 1))
            for unit in range(RAW * turns, UNITS):
                load(unit, slot(RAW, unit), unit - RAW + 1)
            for d in range(KB):
                sp.wait_ge(y_ready, d + 1)
                sp.dma_start(out[:, d, :], g_out[:, d, :]).then_inc(stored, 16)
            sp.wait_ge(stored, 16 * KB)

        @block.scalar
        def _(act):
            def split_hi(unit, s_raw, s_ring, known=None):
                act.wait_ge(raw_in[s_raw], 16 * (known if known is not None else unit // RAW + 1))
                if not isinstance(unit, int) or unit >= RING:
                    act.wait_ge(unit_done, unit - RING + 1)
                act.activation(w_hi[:, s_ring, :], raw[:, s_raw, :], ACT.Copy).then_inc(hi_ready, 1)

            def split_after(done):
                if done + RING < UNITS:
                    n = done + RING
                    split_hi(n, n % RAW, n % RING)

            def silu(n, f):
                act.wait_ge(gu_scaled, NF * n + f + 1)
                act.activation(tmp[:, f % 2, 2, :], tmp[:, f % 2, 0, :], ACT.Silu).then_inc(silu_ready, 1)

            def round_h(n, f):
                act.wait_ge(h_ready, NF * n + f + 1)
                act.activation(h_hi[:, f % 2, :], tmp[:, f % 2, 3, :], ACT.Copy).then_inc(hhi_ready, 1)

            def root(n):
                act.wait_ge(sum_ready, n + 1)
                if n == 0:
                    act.wait_ge(eps_ready, 1)
                else:
                    act.wait_ge(rstd_ready, n)
                act.activation(rstd[:, :], mx[:, 1, 0:SEQ], ACT.Sqrt, scale=1.0 / D,
                               bias=eps[:, :]).then_inc(root_ready, 1)

            def ffn_first(n, norm_index):
                root(norm_index)
                split_after(FFN_BASE[n])
                silu(n, 0)
                split_after(FFN_BASE[n] + 1)
                round_h(n, 0)

            def ffn_second(n):
                g = gate_unit(FFN_BASE[n], 1)
                split_after(g)
                silu(n, 1)
                split_after(g + 1)
                round_h(n, 1)
                split_after(g + 2)

            def ffn_turn(n, i):
                base = FFN_BASE[n]
                for m in range(BODY):
                    g0 = gate_unit(base, 2 + m)
                    f0 = NF * n + 2 + m
                    for k in range(3):
                        if k == 1:
                            act.wait_ge(gu_scaled, BODY * i + (f0 + 1))
                            act.activation(tmp[:, m % 2, 2, :], tmp[:, m % 2, 0, :],
                                           ACT.Silu).then_inc(silu_ready, 1)
                            act.wait_ge(h_ready, BODY * i + (f0 + 1))
                            act.activation(h_hi[:, m % 2, :], tmp[:, m % 2, 3, :],
                                           ACT.Copy).then_inc(hhi_ready, 1)
                        n0 = g0 + k + RING
                        if isinstance(i, int) and n0 + 3 * BODY * i >= UNITS:
                            continue
                        act.wait_ge(raw_in[n0 % RAW], (16 * 3 * BODY // RAW) * i + 16 * (n0 // RAW + 1))
                        act.wait_ge(unit_done, 3 * BODY * i + (g0 + k + 1))
                        act.activation(w_hi[:, n0 % RING, :], raw[:, n0 % RAW, :],
                                       ACT.Copy).then_inc(hi_ready, 1)

            def ffn_loop(n, first, last):
                with act.Fori(first, last) as i:
                    ffn_turn(n, i)

            def scaled_block(n, d):
                if n == 0:
                    act.wait_ge(x_loaded[d // 4], 16)
                    act.wait_ge(gain_loaded, 16)
                else:
                    act.wait_ge(x_ready, KB * (n - 1) + d + 1)
                act.activation(g_hi[:, d, :], x[:, d, :], ACT.Copy,
                               scale=gain[:, n, d:d + 1]).then_inc(ghi_ready, 1)

            def squared_block(n, d):
                if d == 0:
                    if n:
                        act.wait_ge(sum_ready, n)
                    act.activation(ssq[:, :], x[:, d, :], ACT.Square).then_inc(sq_ready, 1)
                else:
                    if d >= 3:
                        act.wait_ge(sq_added, (KB - 1) * n + d - 2)
                    act.activation(tmp[:, d % 2, 0, :], x[:, d, :], ACT.Square).then_inc(sq_ready, 1)

            def norm_block(n, d):
                scaled_block(n, d)
                squared_block(n, d)

            def norm(n):
                for d in range(KB):
                    scaled_block(n, d)
                    if d:
                        squared_block(n, d - 1)
                squared_block(n, KB - 1)

            def s5_time_steps():
                pr = lambda k: par[:, k, :]
                act.wait_ge(s5_loaded, 16 * 9)
                act.activation(pr(3), pr(2), ACT.Exp).then_inc(par_act, 1)

            def s5_exponentials():
                pr = lambda k: par[:, k, :]
                act.wait_ge(par_ready, 2)
                act.activation(pr(6), pr(4), ACT.Exp).then_inc(par_act, 1)
                act.wait_ge(par_ready, 3)
                act.activation(pr(8), pr(7), ACT.Abs).then_inc(par_act, 1)
                act.activation(pr(9), pr(7), ACT.Sin).then_inc(par_act, 1)
                act.wait_ge(par_ready, 4)
                act.activation(pr(10), pr(8), ACT.Sin).then_inc(par_act, 1)

            def s5_prepare():
                for k in range(1, 16, 2):
                    act.wait_ge(turned, k + 1)
                    act.activation(state_in[k // 8][:, 4 * (k % 8):4 * (k % 8) + 4, :],
                                   mx[:, 1, :].rearrange("p (a s) -> p a s", a=4), ACT.Copy).then_inc(prep_act, 1)

            def s5_mixer():
                b = S5_BASE
                for k in range(S5_IN):
                    if k == 2:
                        root(1)
                    split_after(b + k)

                def gelu(q):
                    act.wait_ge(y_done, q + 1)
                    act.activation(z_of(q), acc[:, q, :].rearrange("p (i j h) -> p j i h", i=4, j=STEPS),
                                   ACT.Gelu_apprx_tanh).then_inc(z_ready, 1)

                def round_z(q):
                    act.wait_ge(z_turned, q + 1)
                    act.activation(m_hi[:, 2 * q:2 * q + 2, :].rearrange("p t (c j) -> p t c j", j=STEPS),
                                   turned_z(q), ACT.Copy).then_inc(m_hi_ready, 2)

                gelu(0)
                gelu(1)
                gelu(2)
                round_z(0)
                round_z(1)
                gelu(3)
                round_z(2)
                round_z(3)
                for cb in range(KB):
                    if cb:
                        norm_block(2, cb - 1)
                    split_after(b + KB + 2 * cb)
                    act.wait_ge(unit_done, b + KB + 2 * cb + 2)
                    act.activation(tmp[:, cb % 2, 2, :], gu[:, cb % 2, SEQ:2 * SEQ],
                                   ACT.Sigmoid).then_inc(sg_ready, 1)
                    split_after(b + KB + 2 * cb + 1)
                norm_block(2, KB - 1)

            def attention():
                b = ATT_BASE
                for k in range(3):
                    split_after(b + k)
                root(4)
                for k in range(3, KB):
                    split_after(b + k)
                q_ = b + KB

                def values(t, half):
                    act.activation(v[:, t, 512 * half:512 * half + 512], acc[:, 2 * t + half, :], ACT.Copy,
                                   scale=r_col[:, t:t + 1]).then_inc(v_ready, 1)

                def exponential(cb):
                    act.wait_ge(logits_done, cb + 1)
                    if cb:
                        act.wait_ge(sp_ready, cb)
                    act.activation(az, z_banks(cb), ACT.Abs).then_inc(az_ready, 1)
                    act.wait_ge(az_ready, cb + 1)
                    act.activation(ez, az, ACT.Exp, scale=-1.0).then_inc(ez_ready, 1)

                def logarithm(cb):
                    act.wait_ge(ez_ready, cb + 1)
                    act.activation(az, ez, ACT.Ln, bias=1.0).then_inc(ln_ready, 1)

                def weights(cb):
                    act.wait_ge(arg_done, cb + 1)
                    if cb:
                        act.wait_ge(o_done, cb)
                    act.activation(wts, z_banks(cb), ACT.Exp).then_inc(wts_ready, 1)

                act.wait_ge(rcol_ready, 1)
                values(0, 0)
                values(0, 1)
                split_after(q_)
                values(1, 0)
                values(1, 1)
                split_after(q_ + 1)
                split_after(q_ + 2)
                exponential(0)
                logarithm(0)
                split_after(q_ + 3)
                for cb in range(KB):
                    if cb + 2 < KB:
                        split_after(q_ + 2 * cb + 4)
                    if cb + 1 < KB:
                        exponential(cb + 1)
                    weights(cb)
                    if cb + 1 < KB:
                        logarithm(cb + 1)
                    if cb + 2 < KB:
                        split_after(q_ + 2 * cb + 5)
                    act.wait_ge(o_done, cb + 1)
                    act.activation(m_hi[:, cb, :], acc[:, cb % 2, 0:SEQ], ACT.Copy).then_inc(m_hi_ready, 1)
                for cb in range(KB):
                    if cb:
                        norm_block(5, cb - 1)
                    split_after(b + 3 * KB + cb)
                norm_block(5, KB - 1)

            def last_squares():
                for d in range(KB):
                    act.wait_ge(x_ready, 5 * KB + d + 1)
                    act.activation(squares_out[:, d, :], x[:, d, :], ACT.Square).then_inc(sq_ready, 1)

            act.dma_start(gain[:, :, :], gains).then_inc(gain_loaded, 16)
            split_hi(0, 0, 0)
            for d in range(KB):
                scaled_block(0, d)
            split_hi(1, 1, 1)
            for d in range(KB):
                squared_block(0, d)
            for unit in (2, 3):
                split_hi(unit, unit % RAW, unit % RING)
            ffn_first(0, 0)
            s5_time_steps()
            ffn_second(0)
            s5_exponentials()
            ffn_loop(0, 0, PREP_TURN)
            s5_prepare()
            ffn_loop(0, PREP_TURN, TURNS)
            for d in range(KB):
                scaled_block(1, d)
            for d in range(KB):
                squared_block(1, d)
            split_after(FFN_BASE[0] + FFN_UNITS - 1)
            s5_mixer()
            for n in (1, 2, 3):
                ffn_first(n, (2, 3, 5)[n - 1])
                ffn_second(n)
                ffn_loop(n, 0, TURNS - (n == 3))
                if n == 3:
                    ffn_turn(n, TURNS - 1)
                else:
                    norm(n + 2)
                split_after(FFN_BASE[n] + FFN_UNITS - 1)
                if n == 2:
                    attention()
            last_squares()
            root(6)

        @block.vector
        def _(dve):
            count = [0]

            def step(ins):
                count[0] += 1
                ins.then_inc(dve_step, 1)
                dve.wait_ge(dve_step, count[0])

            def split_lo(n):
                dve.wait_ge(hi_ready, n + 1)
                dve.tensor_tensor(w_lo[:, n % RING, :], raw[:, n % RAW, :], w_hi[:, n % RING, :].bitcast(F32),
                                  ALU.subtract).then_inc(lo_ready, 1)

            def split_after(done):
                if done + RING < UNITS:
                    split_lo(done + RING)

            def scale_gu(m, wait_units):
                dve.wait_ge(unit_done, wait_units)
                dve.tensor_tensor(tmp[:, m, 0:2, :], gu[:, m, :].rearrange("p (r t) -> p r t", r=2),
                                  rstd[:, :].unsqueeze(1).broadcast_to([P, 2, SEQ]), ALU.mult).then_inc(gu_scaled, 1)

            def hidden(m, n_f):
                dve.wait_ge(gu_scaled, n_f)
                dve.wait_ge(silu_ready, n_f)
                dve.tensor_tensor(tmp[:, m, 3, :], tmp[:, m, 2, :], tmp[:, m, 1, :], ALU.mult).then_inc(h_ready, 1)
                dve.wait_ge(h_ready, n_f)
                dve.wait_ge(hhi_ready, n_f)
                dve.tensor_tensor(h_lo[:, m, :], tmp[:, m, 3, :], h_hi[:, m, :].bitcast(F32),
                                  ALU.subtract).then_inc(hlo_ready, 1)

            def ffn_first(n, norm_index):
                root(norm_index)
                scale_gu(0, FFN_BASE[n] + 2)
                split_after(FFN_BASE[n])
                hidden(0, NF * n + 1)
                split_after(FFN_BASE[n] + 1)

            def ffn_second(n):
                g = gate_unit(FFN_BASE[n], 1)
                split_after(g)
                scale_gu(1, g + 2)
                split_after(g + 1)
                hidden(1, NF * n + 2)
                split_after(g + 2)

            def ffn_turn(n, i):
                base = FFN_BASE[n]
                for m in range(BODY):
                    g0 = gate_unit(base, 2 + m)
                    f1 = BODY * i + (NF * n + 2 + m + 1)
                    for k in range(3):
                        if k == 1:
                            scale_gu(m % 2, 3 * BODY * i + (g0 + 2))
                            hidden(m % 2, f1)
                        n0 = g0 + k + RING
                        if isinstance(i, int) and n0 + 3 * BODY * i >= UNITS:
                            continue
                        dve.wait_ge(hi_ready, 3 * BODY * i + (n0 + 1))
                        dve.tensor_tensor(w_lo[:, n0 % RING, :], raw[:, n0 % RAW, :],
                                          w_hi[:, n0 % RING, :].bitcast(F32),
                                          ALU.subtract).then_inc(lo_ready, 1)

            def ffn_loop(n, first, last):
                with dve.Fori(first, last) as i:
                    ffn_turn(n, i)

            def root(n):
                dve.wait_ge(root_ready, n + 1)
                dve.reciprocal(rstd[:, :], rstd[:, :]).then_inc(rstd_ready, 1)
                dve.wait_ge(rstd_ready, n + 1)

            def low_part(n, d):
                dve.wait_ge(ghi_ready, KB * n + d + 1)
                dve.scalar_tensor_tensor(g_lo[:, d, :], x[:, d, :], gain[:, n, d:d + 1], g_hi[:, d, :].bitcast(F32),
                                         ALU.mult, ALU.subtract).then_inc(g_ready, 1)

            def ffn_update(n, bank):
                if bank < 3:
                    dve.wait_ge(acc_ready, 3 * n + bank + 1)
                else:
                    dve.wait_ge(unit_done, FFN_BASE[n] + FFN_UNITS)
                two = x[:, 2 * bank:2 * bank + 2, :].rearrange("p k t -> p (k t)")
                dve.scalar_tensor_tensor(two, acc[:, bank, :], 0.5, two, ALU.mult, ALU.add).then_inc(x_ready, 2)

            def norm(n, layer):
                for bank in range(5):
                    if bank < 4:
                        ffn_update(layer, bank)
                    if bank:
                        dve.wait_ge(x_ready, KB * (n - 1) + 2 * bank)
                        low_part(n, 2 * bank - 2)
                        low_part(n, 2 * bank - 1)

            def s5_prepare():
                def copy_turned(k):
                    dve.wait_ge(turned, k + 1)
                    dve.tensor_copy(state_in[k // 8][:, 4 * (k % 8):4 * (k % 8) + 4, :],
                                    mx[:, 0, :].rearrange("p (a s) -> p a s", a=4)).then_inc(prep_dve, 1)

                for k in range(0, 8, 2):
                    copy_turned(k)
                dve.wait_ge(zeroed, 1)
                for k in range(8):
                    dve.wait_ge(kernels_done, k + 1)
                    src = mx[0:CH, k % 2, :].rearrange("p (a s) -> p a s", a=4)
                    for j in range(STEPS):
                        last = dve.tensor_copy(toep[CH * j:CH * (j + 1), 4 * k:4 * k + 4, CH * j:P],
                                               src[:, :, 0:P - CH * j])
                    last.then_inc(prep_dve, 1)
                for k in range(8, 16, 2):
                    copy_turned(k)

            def s5_scale_u(q):
                dve.wait_ge(unit_done, S5_BASE + 2 * q + 2)
                if q == 0:
                    dve.wait_ge(rot_ready, 1)
                for j in range(STEPS):
                    for i in range(4):
                        src = acc[CH * i:CH * (i + 1), q, :].rearrange("p (t c j) -> p t c j", t=2, j=STEPS)[:, :, :, j]
                        r = rstd[CH * i:CH * (i + 1), :].rearrange("p (c j) -> p c j", j=STEPS)[:, :, j]
                        dst = u[CH * j:CH * (j + 1), QP * q:QP * (q + 1), :].rearrange(
                            "p (t i) c -> p t i c", t=2)[:, :, i, :]
                        last = dve.tensor_tensor(dst, src, r.unsqueeze(1).broadcast_to([CH, 2, CHUNKS]), ALU.mult)
                last.then_inc(u_ready, 1)

            def s5_scan(q):
                dve.wait_ge(inflow_done, q + 1)
                if q:
                    dve.wait_ge(scan_read, q)
                    dve.wait_ge(real_ready, q)
                else:
                    dve.wait_ge(hlo_ready, NF)
                re, im = ((gu, mx)[q % 2][:, r, :] for r in range(2))
                cos, sin = (rot[:, r, QP * q:QP * (q + 1), :].rearrange("p a c -> p (a c)") for r in range(2))
                dve.tensor_tensor(mod[:, 0, :], re, cos, ALU.mult)
                dve.tensor_tensor(mod[:, 1, :], im, sin, ALU.mult)
                dve.tensor_tensor(mod[:, 2, :], im, cos, ALU.mult)
                step(dve.tensor_tensor(mod[:, 3, :], re, sin, ALU.mult))
                dve.tensor_tensor(mod[:, 0, :], mod[:, 0, :], mod[:, 1, :], ALU.add).then_inc(inflow_read, 1)
                step(dve.tensor_tensor(mod[:, 2, :], mod[:, 2, :], mod[:, 3, :], ALU.subtract))
                decay = rho[:, QP * q:QP * (q + 1), :].rearrange("p a c -> p (a c)")
                dve.tensor_tensor_scan(mod[:, 1, :], decay, mod[:, 0, :], 0.0, ALU.mult, ALU.add)
                dve.tensor_tensor_scan(mod[:, 3, :], decay, mod[:, 2, :], 0.0, ALU.mult, ALU.add).then_inc(v_scanned, 1)

            def s5_real(q):
                dve.wait_ge(v_scanned, q + 1)
                real = u[:, QP * q:QP * (q + 1), :]
                dve.wait_ge(own_done, q + 1)
                dve.memset(real[:, :, 0:1], 0.0)
                cos, sin = (rot[:, r, QP * q:QP * (q + 1), :].rearrange("p a c -> p (a c)") for r in range(2))
                dve.tensor_tensor(mod[:, 0, :], mod[:, 1, :], cos, ALU.mult)
                step(dve.tensor_tensor(mod[:, 2, :], mod[:, 3, :], sin, ALU.mult))
                a_, b_ = (mod[:, k, :].rearrange("p (a c) -> p a c", a=QP)[:, :, 0:CHUNKS - 1] for k in (0, 2))
                dve.tensor_tensor(real[:, :, 1:CHUNKS], a_, b_, ALU.subtract).then_inc(real_ready, 1)

            def s5_low(q):
                dve.wait_ge(m_hi_ready, 2 * q + 2)
                m = (t[:, 2 * q:2 * q + 2, :].rearrange("p t (c j) -> p t c j", j=STEPS) for t in (m_lo, m_hi))
                lo, hi = m
                for t in range(2):
                    last = dve.tensor_tensor(lo[:, t], turned_z(q)[:, t], hi[:, t].bitcast(F32), ALU.subtract)
                last.then_inc(m_ready, 2)

            def s5_mixer():
                b = S5_BASE
                split_after(b)
                split_after(b + 1)
                root(1)
                split_after(b + 2)
                s5_scale_u(0)
                split_after(b + 3)
                s5_scale_u(1)
                s5_scan(0)
                s5_real(0)
                s5_scale_u(2)
                s5_scan(1)
                s5_real(1)
                split_after(b + 4)
                s5_scale_u(3)
                s5_scan(2)
                s5_real(2)
                split_after(b + 5)
                s5_scan(3)
                s5_real(3)
                split_after(b + 6)
                split_after(b + 7)
                for q in range(QUARTERS):
                    s5_low(q)
                for cb in range(KB):
                    split_after(b + KB + 2 * cb)
                    dve.wait_ge(sg_ready, cb + 1)
                    if cb >= 2:
                        dve.wait_ge(x_ready, KB + cb - 1)
                    dve.tensor_tensor(tmp[:, cb % 2, 3, :], gu[:, cb % 2, 0:SEQ], tmp[:, cb % 2, 2, :],
                                      ALU.mult).then_inc(mix_read, 1)
                    dve.wait_ge(mix_read, cb + 1)
                    dve.tensor_tensor(x[:, cb, :], x[:, cb, :], tmp[:, cb % 2, 3, :], ALU.add).then_inc(x_ready, 1)
                    split_after(b + KB + 2 * cb + 1)
                    if cb:
                        low_part(2, cb - 1)
                low_part(2, KB - 1)

            def attention():
                b = ATT_BASE
                for k in range(3):
                    split_after(b + k)
                root(4)
                for k in range(3, KB):
                    split_after(b + k)
                dve.wait_ge(rcol_done, 1)
                dve.tensor_copy(r_col, mx[:, 0, 0:2]).then_inc(rcol_ready, 1)

                def scale_qk(cb):
                    dve.wait_ge(unit_done, b + KB + 2 * cb + 2)
                    dve.scalar_tensor_tensor(qk[:, cb % 2, 0, :], gu[:, cb % 2, 0:SEQ], HEAD ** -0.5, rstd[:, :],
                                             ALU.mult, ALU.mult)
                    dve.tensor_tensor(qk[:, cb % 2, 1, :], gu[:, cb % 2, SEQ:2 * SEQ], rstd[:, :],
                                      ALU.mult).then_inc(qk_ready, 1)

                def softplus(cb):
                    dve.wait_ge(ln_ready, cb + 1)
                    if cb:
                        dve.wait_ge(arg_done, cb)
                    step(dve.scalar_tensor_tensor(sp_, z_banks(cb), 0.0, az, ALU.max, ALU.add))
                    diag = diagonal(sp_)
                    dve.tensor_tensor(diag, diag, keep.unsqueeze(1).unsqueeze(1).broadcast_to([P, 2, 2, P]),
                                      ALU.mult).then_inc(sp_ready, 1)

                def low_o(cb):
                    dve.wait_ge(m_hi_ready, KB + cb + 1)
                    dve.tensor_tensor(m_lo[:, cb, :], acc[:, cb % 2, 0:SEQ], m_hi[:, cb, :].bitcast(F32),
                                      ALU.subtract).then_inc(m_ready, 1)

                q_ = b + KB
                split_after(q_)
                scale_qk(0)
                split_after(q_ + 1)
                split_after(q_ + 2)
                scale_qk(1)
                dve.wait_ge(att_const, 1)
                softplus(0)
                split_after(q_ + 3)
                for cb in range(KB):
                    if cb + 2 < KB:
                        split_after(q_ + 2 * cb + 4)
                    if cb:
                        low_o(cb - 1)
                    if cb + 2 < KB:
                        scale_qk(cb + 2)
                    if cb + 1 < KB:
                        softplus(cb + 1)
                    if cb + 2 < KB:
                        split_after(q_ + 2 * cb + 5)
                low_o(KB - 1)
                for cb in range(KB):
                    dve.wait_ge(unit_done, b + 3 * KB + cb + 1)
                    dve.tensor_tensor(x[:, cb, :], x[:, cb, :], gu[:, cb % 2, 0:SEQ], ALU.add).then_inc(x_ready, 1)
                    if cb:
                        low_part(5, cb - 1)
                    split_after(b + 3 * KB + cb)
                low_part(5, KB - 1)

            dve.memset(eps[:, :], EPS).then_inc(eps_ready, 1)
            split_lo(0)
            for d in range(KB):
                low_part(0, d)
            split_lo(1)
            split_lo(2)
            split_lo(3)
            ffn_first(0, 0)
            dve.wait_ge(par_ready, 1)
            dve.reciprocal(par[:, 11, :], par[:, 18, :]).then_inc(par_dve, 1)
            ffn_second(0)
            ffn_loop(0, 0, PREP_TURN)
            s5_prepare()
            ffn_loop(0, PREP_TURN, TURNS)
            norm(1, 0)
            split_after(FFN_BASE[0] + FFN_UNITS - 1)
            s5_mixer()
            for n in (1, 2, 3):
                ffn_first(n, (2, 3, 5)[n - 1])
                ffn_second(n)
                ffn_loop(n, 0, TURNS - (n == 3))
                if n == 3:
                    ffn_turn(n, TURNS - 1)
                else:
                    norm(n + 2, n)
                split_after(FFN_BASE[n] + FFN_UNITS - 1)
                if n == 2:
                    attention()
            for bank in range(4):
                ffn_update(3, bank)
            root(6)
            dve.wait_ge(x_ready, 6 * KB)
            for d in range(KB):
                dve.scalar_tensor_tensor(g_out[:, d, :], x[:, d, :], gain[:, 6, d:d + 1], rstd[:, :],
                                         ALU.mult, ALU.mult).then_inc(y_ready, 1)

        @block.tensor
        def _(pe):
            def three(dst, unit_slot, cols, hi, lo, start, stop, check=False):
                a, b_ = w_hi[:, unit_slot, cols], w_lo[:, unit_slot, cols]
                pe.matmul(dst, a, hi, start=start, stop=False, skip_group_check=check)
                pe.matmul(dst, a, lo, start=False, stop=False, skip_group_check=check)
                return pe.matmul(dst, b_, hi, start=False, stop=stop, skip_group_check=check)

            def column_unit(dst, s):
                for kb in range(KB):
                    last = three(dst, s, slice(P * kb, P * kb + P), g_hi[:, kb, :], g_lo[:, kb, :],
                                 kb == 0, kb == KB - 1)
                last.then_inc(unit_done, 1)

            def two_units(bank, n, ready, first, hi, lo, after_third=None):
                pe.wait_ge(lo_ready, n + 1)
                for kb in range(KB):
                    pe.wait_ge(ready, first + kb + 1)
                    if kb == 0:
                        pe.wait_ge(lo_ready, n + 2)
                    for r in range(2):
                        mm = three(bank[:, SEQ * r:SEQ * (r + 1)], (n + r) % RING, slice(P * kb, P * kb + P),
                                   hi[:, kb, :], lo[:, kb, :], kb == 0 and r == 0, kb == KB - 1, check=True)
                        if kb == KB - 1:
                            mm.then_inc(unit_done, 1)
                    if kb == 2 and after_third:
                        after_third()

            def down_unit(s, m, first=False, last_block=False):
                for d in range(KB):
                    mm = three(acc[:, d // 2, SEQ * (d % 2):SEQ * (d % 2 + 1)], s, slice(P * d, P * d + P),
                               h_hi[:, m, :], h_lo[:, m, :], first and d % 2 == 0, last_block, check=True)
                    if last_block and d % 2 and d < KB - 1:
                        mm.then_inc(acc_ready, 1)
                mm.then_inc(unit_done, 1)

            def squares(n):
                pe.wait_ge(ssq_ready, n + 1)
                if n == 0:
                    pe.wait_ge(const_ready, 1)
                pe.matmul(mx[:, 1, 0:SEQ], ones[:, :], ssq[:, :], start=True, stop=True).then_inc(sum_ready, 1)

            def ffn_first(n, norm_index):
                if n:
                    pe.wait_ge(gu_scaled, NF * n - 1)
                if n == 1:
                    pe.wait_ge(mix_read, KB - 1)
                if n == 3:
                    pe.wait_ge(x_ready, 5 * KB - 1)
                if n:
                    two_units(gu[:, 0, :], FFN_BASE[n], g_ready, KB * norm_index, g_hi, g_lo)
                else:
                    pe.wait_ge(lo_ready, 1)
                    for kb in range(KB):
                        pe.wait_ge(g_ready, kb + 1)
                        mm = three(gu[:, 0, 0:SEQ], 0, slice(P * kb, P * kb + P), g_hi[:, kb, :], g_lo[:, kb, :],
                                   kb == 0, kb == KB - 1)
                    mm.then_inc(unit_done, 1)
                    pe.wait_ge(lo_ready, 2)
                    column_unit(gu[:, 0, SEQ:2 * SEQ], 1)
                squares(norm_index)

            def ffn_second(n):
                g = gate_unit(FFN_BASE[n], 1)
                if n:
                    pe.wait_ge(gu_scaled, NF * n)
                if n == 1:
                    pe.wait_ge(mix_read, KB)
                if n == 3:
                    pe.wait_ge(x_ready, 5 * KB)
                pe.wait_ge(lo_ready, g + 1)
                column_unit(gu[:, 1, 0:SEQ], g % RING)
                pe.wait_ge(lo_ready, g + 2)
                column_unit(gu[:, 1, SEQ:2 * SEQ], (g + 1) % RING)
                pe.wait_ge(lo_ready, g + 3)
                pe.wait_ge(hlo_ready, NF * n + 1)
                down_unit((g + 2) % RING, 0, first=True)

            def ffn_loop(n, first, last):
                base = FFN_BASE[n]
                with pe.Fori(first, last) as i:
                    for m in range(BODY):
                        g0 = gate_unit(base, 2 + m)
                        f0 = NF * n + 2 + m
                        pe.wait_ge(gu_scaled, BODY * i + (f0 - 1))
                        pe.wait_ge(lo_ready, 3 * BODY * i + (g0 + 1))
                        column_unit(gu[:, m % 2, 0:SEQ], g0 % RING)
                        pe.wait_ge(lo_ready, 3 * BODY * i + (g0 + 2))
                        column_unit(gu[:, m % 2, SEQ:2 * SEQ], (g0 + 1) % RING)
                        pe.wait_ge(lo_ready, 3 * BODY * i + (g0 + 3))
                        pe.wait_ge(hlo_ready, BODY * i + f0)
                        down_unit((g0 + 2) % RING, (m + 1) % 2)

            def ffn_tail(n):
                g = gate_unit(FFN_BASE[n], NF - 1)
                pe.wait_ge(lo_ready, g + 4)
                pe.wait_ge(hlo_ready, NF * n + NF)
                down_unit((g + 3) % RING, (NF - 1) % 2, last_block=True)

            def s5_prepare():
                pe.wait_ge(matrices_ready, 1)
                pe.wait_ge(const_ready, 1)

                def turn(k):
                    for a in range(4):
                        mm = pe.transpose(mx[:, k % 2, P * a:P * (a + 1)], b_pow[:, k // 8, 4 * (k % 8) + a, :],
                                          ident[:, :])
                    mm.then_inc(turned, 1)

                for k in range(8):
                    if k >= 2:
                        pe.wait_ge((prep_dve, prep_act)[k % 2], k // 2)
                    turn(k)
                for k in range(8):
                    if k == 1:
                        pe.wait_ge(prep_act, 4)
                    else:
                        pe.wait_ge(prep_dve, 4 + max(k - 1, 0))
                    for a in range(4):
                        pair = 4 * k + a
                        for r in range(2):
                            pe.matmul(mx[0:CH, k % 2, P * a:P * a + CH], b_pow[:, r, pair, 3 * CH:4 * CH],
                                      c_zero[:, r, pair, :], start=a == 0 and r == 0, stop=False,
                                      skip_group_check=True)
                        for r in range(2):
                            pe.matmul(mx[0:CH, k % 2, P * a + CH:P * (a + 1)], b_pow[:, r, pair, 3 * CH:4 * CH],
                                      state_out[:, r, pair, 0:3 * CH], start=False, stop=False, skip_group_check=True)
                    mm = pe.matmul(mx[0:CH, k % 2, :].rearrange("p (a s) -> p a s", a=4)[:, :, 0:CH],
                                   ident[0:CH, 0:CH], skip_diag[:, 4 * k:4 * k + 4, :], start=False, stop=True,
                                   skip_group_check=True)
                    mm.then_inc(kernels_done, 1)
                for k in range(8, 16):
                    if k == 8:
                        pe.wait_ge(prep_dve, 11)
                    elif k % 2 == 0:
                        pe.wait_ge(prep_dve, 8 + k // 2)
                    elif k == 9:
                        pe.wait_ge(prep_dve, 12)
                    else:
                        pe.wait_ge(prep_act, k // 2)
                    turn(k)

            def s5_inflow(q):
                pe.wait_ge(u_ready, q + 1)
                if q >= 2:
                    pe.wait_ge(inflow_read, q - 1)
                bank = (gu, mx)[q % 2]
                for a in range(QP):
                    for r in range(2):
                        mm = pe.matmul(bank[:, r, CHUNKS * a:CHUNKS * (a + 1)], state_in[r][:, QP * q + a, :],
                                       u[:, QP * q + a, :], start=True, stop=True)
                mm.then_inc(inflow_done, 1)
                for a in range(QP):
                    mm = pe.matmul(y_of(q, a), u[:, QP * q + a, :], toep[:, QP * q + a, :],
                                   start=a % 4 == 0, stop=False, skip_group_check=True)
                mm.then_inc(own_done, 1)

            def y_of(q, a):
                rows = slice(CHUNKS * (a // 4), CHUNKS * (a // 4 + 1))
                return acc[rows, q, P * (a % 4):P * (a % 4 + 1)]

            def s5_outflow(q):
                pe.wait_ge(real_ready, q + 1)
                pe.wait_ge(imag_ready, q + 1)
                for a in range(QP):
                    for r in range(2):
                        state = (u[:, QP * q + a, :], state_im[:, q % 2, a, :])[r]
                        mm = pe.matmul(y_of(q, a), state, state_out[:, r, QP * q + a, :],
                                       start=False, stop=r == 1, skip_group_check=True)
                mm.then_inc(y_done, 1)

            def s5_turn(q):
                pe.wait_ge(z_ready, q + 1)
                zq = u[:, QP * q:QP * (q + 1), :].rearrange("p a c -> p (a c)")
                for j in range(STEPS):
                    mm = pe.transpose((gu, mx)[q // 2][:, q % 2, P * j:P * (j + 1)], zq[:, P * j:P * (j + 1)], ident[:, :])
                mm.then_inc(z_turned, 1)

            def s5_mixer():
                b = S5_BASE

                def project(k):
                    pe.wait_ge(lo_ready, b + k + 1)
                    column_unit(acc[:, k // 2, SEQ * (k % 2):SEQ * (k % 2 + 1)], (b + k) % RING)

                two_units(acc[:, 0, :], b, g_ready, KB, g_hi, g_lo)
                project(2)
                squares(1)
                project(3)
                project(4)
                project(5)
                project(6)
                s5_inflow(0)
                s5_inflow(1)
                project(7)
                s5_outflow(0)
                s5_inflow(2)
                s5_outflow(1)
                s5_inflow(3)
                s5_outflow(2)
                s5_turn(0)
                s5_turn(1)
                s5_outflow(3)
                s5_turn(2)
                for cb in range(KB):
                    n = b + KB + 2 * cb
                    if cb == 0:
                        two_units(gu[:, 0, :], n, m_ready, 0, m_hi, m_lo, after_third=lambda: s5_turn(3))
                        continue
                    if cb == 1:
                        pe.wait_ge(m_ready, KB)
                    if cb >= 2:
                        pe.wait_ge(mix_read, cb - 1)
                    for r in range(2):
                        pe.wait_ge(lo_ready, n + r + 1)
                        output_unit(gu[:, cb % 2, SEQ * r:SEQ * (r + 1)], (n + r) % RING)

            def output_unit(dst, s):
                for kb in range(KB):
                    mm = three(dst, s, slice(P * kb, P * kb + P), m_hi[:, kb, :], m_lo[:, kb, :],
                               kb == 0, kb == KB - 1)
                mm.then_inc(unit_done, 1)

            def attention():
                b = ATT_BASE
                for kb in range(KB):
                    pe.wait_ge(lo_ready, b + kb + 1)
                    pe.wait_ge(g_ready, 4 * KB + kb + 1)
                    s = (b + kb) % RING
                    for t in range(2):
                        gh, gl = g_hi[:, kb, P * t:P * (t + 1)], g_lo[:, kb, P * t:P * (t + 1)]
                        for half in range(2):
                            if kb == 0:
                                pe.wait_ge(x_ready, 3 * KB + 2 * (2 * t + half) + 2)
                            cols = slice(512 * half, 512 * half + 512)
                            dst = acc[:, 2 * t + half, :]
                            pe.matmul(dst, gh, w_hi[:, s, cols], start=kb == 0, stop=False)
                            pe.matmul(dst, gh, w_lo[:, s, cols], start=False, stop=False)
                            mm = pe.matmul(dst, gl, w_hi[:, s, cols], start=False, stop=kb == KB - 1)
                    mm.then_inc(unit_done, 1)
                    if kb == 2:
                        squares(4)
                pe.wait_ge(rstd_ready, 5)
                for t in range(2):
                    mm = pe.matmul(mx[:, 0, t:t + 1], rstd[0:1, P * t:P * (t + 1)], ones[0:1, 0:1],
                                   start=True, stop=True)
                mm.then_inc(rcol_done, 1)

                def project(cb, r):
                    n = b + KB + 2 * cb + r
                    pe.wait_ge(lo_ready, n + 1)
                    if cb >= 2:
                        pe.wait_ge(qk_ready, cb - 1)
                    column_unit(gu[:, cb % 2, SEQ * r:SEQ * (r + 1)], n % RING)

                def logits(cb):
                    pe.wait_ge(qk_ready, cb + 1)
                    if cb == 0:
                        pe.wait_ge(rcol_ready, 1)
                    elif cb == 1:
                        pe.wait_ge(v_ready, 4)
                    else:
                        pe.wait_ge(wts_ready, cb - 1)
                    z = z_banks(cb)
                    for hh in range(2):
                        rows = slice(HEAD * hh, HEAD * (hh + 1))
                        q_, k_ = qk[rows, cb % 2, 0, :], qk[rows, cb % 2, 1, :]
                        pe.matmul(z[:, hh, 0:SEQ], k_[:, 0:P], q_, start=True, stop=False, skip_group_check=True)
                        mm = pe.matmul(z[:, hh, SEQ:384], k_[:, P:SEQ], q_[:, P:SEQ], start=False, stop=False,
                                       skip_group_check=True)
                    mm.then_inc(logits_done, 1)

                def arguments(cb):
                    pe.wait_ge(sp_ready, cb + 1)
                    z = z_banks(cb)
                    for hh in range(2):
                        s_ = sp_[:, hh, :]
                        args = [(z[:, hh, 0:SEQ], ntri, s_[:, 0:SEQ]), (z[:, hh, P:SEQ], nones, s_[:, SEQ:384]),
                                (z[:, hh, SEQ:384], ntri, s_[:, SEQ:384]),
                                (z[:, hh, 0:P], ident_b, big_b), (z[:, hh, SEQ:384], ident_b, big_b)]
                        for k, (dst, a, m_) in enumerate(args):
                            mm = pe.matmul(dst, a, m_, start=False, stop=k == 4, skip_group_check=True)
                    mm.then_inc(arg_done, 1)

                def outputs(cb):
                    pe.wait_ge(wts_ready, cb + 1)
                    if cb >= 2:
                        pe.wait_ge(m_ready, KB + cb - 1)
                    for hh in range(2):
                        c0 = P * cb + HEAD * hh
                        dst = acc[HEAD * hh:HEAD * (hh + 1), cb % 2, 0:SEQ]
                        pe.matmul(dst, v[:, 0, c0:c0 + HEAD], wts[:, hh, 0:SEQ], start=True, stop=False,
                                  skip_group_check=True)
                        mm = pe.matmul(dst[:, P:SEQ], v[:, 1, c0:c0 + HEAD], wts[:, hh, SEQ:384], start=False,
                                       stop=True, skip_group_check=True)
                    mm.then_inc(o_done, 1)

                def first_outputs(kbs):
                    n = b + 3 * KB
                    pe.wait_ge(lo_ready, n + 2)
                    pe.wait_ge(qk_ready, KB)
                    for kb in kbs:
                        pe.wait_ge(m_ready, KB + kb + 1)
                        for r in range(2):
                            mm = three(gu[:, r, 0:SEQ], (n + r) % RING, slice(P * kb, P * kb + P),
                                       m_hi[:, kb, :], m_lo[:, kb, :], kb == 0, kb == KB - 1, check=True)
                            if kb == KB - 1:
                                mm.then_inc(unit_done, 1)

                project(0, 0)
                project(0, 1)
                project(1, 0)
                logits(0)
                project(1, 1)
                for cb in range(KB):
                    if cb + 2 < KB:
                        project(cb + 2, 0)
                    if cb == KB - 1:
                        first_outputs([KB - 3])
                    if cb + 1 < KB:
                        logits(cb + 1)
                    arguments(cb)
                    if cb + 2 < KB:
                        project(cb + 2, 1)
                    elif cb + 1 < KB:
                        first_outputs(range(KB - 3))
                    else:
                        first_outputs([KB - 2])
                    outputs(cb)
                first_outputs([KB - 1])
                for cb in range(2, KB):
                    n = b + 3 * KB + cb
                    pe.wait_ge(lo_ready, n + 1)
                    pe.wait_ge(x_ready, 4 * KB + cb - 1)
                    output_unit(gu[:, cb % 2, 0:SEQ], n % RING)

            def last_sum():
                for d in range(KB):
                    pe.wait_ge(sq_ready, 6 * KB + d + 1)
                    mm = pe.matmul(mx[:, 1, 0:SEQ], ones[:, :], squares_out[:, d, :], start=d == 0, stop=d == KB - 1)
                mm.then_inc(sum_ready, 1)

            ffn_first(0, 0)
            ffn_second(0)
            ffn_loop(0, 0, PREP_TURN)
            s5_prepare()
            ffn_loop(0, PREP_TURN, TURNS)
            ffn_tail(0)
            s5_mixer()
            for n in (1, 2, 3):
                ffn_first(n, (2, 3, 5)[n - 1])
                ffn_second(n)
                ffn_loop(n, 0, TURNS)
                ffn_tail(n)
                if n == 2:
                    attention()
            last_sum()

        @block.gpsimd
        def _(pool):
            count = [0]

            def step(ins):
                count[0] += 1
                ins.then_inc(pool_step, 1)
                pool.wait_ge(pool_step, count[0])

            def norm(n):
                for d in range(1, KB):
                    pool.wait_ge(sq_ready, KB * n + d + 1)
                    if d > 1:
                        pool.wait_ge(sq_added, (KB - 1) * n + d - 1)
                    pool.tensor_tensor(ssq[:, :], ssq[:, :], tmp[:, d % 2, 0, :], ALU.add).then_inc(sq_added, 1)
                pool.wait_ge(sq_added, (KB - 1) * (n + 1))
                pool.sem_inc(ssq_ready, 1)

            def halves(fn):
                for g2 in range(2):
                    fn(slice(STATE * g2, STATE * (g2 + 1)), slice(GROUP * g2, GROUP * (g2 + 1)))

            def times(dst_re, dst_im, re, im, l_re, l_im, t, conj):
                tt = pool.tensor_tensor
                step(tt(t[0], re, l_re, ALU.mult))
                step(tt(t[1], im, l_im, ALU.mult))
                step(tt(dst_re, t[0], t[1], ALU.add if conj else ALU.subtract))
                step(tt(t[0], im, l_re, ALU.mult))
                step(tt(t[1], re, l_im, ALU.mult))
                step(tt(dst_im, t[0], t[1], ALU.subtract if conj else ALU.add))

            def s5_parameters():
                pr = lambda k: par[:, k, :]
                tt_ = lambda a, b_, c, op: pool.tensor_tensor(pr(a), pr(b_), pr(c), op)
                tt = lambda *o: step(tt_(*o))
                pool.wait_ge(s5_loaded, 16 * 9)
                tt(18, 0, 0, ALU.mult)
                tt(19, 1, 1, ALU.mult)
                tt_(18, 18, 19, ALU.add).then_inc(par_ready, 1)
                pool.wait_ge(par_act, 1)
                tt(4, 0, 3, ALU.mult)
                tt_(5, 1, 3, ALU.mult).then_inc(par_ready, 1)
                pool.wait_ge(par_ready, 2)
                step(pool.tensor_scalar(par_i[:, :], pr(5), 1 / TWO_PI, None, ALU.mult))
                step(pool.tensor_copy(pr(10), par_i[:, :]))
                for k, c in enumerate((C1, C2, C3)):
                    step(pool.tensor_scalar(pr(7), pr(10), c, None, ALU.mult))
                    tt(5, 5, 7, ALU.subtract)
                pool.tensor_scalar(pr(7), pr(5), 0.5, None, ALU.mult).then_inc(par_ready, 1)
                step(pool.memset(b_pow[:, 0], 0.0))
                pool.wait_ge(par_act, 3)
                pool.tensor_scalar(pr(8), pr(8), -1.0, math.pi / 2, ALU.mult, ALU.add).then_inc(par_ready, 1)
                pool.wait_ge(par_ready, 4)
                step(pool.memset(c_zero, 0.0))
                pool.wait_ge(par_act, 5)
                tt(13, 9, 10, ALU.mult)
                step(pool.tensor_scalar(pr(13), pr(13), 2.0, None, ALU.mult))
                tt(12, 9, 9, ALU.mult)
                step(pool.tensor_scalar(pr(12), pr(12), -2.0, 1.0, ALU.mult, ALU.add))
                tt(14, 6, 12, ALU.mult)
                tt(15, 6, 13, ALU.mult)
                step(pool.tensor_scalar(pr(5), pr(14), -1.0, None, ALU.add))
                t = [pr(7), pr(8)]
                times(pr(16), pr(17), pr(5), pr(15), pr(0), pr(1), t, True)
                pool.wait_ge(par_dve, 1)
                tt(16, 16, 11, ALU.mult)
                tt(17, 17, 11, ALU.mult)
                for w, k, at, first in ((0, 16, STEPS - 1, -1), (1, 14, 0, 1)):
                    for r in range(2):
                        step(pool.tensor_copy(powers[:, w, r, :, at], pr(k + r)))
                    for _ in range(STEPS - 1):
                        src, dst = ([powers[:, w, r, :, j] for r in range(2)] for j in (at, at + first))
                        times(*dst, *src, pr(14), pr(15), t, False)
                        at += first
                tt(18, 6, 6, ALU.mult)
                tt(19, 18, 18, ALU.mult)
                src = (12, 13)
                for dst in [(12, 13)] + ROTATIONS:
                    tt(14, src[0], src[0], ALU.mult)
                    tt(15, src[1], src[1], ALU.mult)
                    tt(16, src[0], src[1], ALU.mult)
                    tt(dst[0], 14, 15, ALU.subtract)
                    step(pool.tensor_scalar(pr(dst[1]), pr(16), 2.0, None, ALU.mult))
                    src = dst

            def s5_matrices():
                tt = pool.tensor_tensor
                each = lambda raw_: raw_.unsqueeze(2).broadcast_to([P, PAIRS, STEPS, GROUP])
                power = lambda w, r: powers[:, w, r].unsqueeze(3).broadcast_to([P, PAIRS, STEPS, GROUP])
                step(pool.tensor_scalar(c_raw[:, 1], c_raw[:, 1], -1.0, None, ALU.mult))
                for r in range(2):
                    halves(lambda rows, cols: step(pool.tensor_copy(c_zero[rows, r, :, cols], c_raw[rows, r])))
                for w, src, dst in ((0, b_raw, b_pow), (1, c_raw, state_out)):
                    dst = dst.rearrange("p r a (j c) -> p r a j c", j=STEPS)
                    for r in range(2):
                        step(tt(prep_tmp[0], each(src[:, r]), power(w, 0), ALU.mult))
                        step(tt(prep_tmp[1], each(src[:, 1 - r]), power(w, 1), ALU.mult))
                        op = (ALU.subtract, ALU.add)[(r + w) % 2]
                        halves(lambda rows, cols: step(tt(dst[rows, r, :, :, cols], prep_tmp[0][rows],
                                                          prep_tmp[1][rows], op)))
                step(pool.tensor_tensor(skip_diag, ident[0:CH, 0:CH].unsqueeze(1).broadcast_to([CH, PAIRS, CH]),
                                        skip_col[0:CH, :].unsqueeze(2).broadcast_to([CH, PAIRS, CH]), ALU.mult))

            def s5_tables():
                pool.wait_ge(prep_dve, 16)
                pool.wait_ge(prep_act, 8)
                wide = lambda k, n: par[:, k, :].unsqueeze(2).broadcast_to([P, PAIRS, n])
                step(pool.memset(rot[:, 0, :, 0:1], 1.0))
                step(pool.memset(rot[:, 1, :, 0:1], 0.0))
                step(pool.tensor_scalar(rho, par[:, 19, :].unsqueeze(2).broadcast_to([P, PAIRS, CHUNKS]), 1.0, None,
                                        ALU.mult))
                step(pool.memset(rho[:, :, 0:1], 0.0))
                for k, step_ in enumerate(ROTATIONS):
                    n = 2 ** k
                    t = [rot_tmp[:, r, :, 0:n] for r in range(2)]
                    times(rot[:, 0, :, n:2 * n], rot[:, 1, :, n:2 * n], rot[:, 0, :, 0:n], rot[:, 1, :, 0:n],
                          wide(step_[0], n), wide(step_[1], n), t, False)

            def s5_imaginary(q):
                pool.wait_ge(v_scanned, q + 1)
                cos, sin = (rot[:, r, QP * q:QP * (q + 1), :] for r in range(2))
                vr, vi = (mod[:, k, :].rearrange("p (a c) -> p a c", a=QP) for k in (1, 3))
                step(pool.tensor_tensor(pool_tmp[:, 0], vr, sin, ALU.mult))
                step(pool.tensor_tensor(pool_tmp[:, 1], vi, cos, ALU.mult))
                pool.sem_inc(scan_read, 1)
                if q >= 2:
                    pool.wait_ge(y_done, q - 1)
                pool.tensor_tensor(state_im[:, q % 2, :, 1:CHUNKS], pool_tmp[:, 0, :, 0:CHUNKS - 1],
                                   pool_tmp[:, 1, :, 0:CHUNKS - 1], ALU.add).then_inc(imag_ready, 1)
                pool.wait_ge(imag_ready, q + 1)

            def attention_masks():
                pool.wait_ge(x_ready, 2 * KB)
                step(pool.memset(nones, -1.0))
                step(pool.memset(keep, 1.0))
                step(pool.memset(big, 0.0))
                step(pool.affine_select(out=ntri, in_=nones, compare_op=ALU.is_ge, fill=0.0, base=0,
                                        pattern=[[-1, P]], channel_multiplier=1))
                step(pool.affine_select(out=keep, in_=keep, compare_op=ALU.is_gt, fill=0.0, base=0,
                                        pattern=[[1, P]], channel_multiplier=-1))
                step(pool.affine_select(out=big, in_=big, compare_op=ALU.is_gt, fill=NEG, base=0,
                                        pattern=[[1, P]], channel_multiplier=-1))
                step(pool.tensor_copy(ident_b, ident[:, :]))
                pool.tensor_copy(big_b, big).then_inc(att_const, 1)

            step(pool.memset(ident[:, :], 0.0))
            step(pool.affine_select(out=ident[:, :], in_=ident[:, :], compare_op=ALU.not_equal, fill=1.0, base=0,
                                    pattern=[[-1, P]], channel_multiplier=1))
            pool.memset(ones[:, :], 1.0).then_inc(const_ready, 1)
            norm(0)
            s5_parameters()
            step(pool.memset(b_pow[:, 1], 0.0))
            step(pool.memset(state_out, 0.0))
            s5_matrices()
            pool.sem_inc(matrices_ready, 1)
            pool.memset(toep, 0.0).then_inc(zeroed, 1)
            s5_tables()
            step(pool.memset(state_im[:, :, :, 0:1], 0.0))
            pool.sem_inc(rot_ready, 1)
            norm(1)
            for q in range(QUARTERS):
                s5_imaginary(q)
            norm(2)
            attention_masks()
            for n in (3, 4, 5):
                norm(n)


PREP_TURN = 4


def lay_out(a):
    import numpy as np

    stream = np.empty((UNITS, P, D), np.float32)
    at = [0]

    def put(block):
        stream[at[0]] = block
        at[0] += 1

    def columns(w, c):
        put(w[:, P * c:P * (c + 1)].reshape(KB, P, P).transpose(1, 0, 2).reshape(P, D))

    def ffn(w_in, w_out):
        for f in range(NF):
            columns(w_in, f)
            columns(w_in, NF + f)
            if f:
                put(w_out[P * (f - 1):P * f])
        put(w_out[P * (NF - 1):])

    ffn(a["ffn1_w_in"][0], a["ffn1_w_out"][0])
    for c in range(KB):
        columns(a["s5_w_in"][0], c)
    for c in range(KB):
        columns(a["s5_w_out"][0], c)
        columns(a["s5_w_out"][0], KB + c)
    ffn(a["ffn2_w_in"][0], a["ffn2_w_out"][0])
    ffn(a["ffn1_w_in"][1], a["ffn1_w_out"][1])
    qkv = a["sb_w_qkv"][0]
    for k in range(KB):
        put(qkv[P * k:P * (k + 1), 2 * D:])
    for c in range(KB):
        columns(qkv, c)
        columns(qkv, KB + c)
    for c in range(KB):
        columns(a["sb_w_out"][0], c)
    ffn(a["ffn2_w_in"][1], a["ffn2_w_out"][1])

    def block_vector(g):
        return g.reshape(KB, P).T

    def states(m):
        m = m.reshape(PAIRS, 2, STATE, *m.shape[2:])
        return m.transpose(1, 2, 0, *range(3, m.ndim)).reshape(P, PAIRS, *m.shape[3:])

    gains = np.stack([block_vector(g) for g in (
        a["ffn1_norm"][0], a["mix_norm"][0], a["ffn2_norm"][0], a["ffn1_norm"][1], a["mix_norm"][1],
        a["ffn2_norm"][1], a["final_norm"])], axis=1)
    return {
        "x_in": a["x"][0].T.reshape(KB, P, SEQ).transpose(1, 0, 2),
        "gains": gains,
        "wstream": stream,
        "lam_re": states(a["s5_lam_re"][0]),
        "lam_im": states(a["s5_lam_im"][0]),
        "log_dt": a["s5_log_dt"][0].reshape(PAIRS, 2).T,
        "b_re": states(a["s5_b_re"][0]),
        "b_im": states(a["s5_b_im"][0]),
        "c_re": states(a["s5_c_re"][0].transpose(0, 2, 1)),
        "c_im": states(a["s5_c_im"][0].transpose(0, 2, 1)),
        "skip": np.concatenate([a["s5_d"][0].reshape(PAIRS, CH).T] * STEPS),
    }


def kernel(**inputs):
    import numpy as np
    import concourse.bacc as bacc
    from concourse.bass_utils import run_bass_kernel_spmd as run

    nc = bacc.Bacc("TRN2", target_bir_lowering=False, num_devices=1)
    arrays, args = {}, []
    for name, a in lay_out({k: np.asarray(v) for k, v in inputs.items()}).items():
        a = np.ascontiguousarray(a)
        arrays[f"{name}_dram"] = a
        args.append(nc.dram_tensor(f"{name}_dram", a.shape, mybir.dt.from_np(a.dtype), kind="ExternalInput").ap())
    out = nc.dram_tensor("out_dram", (P, KB, SEQ), F32, kind="ExternalOutput").ap()
    trunk(nc, *args, out)
    result = run(nc, [arrays], core_ids=[0]).results[0]["out_dram"]
    return result.transpose(1, 0, 2).reshape(1, D, SEQ).transpose(0, 2, 1)
```

```python
import math
from contextlib import ExitStack

import concourse.bass as bass
from concourse import mybir

F32, F32R, BF16, I32 = mybir.dt.float32, mybir.dt.float32r, mybir.dt.bfloat16, mybir.dt.int32
ALU = mybir.AluOpType
ACT = mybir.ActivationFunctionType

P = 128
SEQ = 256
D = 1024
DF = 2816
KB = D // P
NF = DF // P
EPS = 1e-6

RAW = 3
RING = 4
FFN_UNITS = 3 * NF
S5_IN, S5_OUT = KB, 2 * KB
FFN_BASE = [0, FFN_UNITS + S5_IN + S5_OUT]
S5_BASE = FFN_UNITS
FFN_BASE += [FFN_BASE[1] + FFN_UNITS]
ATT_BASE = FFN_BASE[2] + FFN_UNITS
FFN_BASE += [ATT_BASE + 4 * KB]
UNITS = FFN_BASE[3] + FFN_UNITS
BODY = 4
TURNS = (NF - 2) // BODY
assert (NF - 2) % BODY == 0 and (3 * BODY) % RAW == 0 and (3 * BODY) % RING == 0

S5_ARRAYS = 9
GROUP, STATE = 16, 64
PAIRS = 32
CH = 2 * GROUP
STEPS = 4
CHUNKS = SEQ // STEPS
QUARTERS = 4
QP = PAIRS // QUARTERS
ROTATIONS = [(0, 1), (2, 3), (4, 5), (6, 7), (8, 9), (10, 11)]
assert 2 ** len(ROTATIONS) == CHUNKS
HEAD = 64
NEG = -1e30

TWO_PI = 2 * math.pi
C1 = 6.28125
C2 = 2029 / 1048576
C3 = TWO_PI - C1 - C2


def gate_unit(base, f):
    return base + 3 * f - 1


def trunk(nc, x_in, gains, wstream, lam_re, lam_im, log_dt, b_re, b_im, c_re, c_im, skip, out):
    with ExitStack() as ctx:
        def sb(name, shape, dt=F32):
            return ctx.enter_context(nc.sbuf_tensor(name, shape, dt))

        def sem(name):
            return ctx.enter_context(nc.semaphore(name))

        raw = sb("raw", [P, RAW, D])
        w_hi = sb("w_hi", [P, RING, D], F32R)
        w_lo = sb("w_lo", [P, RING, D], F32R)
        x = sb("x", [P, KB, SEQ])
        g_hi = sb("g_hi", [P, KB, SEQ], F32R)
        g_lo = sb("g_lo", [P, KB, SEQ], F32R)
        h_hi = sb("h_hi", [P, 2, SEQ], F32R)
        h_lo = sb("h_lo", [P, 2, SEQ], F32R)
        tmp = sb("tmp", [P, 2, 4, SEQ])
        rstd = sb("rstd", [P, SEQ])
        ssq = sb("ssq", [P, 2 * SEQ])
        gain = sb("gain", [P, 7, KB])
        ones = sb("ones", [P, P])
        eps = sb("eps", [P, 1])
        ident = sb("ident", [P, P])
        par = sb("par", [P, 20, PAIRS])
        par_i = sb("par_i", [P, PAIRS], I32)
        skip_col = sb("skip_col", [P, PAIRS])
        with nc.sbuf_tensor("low_part", [P, 4096], F32) as low:
            pass
        m_hi = sb("m_hi", [P, KB, SEQ], F32R)
        m_lo = sb("m_lo", [P, KB, SEQ], F32R)
        with nc.sbuf_tensor("s5_memory", [P, 26 * 1024], F32) as arena:
            pass
        state_in = [low[:, :].rearrange("p (a s) -> p a s", a=PAIRS),
                    arena[:, 0:4096].rearrange("p (a s) -> p a s", a=PAIRS)]
        toep = arena[:, 4096:8192].rearrange("p (a s) -> p a s", a=PAIRS)
        state_out = arena[:, 8192:16384].rearrange("p (r a s) -> p r a s", r=2, a=PAIRS)
        b_pow = arena[:, 16384:24576].rearrange("p (r a s) -> p r a s", r=2, a=PAIRS)
        c_zero = arena[:, 24576:26624].rearrange("p (r a s) -> p r a s", r=2, a=PAIRS)
        b_raw = arena[:, 0:1024].rearrange("p (r a h) -> p r a h", r=2, a=PAIRS)
        c_raw = arena[:, 1024:2048].rearrange("p (r a h) -> p r a h", r=2, a=PAIRS)
        prep_tmp = [low[:, 2048 * k:2048 * k + 2048].rearrange("p (a j h) -> p a j h", a=PAIRS, j=STEPS)
                    for k in range(2)]
        powers = arena[:, 2048:2560].rearrange("p (w r a k) -> p w r a k", w=2, r=2, a=PAIRS)
        skip_diag = arena[0:CH, 2560:3584].rearrange("p (a c) -> p a c", a=PAIRS)
        rot = arena[:, 16384:20480].rearrange("p (r a c) -> p r a c", r=2, a=PAIRS)
        rho = arena[:, 20480:22528].rearrange("p (a c) -> p a c", a=PAIRS)
        u = arena[:, 22528:24576].rearrange("p (a c) -> p a c", a=PAIRS)
        rot_tmp = arena[:, 24576:26624].rearrange("p (r a c) -> p r a c", r=2, a=PAIRS)
        state_im = arena[:, 24576:25600].rearrange("p (k a c) -> p k a c", k=2, a=QP)
        pool_tmp = arena[:, 25600:26624].rearrange("p (k a c) -> p k a c", k=2, a=QP)
        mod = tmp[:, :, :, :].rearrange("p a b t -> p (a b t)").rearrange("p (k n) -> p k n", k=4)

        v = sb("v", [P, 2, D])
        qk = sb("qk", [P, 2, 2, SEQ])
        az = sb("az", [P, 2, 2, 384])
        ez = sb("ez", [P, 2, 384])
        sp_ = sb("softplus", [P, 2, 384])
        sp_hi = sb("sp_hi", [P, 2, 384], F32R)
        sp_lo = sb("sp_lo", [P, 2, 384], F32R)
        wts = sb("wts", [P, 2, 384])
        neg = sb("neg", [P, 2, P])
        neg_r = sb("neg_r", [P, 2, P], F32R)
        ntri, nones = neg_r[:, 0, :], neg_r[:, 1, :]
        keep = sb("keep", [P, P])
        big = sb("big", [P, P])
        r_col = sb("r_col", [P, 2])
        ident_b = sb("ident_b", [P, P], BF16)
        big_b = sb("big_b", [P, P], BF16)
        squares_out = sb("squares_out", [P, KB, SEQ])
        g_out = sb("g_out", [P, KB, SEQ])

        acc = ctx.enter_context(nc.psum_tensor("acc", [P, 4, 512], F32))
        gu = ctx.enter_context(nc.psum_tensor("gu", [P, 2, 512], F32))
        mx = ctx.enter_context(nc.psum_tensor("mx", [P, 2, 512], F32))

        raw_in = [sem(f"raw_in{s}") for s in range(RAW)]
        hi_ready, lo_ready, unit_done = sem("hi_ready"), sem("lo_ready"), sem("unit_done")
        x_loaded = [sem(f"x_loaded{h}") for h in range(KB // 2)]
        first_half, half_hi, half_lo = sem("first_half"), sem("half_hi"), sem("half_lo")
        gain_loaded, s5_loaded = sem("gain_loaded"), sem("s5_loaded")
        x_ready, ghi_ready, g_ready = sem("x_ready"), sem("ghi_ready"), sem("g_ready")
        sq_ready, sq_added = sem("sq_ready"), sem("sq_added")
        sum_ready, rstd_ready = sem("sum_ready"), sem("rstd_ready")
        root_ready = sem("root_ready")
        acc_ready = sem("acc_ready")
        gu_scaled, silu_ready, h_ready = sem("gu_scaled"), sem("silu_ready"), sem("h_ready")
        hhi_ready, hlo_ready = sem("hhi_ready"), sem("hlo_ready")
        const_ready, eps_ready = sem("const_ready"), sem("eps_ready")
        par_ready, par_act, par_dve = sem("par_ready"), sem("par_act"), sem("par_dve")
        matrices_ready, turned, kernels_done = sem("matrices_ready"), sem("turned"), sem("kernels_done")
        prep_dve, prep_act = sem("prep_dve"), sem("prep_act")
        rot_ready = sem("rot_ready")
        u_scaled, turned_back = sem("u_scaled"), sem("turned_back")
        zeroed, own_done = sem("zeroed"), sem("own_done")
        u_ready, inflow_done, inflow_read = sem("u_ready"), sem("inflow_done"), sem("inflow_read")
        v_scanned, scan_read = sem("v_scanned"), sem("scan_read")
        real_ready, imag_ready = sem("real_ready"), sem("imag_ready")
        y_done, z_ready, z_turned = sem("y_done"), sem("z_ready"), sem("z_turned")
        m_hi_ready, m_ready = sem("m_hi_ready"), sem("m_ready")
        sg_ready, mix_read = sem("sg_ready"), sem("mix_read")
        rcol_done, rcol_ready, v_ready = sem("rcol_done"), sem("rcol_ready"), sem("v_ready")
        att_const, qk_ready, logits_done = sem("att_const"), sem("qk_ready"), sem("logits_done")
        az_ready, ez_ready, ln_ready = sem("az_ready"), sem("ez_ready"), sem("ln_ready")
        sp_ready, arg_done = sem("sp_ready"), sem("arg_done")
        wts_ready, o_done = sem("wts_ready"), sem("o_done")
        dve_step, pool_step = sem("dve_step"), sem("pool_step")
        xg_ready, y_ready, stored = sem("xg_ready"), sem("y_ready"), sem("stored")

        def z_of(q):
            return u[:, QP * q:QP * (q + 1), :].rearrange("p a c -> p (a c)").rearrange(
                "p (j i h) -> p j i h", j=STEPS, i=4)

        def turned_z(q):
            return acc[:, q, :].rearrange("p (j t c) -> p t c j", j=STEPS, t=2)

        def two_squares(p):
            return tmp[:, p % 2, 0:2, :].rearrange("p k t -> p (k t)")

        def diagonal(t):
            return bass.AP(t.tensor, t.offset, [list(t.ap[0]), [384, 2], [256, 2], [1, P]])

        scaled_u = ssq[:, :].rearrange("p (t n) -> p t n", t=2)

        def copy_u(copy, q, js):
            for j in js:
                for i in range(4):
                    src = scaled_u[CH * i:CH * (i + 1)].rearrange("p t (c j) -> p t c j", j=STEPS)[:, :, :, j]
                    last = copy(u[CH * j:CH * (j + 1), QP * q:QP * (q + 1), :].rearrange(
                        "p (t i) c -> p t i c", t=2)[:, :, i, :], src)
            return last

        def out_bank(cb):
            return (gu, mx)[cb // 2 % 2][:, cb % 2, 0:SEQ]

        def z_banks(cb):
            return acc[:, 2:4, 0:384] if cb % 2 else mx[:, :, 0:384]

        block = ctx.enter_context(nc.Block())

        def slot(ring, unit):
            return unit % ring

        @block.sync
        def _(sp):
            def load(unit, s, turn):
                if turn is not None:
                    sp.wait_ge(lo_ready, turn)
                sp.dma_start(raw[:, s, :], wstream[unit] if isinstance(unit, int)
                             else wstream[bass.ds(unit, 1)].rearrange("a p n -> (a p) n")).then_inc(raw_in[s], 16)

            def load_x(h):
                sp.dma_start(x[:, 2 * h:2 * h + 2, :], x_in[:, 2 * h:2 * h + 2, :]).then_inc(x_loaded[h], 16)

            sp.dma_start(raw[:, 0, 0:D // 2], wstream[0][:, 0:D // 2]).then_inc(first_half, 16)
            load_x(0)
            sp.dma_start(raw[:, 0, D // 2:D], wstream[0][:, D // 2:D]).then_inc(raw_in[0], 16)
            for h in range(1, KB // 2):
                load_x(h)
            load(1, 1, None)
            load(2, 2, None)
            for unit in range(RAW, 2 * RAW):
                load(unit, unit - RAW, unit - RAW + 1)
            for dst, src in ((par[:, 0, :], lam_re), (par[:, 1, :], lam_im),
                             (par[0:STATE, 2, :], log_dt[0:1, :].broadcast_to([STATE, PAIRS])),
                             (par[STATE:P, 2, :], log_dt[1:2, :].broadcast_to([STATE, PAIRS])),
                             (b_raw[:, 0], b_re), (b_raw[:, 1], b_im), (c_raw[:, 0], c_re), (c_raw[:, 1], c_im),
                             (skip_col[:, :], skip)):
                sp.dma_start(dst, src).then_inc(s5_loaded, 16)
            turns = UNITS // RAW
            with sp.Fori(2, turns) as i:
                for s in range(RAW):
                    load(RAW * i + s, s, RAW * i + (s - RAW + 1))
            for unit in range(RAW * turns, UNITS):
                load(unit, slot(RAW, unit), unit - RAW + 1)
            for h in range(KB // 2):
                sp.wait_ge(y_ready, h + 1)
                sp.dma_start(out[:, 2 * h:2 * h + 2, :], g_out[:, 2 * h:2 * h + 2, :]).then_inc(stored, 16)
            sp.wait_ge(stored, 16 * (KB // 2))

        @block.scalar
        def _(act):
            def split_hi(unit, s_raw, s_ring, known=None):
                act.wait_ge(raw_in[s_raw], 16 * (known if known is not None else unit // RAW + 1))
                if not isinstance(unit, int) or unit >= RING:
                    act.wait_ge(unit_done, unit - RING + 1)
                act.activation(w_hi[:, s_ring, :], raw[:, s_raw, :], ACT.Copy).then_inc(hi_ready, 1)

            def split_after(done):
                if done + RING < UNITS:
                    n = done + RING
                    split_hi(n, n % RAW, n % RING)

            def silu(n, f):
                act.wait_ge(gu_scaled, NF * n + f + 1)
                act.activation(tmp[:, f % 2, 2, :], tmp[:, f % 2, 0, :], ACT.Silu).then_inc(silu_ready, 1)

            def round_h(n, f):
                act.wait_ge(h_ready, NF * n + f + 1)
                act.activation(h_hi[:, f % 2, :], tmp[:, f % 2, 3, :], ACT.Copy).then_inc(hhi_ready, 1)

            def root(n):
                act.wait_ge(sum_ready, n + 1)
                if n == 0:
                    act.wait_ge(eps_ready, 1)
                else:
                    act.wait_ge(rstd_ready, n)
                act.activation(rstd[:, :], mx[:, 1, 0:SEQ], ACT.Sqrt, scale=1.0 / D,
                               bias=eps[:, :]).then_inc(root_ready, 1)

            def ffn_first(n, norm_index):
                root(norm_index)
                split_after(FFN_BASE[n])
                silu(n, 0)
                round_h(n, 0)
                split_after(FFN_BASE[n] + 1)

            def ffn_second(n):
                g = gate_unit(FFN_BASE[n], 1)
                split_after(g)
                silu(n, 1)
                round_h(n, 1)
                split_after(g + 1)
                split_after(g + 2)

            def ffn_turn(n, i):
                base = FFN_BASE[n]
                for m in range(BODY):
                    g0 = gate_unit(base, 2 + m)
                    f0 = NF * n + 2 + m
                    for k in range(3):
                        if k == 1:
                            act.wait_ge(gu_scaled, BODY * i + (f0 + 1))
                            act.activation(tmp[:, m % 2, 2, :], tmp[:, m % 2, 0, :],
                                           ACT.Silu).then_inc(silu_ready, 1)
                            act.wait_ge(h_ready, BODY * i + (f0 + 1))
                            act.activation(h_hi[:, m % 2, :], tmp[:, m % 2, 3, :],
                                           ACT.Copy).then_inc(hhi_ready, 1)
                        n0 = g0 + k + RING
                        if isinstance(i, int) and n0 + 3 * BODY * i >= UNITS:
                            continue
                        act.wait_ge(raw_in[n0 % RAW], (16 * 3 * BODY // RAW) * i + 16 * (n0 // RAW + 1))
                        act.wait_ge(unit_done, 3 * BODY * i + (g0 + k + 1))
                        act.activation(w_hi[:, n0 % RING, :], raw[:, n0 % RAW, :],
                                       ACT.Copy).then_inc(hi_ready, 1)

            def ffn_loop(n, first, last):
                with act.Fori(first, last) as i:
                    ffn_turn(n, i)

            def scaled_block(n, d):
                if n == 0:
                    act.wait_ge(x_loaded[d // 2], 16)
                    act.wait_ge(gain_loaded, 16)
                else:
                    act.wait_ge(x_ready, KB * (n - 1) + d + 1)
                act.activation(g_hi[:, d, :], x[:, d, :], ACT.Copy,
                               scale=gain[:, n, d:d + 1]).then_inc(ghi_ready, 1)

            def squared_pair(n, p):
                two = x[:, 2 * p:2 * p + 2, :].rearrange("p k t -> p (k t)")
                if p == 0:
                    if n:
                        act.wait_ge(sum_ready, n)
                    dst = ssq[:, :]
                else:
                    if p == 3:
                        act.wait_ge(sq_added, 3 * n + 1)
                    dst = two_squares(p)
                act.activation(dst, two, ACT.Square).then_inc(sq_ready, 1)

            def norm_block(n, d):
                scaled_block(n, d)
                if d % 2:
                    squared_pair(n, d // 2)

            def norm(n):
                for d in range(KB):
                    norm_block(n, d)

            def s5_time_steps():
                pr = lambda k: par[:, k, :]
                act.wait_ge(s5_loaded, 16 * S5_ARRAYS)
                act.activation(pr(3), pr(2), ACT.Exp).then_inc(par_act, 1)

            def s5_exponentials():
                pr = lambda k: par[:, k, :]
                act.wait_ge(par_ready, 2)
                act.activation(pr(6), pr(4), ACT.Exp).then_inc(par_act, 1)
                act.wait_ge(par_ready, 3)
                act.activation(pr(9), pr(7), ACT.Sin).then_inc(par_act, 1)
                act.activation(pr(10), pr(8), ACT.Sin).then_inc(par_act, 1)

            def s5_prepare():
                for k in range(1, 16, 2):
                    act.wait_ge(turned, k + 1)
                    act.activation(state_in[k // 8][:, 4 * (k % 8):4 * (k % 8) + 4, :],
                                   mx[:, 1, :].rearrange("p (a s) -> p a s", a=4), ACT.Copy).then_inc(prep_act, 1)

            def s5_mixer():
                b = S5_BASE
                def inputs(q):
                    act.wait_ge(u_scaled, q + 1)
                    copy = lambda dst, src: act.activation(dst, src, ACT.Copy)
                    if q:
                        copy_u(copy, q, (0, 1)).then_inc(u_ready, 1)
                    copy_u(copy, q, (2, 3)).then_inc(u_ready, 1)

                split_after(b)
                split_after(b + 1)
                root(1)
                split_after(b + 2)
                inputs(0)
                split_after(b + 3)
                split_after(b + 4)
                split_after(b + 5)
                inputs(1)
                inputs(2)
                split_after(b + 6)
                inputs(3)
                split_after(b + 7)

                def gelu(q):
                    act.wait_ge(y_done, q + 1)
                    act.activation(z_of(q), acc[:, q, :].rearrange("p (i j h) -> p j i h", i=4, j=STEPS),
                                   ACT.Gelu_apprx_tanh).then_inc(z_ready, 1)

                def round_z(q):
                    act.wait_ge(z_turned, q + 1)
                    act.activation(m_hi[:, 2 * q:2 * q + 2, :].rearrange("p t (c j) -> p t c j", j=STEPS),
                                   turned_z(q), ACT.Copy).then_inc(m_hi_ready, 2)

                gelu(0)
                gelu(1)
                round_z(0)
                round_z(1)
                gelu(2)
                gelu(3)
                round_z(2)
                round_z(3)
                for cb in range(KB):
                    if cb:
                        norm_block(2, cb - 1)
                    split_after(b + KB + 2 * cb)
                    act.wait_ge(unit_done, b + KB + 2 * cb + 2)
                    act.activation(tmp[:, cb % 2, 2, :], gu[:, cb % 2, SEQ:2 * SEQ],
                                   ACT.Sigmoid).then_inc(sg_ready, 1)
                    split_after(b + KB + 2 * cb + 1)
                norm_block(2, KB - 1)

            def attention():
                b = ATT_BASE
                for k in range(3):
                    split_after(b + k)
                root(4)
                for k in range(3, KB):
                    split_after(b + k)
                q_ = b + KB

                def values(t, half):
                    act.activation(v[:, t, 512 * half:512 * half + 512], acc[:, 2 * t + half, :], ACT.Copy,
                                   scale=r_col[:, t:t + 1]).then_inc(v_ready, 1)

                def exponential(cb):
                    act.wait_ge(logits_done, cb + 1)
                    if cb >= 2:
                        act.wait_ge(sp_ready, cb - 1)
                    act.activation(az[:, cb % 2], z_banks(cb), ACT.Abs).then_inc(az_ready, 1)
                    act.wait_ge(az_ready, cb + 1)
                    act.activation(ez[:, :, :], az[:, cb % 2], ACT.Exp, scale=-1.0).then_inc(ez_ready, 1)

                def logarithm(cb):
                    act.wait_ge(ez_ready, cb + 1)
                    act.activation(az[:, cb % 2], ez[:, :, :], ACT.Ln, bias=1.0).then_inc(ln_ready, 1)

                def weights(cb):
                    act.wait_ge(arg_done, cb + 1)
                    if cb:
                        act.wait_ge(o_done, cb)
                    act.activation(wts[:, :, :], z_banks(cb), ACT.Exp).then_inc(wts_ready, 1)

                act.wait_ge(rcol_ready, 1)
                values(0, 0)
                values(0, 1)
                split_after(q_)
                values(1, 0)
                values(1, 1)
                split_after(q_ + 1)
                split_after(q_ + 2)
                exponential(0)
                logarithm(0)
                split_after(q_ + 3)
                split_after(q_ + 4)
                for cb in range(KB):
                    if cb + 1 < KB:
                        exponential(cb + 1)
                    if cb + 2 < KB:
                        split_after(q_ + 2 * cb + 5)
                    weights(cb)
                    if cb + 1 < KB:
                        logarithm(cb + 1)
                    if cb + 3 < KB:
                        split_after(q_ + 2 * cb + 6)
                    act.wait_ge(o_done, cb + 1)
                    act.activation(m_hi[:, cb, :], acc[:, cb % 2, 0:SEQ], ACT.Copy).then_inc(m_hi_ready, 1)
                for cb in range(KB):
                    if cb:
                        norm_block(5, cb - 1)
                    split_after(b + 3 * KB + cb)
                norm_block(5, KB - 1)

            def last_squares():
                for d in range(KB):
                    act.wait_ge(x_ready, 5 * KB + d + 1)
                    act.activation(squares_out[:, d, :], x[:, d, :], ACT.Square).then_inc(sq_ready, 1)

            act.dma_start(gain[:, :, :], gains).then_inc(gain_loaded, 16)
            half = slice(0, D // 2)
            act.wait_ge(first_half, 16)
            act.activation(w_hi[:, 0, half], raw[:, 0, half], ACT.Copy).then_inc(half_hi, 1)
            scaled_block(0, 0)
            scaled_block(0, 1)
            half = slice(D // 2, D)
            act.wait_ge(raw_in[0], 16)
            act.activation(w_hi[:, 0, half], raw[:, 0, half], ACT.Copy).then_inc(hi_ready, 1)
            for d in range(2, KB):
                scaled_block(0, d)
                if d % 2:
                    squared_pair(0, d // 2 - 1)
            split_hi(1, 1, 1)
            squared_pair(0, 3)
            for unit in (2, 3):
                split_hi(unit, unit % RAW, unit % RING)
            ffn_first(0, 0)
            s5_time_steps()
            ffn_second(0)
            s5_exponentials()
            ffn_loop(0, 0, PREP_TURN)
            s5_prepare()
            ffn_loop(0, PREP_TURN, TURNS)
            for d in range(KB):
                scaled_block(1, d)
            for d in range(KB):
                if d % 2:
                    squared_pair(1, d // 2)
            split_after(FFN_BASE[0] + FFN_UNITS - 1)
            s5_mixer()
            for n in (1, 2, 3):
                ffn_first(n, (2, 3, 5)[n - 1])
                ffn_second(n)
                ffn_loop(n, 0, TURNS - (n == 3))
                if n == 3:
                    ffn_turn(n, TURNS - 1)
                else:
                    norm(n + 2)
                split_after(FFN_BASE[n] + FFN_UNITS - 1)
                if n == 2:
                    attention()
            last_squares()
            root(6)

        @block.vector
        def _(dve):
            count = [0]

            def step(ins):
                count[0] += 1
                ins.then_inc(dve_step, 1)
                dve.wait_ge(dve_step, count[0])

            def split_lo(n):
                dve.wait_ge(hi_ready, n + 1)
                dve.tensor_tensor(w_lo[:, n % RING, :], raw[:, n % RAW, :], w_hi[:, n % RING, :].bitcast(F32),
                                  ALU.subtract).then_inc(lo_ready, 1)

            def split_after(done):
                if done + RING < UNITS:
                    split_lo(done + RING)

            def scale_gu(m, wait_units):
                dve.wait_ge(unit_done, wait_units)
                dve.tensor_tensor(tmp[:, m, 0:2, :], gu[:, m, :].rearrange("p (r t) -> p r t", r=2),
                                  rstd[:, :].unsqueeze(1).broadcast_to([P, 2, SEQ]), ALU.mult).then_inc(gu_scaled, 1)

            def hidden(m, n_f):
                dve.wait_ge(gu_scaled, n_f)
                dve.wait_ge(silu_ready, n_f)
                dve.tensor_tensor(tmp[:, m, 3, :], tmp[:, m, 2, :], tmp[:, m, 1, :], ALU.mult).then_inc(h_ready, 1)
                dve.wait_ge(h_ready, n_f)
                dve.wait_ge(hhi_ready, n_f)
                dve.tensor_tensor(h_lo[:, m, :], tmp[:, m, 3, :], h_hi[:, m, :].bitcast(F32),
                                  ALU.subtract).then_inc(hlo_ready, 1)

            def ffn_first(n, norm_index):
                root(norm_index)
                scale_gu(0, FFN_BASE[n] + 2)
                split_after(FFN_BASE[n])
                hidden(0, NF * n + 1)
                split_after(FFN_BASE[n] + 1)

            def ffn_second(n):
                g = gate_unit(FFN_BASE[n], 1)
                split_after(g)
                scale_gu(1, g + 2)
                hidden(1, NF * n + 2)
                split_after(g + 1)

            def ffn_turn(n, i):
                base = FFN_BASE[n]
                for m in range(BODY):
                    g0 = gate_unit(base, 2 + m)
                    f1 = BODY * i + (NF * n + 2 + m + 1)
                    for k in (-1, 0, 1):
                        if k == 1:
                            scale_gu(m % 2, 3 * BODY * i + (g0 + 2))
                            hidden(m % 2, f1)
                        n0 = g0 + k + RING
                        if isinstance(i, int) and n0 + 3 * BODY * i >= UNITS:
                            continue
                        dve.wait_ge(hi_ready, 3 * BODY * i + (n0 + 1))
                        dve.tensor_tensor(w_lo[:, n0 % RING, :], raw[:, n0 % RAW, :],
                                          w_hi[:, n0 % RING, :].bitcast(F32),
                                          ALU.subtract).then_inc(lo_ready, 1)

            def ffn_loop(n, first, last):
                with dve.Fori(first, last) as i:
                    ffn_turn(n, i)

            def root(n):
                dve.wait_ge(root_ready, n + 1)
                dve.reciprocal(rstd[:, :], rstd[:, :]).then_inc(rstd_ready, 1)
                dve.wait_ge(rstd_ready, n + 1)

            def low_part(n, d):
                dve.wait_ge(ghi_ready, KB * n + d + 1)
                dve.scalar_tensor_tensor(g_lo[:, d, :], x[:, d, :], gain[:, n, d:d + 1], g_hi[:, d, :].bitcast(F32),
                                         ALU.mult, ALU.subtract).then_inc(g_ready, 1)

            def ffn_update(n, bank):
                if bank < 3:
                    dve.wait_ge(acc_ready, 3 * n + bank + 1)
                else:
                    dve.wait_ge(unit_done, FFN_BASE[n] + FFN_UNITS)
                two = x[:, 2 * bank:2 * bank + 2, :].rearrange("p k t -> p (k t)")
                dve.scalar_tensor_tensor(two, acc[:, bank, :], 0.5, two, ALU.mult, ALU.add).then_inc(x_ready, 2)

            def norm(n, layer):
                for bank in range(5):
                    if bank < 4:
                        ffn_update(layer, bank)
                    if bank:
                        dve.wait_ge(x_ready, KB * (n - 1) + 2 * bank)
                        low_part(n, 2 * bank - 2)
                        low_part(n, 2 * bank - 1)

            def s5_prepare():
                def copy_turned(k):
                    dve.wait_ge(turned, k + 1)
                    dve.tensor_copy(state_in[k // 8][:, 4 * (k % 8):4 * (k % 8) + 4, :],
                                    mx[:, 0, :].rearrange("p (a s) -> p a s", a=4)).then_inc(prep_dve, 1)

                for k in range(0, 8, 2):
                    copy_turned(k)
                dve.wait_ge(zeroed, 1)
                for k in range(8):
                    dve.wait_ge(kernels_done, k + 1)
                    src = mx[0:CH, k % 2, :].rearrange("p (a s) -> p a s", a=4)
                    for j in range(STEPS):
                        last = dve.tensor_copy(toep[CH * j:CH * (j + 1), 4 * k:4 * k + 4, CH * j:P],
                                               src[:, :, 0:P - CH * j])
                    last.then_inc(prep_dve, 1)
                for k in range(8, 16, 2):
                    copy_turned(k)

            def s5_scale_u(q):
                dve.wait_ge(unit_done, S5_BASE + 2 * q + 2)
                if q:
                    dve.wait_ge(u_ready, 2 * q)
                else:
                    dve.wait_ge(rot_ready, 1)
                dve.tensor_tensor(scaled_u, acc[:, q, :].rearrange("p (t n) -> p t n", t=2),
                                  rstd[:, :].unsqueeze(1).broadcast_to([P, 2, SEQ]), ALU.mult).then_inc(u_scaled, 1)
                if q == 0:
                    dve.wait_ge(u_scaled, 1)
                    copy_u(dve.tensor_copy, 0, (0, 1)).then_inc(u_ready, 1)

            def s5_scan(q):
                dve.wait_ge(inflow_done, q + 1)
                if q:
                    dve.wait_ge(scan_read, q)
                    dve.wait_ge(real_ready, q)
                else:
                    dve.wait_ge(hlo_ready, NF)
                re, im = ((gu, mx)[q % 2][:, r, :] for r in range(2))
                cos, sin = (rot[:, r, QP * q:QP * (q + 1), :].rearrange("p a c -> p (a c)") for r in range(2))
                decay = rho[:, QP * q:QP * (q + 1), :].rearrange("p a c -> p (a c)")
                dve.tensor_tensor(mod[:, 0, :], re, cos, ALU.mult)
                step(dve.tensor_tensor(mod[:, 1, :], im, sin, ALU.mult))
                dve.tensor_tensor(mod[:, 0, :], mod[:, 0, :], mod[:, 1, :], ALU.add).then_inc(turned_back, 1)
                dve.tensor_tensor(mod[:, 2, :], im, cos, ALU.mult)
                dve.wait_ge(turned_back, 2 * q + 1)
                dve.tensor_tensor_scan(mod[:, 1, :], decay, mod[:, 0, :], 0.0, ALU.mult, ALU.add).then_inc(v_scanned, 1)
                step(dve.tensor_tensor(mod[:, 3, :], re, sin, ALU.mult))
                dve.sem_inc(inflow_read, 1)
                dve.tensor_tensor(mod[:, 2, :], mod[:, 2, :], mod[:, 3, :], ALU.subtract).then_inc(turned_back, 1)
                dve.wait_ge(turned_back, 2 * q + 2)
                dve.tensor_tensor_scan(mod[:, 3, :], decay, mod[:, 2, :], 0.0, ALU.mult, ALU.add).then_inc(v_scanned, 1)

            def s5_real(q):
                dve.wait_ge(v_scanned, 2 * q + 2)
                real = u[:, QP * q:QP * (q + 1), :]
                dve.wait_ge(own_done, q + 1)
                dve.memset(real[:, :, 0:1], 0.0)
                cos, sin = (rot[:, r, QP * q:QP * (q + 1), :].rearrange("p a c -> p (a c)") for r in range(2))
                dve.tensor_tensor(mod[:, 0, :], mod[:, 1, :], cos, ALU.mult)
                step(dve.tensor_tensor(mod[:, 2, :], mod[:, 3, :], sin, ALU.mult))
                a_, b_ = (mod[:, k, :].rearrange("p (a c) -> p a c", a=QP)[:, :, 0:CHUNKS - 1] for k in (0, 2))
                dve.tensor_tensor(real[:, :, 1:CHUNKS], a_, b_, ALU.subtract).then_inc(real_ready, 1)

            def s5_low(q):
                dve.wait_ge(m_hi_ready, 2 * q + 2)
                m = (t[:, 2 * q:2 * q + 2, :].rearrange("p t (c j) -> p t c j", j=STEPS) for t in (m_lo, m_hi))
                lo, hi = m
                for t in range(2):
                    last = dve.tensor_tensor(lo[:, t], turned_z(q)[:, t], hi[:, t].bitcast(F32), ALU.subtract)
                last.then_inc(m_ready, 2)

            def s5_mixer():
                b = S5_BASE
                split_after(b)
                split_after(b + 1)
                root(1)
                split_after(b + 2)
                s5_scale_u(0)
                split_after(b + 3)
                s5_scale_u(1)
                split_after(b + 4)
                split_after(b + 5)
                s5_scale_u(2)
                s5_scan(0)
                s5_real(0)
                s5_scan(1)
                s5_scale_u(3)
                s5_real(1)
                s5_scan(2)
                s5_real(2)
                s5_scan(3)
                s5_low(0)
                s5_low(1)
                s5_real(3)
                split_after(b + 6)
                split_after(b + 7)
                s5_low(2)
                s5_low(3)
                for cb in range(KB):
                    split_after(b + KB + 2 * cb)
                    dve.wait_ge(sg_ready, cb + 1)
                    if cb >= 2:
                        dve.wait_ge(x_ready, KB + cb - 1)
                    dve.tensor_tensor(tmp[:, cb % 2, 3, :], gu[:, cb % 2, 0:SEQ], tmp[:, cb % 2, 2, :],
                                      ALU.mult).then_inc(mix_read, 1)
                    dve.wait_ge(mix_read, cb + 1)
                    dve.tensor_tensor(x[:, cb, :], x[:, cb, :], tmp[:, cb % 2, 3, :], ALU.add).then_inc(x_ready, 1)
                    split_after(b + KB + 2 * cb + 1)
                    if cb:
                        low_part(2, cb - 1)
                low_part(2, KB - 1)

            def attention():
                b = ATT_BASE
                for k in range(3):
                    split_after(b + k)
                root(4)
                for k in range(3, KB):
                    split_after(b + k)
                dve.wait_ge(rcol_done, 1)
                dve.tensor_copy(r_col[:, :], mx[:, 0, 0:2]).then_inc(rcol_ready, 1)

                def scale_qk(cb):
                    dve.wait_ge(unit_done, b + KB + 2 * cb + 2)
                    dve.scalar_tensor_tensor(qk[:, cb % 2, 0, :], gu[:, cb % 2, 0:SEQ], HEAD ** -0.5, rstd[:, :],
                                             ALU.mult, ALU.mult)
                    dve.tensor_tensor(qk[:, cb % 2, 1, :], gu[:, cb % 2, SEQ:2 * SEQ], rstd[:, :],
                                      ALU.mult).then_inc(qk_ready, 1)

                def softplus(cb):
                    dve.wait_ge(ln_ready, cb + 1)
                    step(dve.scalar_tensor_tensor(sp_[:, :, :], z_banks(cb), 0.0, az[:, cb % 2], ALU.max, ALU.add))
                    diag = diagonal(sp_[:, :, :])
                    step(dve.tensor_tensor(diag, diag, keep[:, :].unsqueeze(1).unsqueeze(1).broadcast_to([P, 2, 2, P]),
                                           ALU.mult))
                    if cb:
                        dve.wait_ge(arg_done, cb)
                    step(dve.tensor_copy(sp_hi[:, :, :], sp_[:, :, :]))
                    dve.tensor_tensor(sp_lo[:, :, :], sp_[:, :, :], sp_hi[:, :, :].bitcast(F32),
                                      ALU.subtract).then_inc(sp_ready, 1)

                def low_o(cb):
                    dve.wait_ge(m_hi_ready, KB + cb + 1)
                    dve.tensor_tensor(m_lo[:, cb, :], acc[:, cb % 2, 0:SEQ], m_hi[:, cb, :].bitcast(F32),
                                      ALU.subtract).then_inc(m_ready, 1)

                q_ = b + KB
                split_after(q_)
                scale_qk(0)
                split_after(q_ + 1)
                split_after(q_ + 2)
                scale_qk(1)
                dve.wait_ge(att_const, 1)
                softplus(0)
                split_after(q_ + 3)
                split_after(q_ + 4)
                for cb in range(KB):
                    if cb + 2 < KB:
                        scale_qk(cb + 2)
                        split_after(q_ + 2 * cb + 5)
                    if cb + 1 < KB:
                        softplus(cb + 1)
                    if cb + 3 < KB:
                        split_after(q_ + 2 * cb + 6)
                    low_o(cb)
                for cb in range(KB):
                    dve.wait_ge(unit_done, b + 3 * KB + cb + 1)
                    dve.tensor_tensor(x[:, cb, :], x[:, cb, :], out_bank(cb), ALU.add).then_inc(x_ready, 1)
                    if cb:
                        low_part(5, cb - 1)
                    split_after(b + 3 * KB + cb)
                low_part(5, KB - 1)

            dve.memset(eps[:, :], EPS).then_inc(eps_ready, 1)
            for h, ready, done in ((0, half_hi, half_lo), (1, hi_ready, lo_ready)):
                half = slice(D // 2 * h, D // 2 * (h + 1))
                dve.wait_ge(ready, 1)
                dve.tensor_tensor(w_lo[:, 0, half], raw[:, 0, half], w_hi[:, 0, half].bitcast(F32),
                                  ALU.subtract).then_inc(done, 1)
                low_part(0, 2 * h)
                low_part(0, 2 * h + 1)
            for d in range(4, KB):
                low_part(0, d)
            split_lo(1)
            split_lo(2)
            split_lo(3)
            ffn_first(0, 0)
            dve.wait_ge(par_ready, 1)
            dve.reciprocal(par[:, 11, :], par[:, 18, :]).then_inc(par_dve, 1)
            ffn_second(0)
            ffn_loop(0, 0, PREP_TURN)
            s5_prepare()
            ffn_loop(0, PREP_TURN, TURNS)
            norm(1, 0)
            split_after(FFN_BASE[0] + FFN_UNITS - 2)
            split_after(FFN_BASE[0] + FFN_UNITS - 1)
            s5_mixer()
            for n in (1, 2, 3):
                ffn_first(n, (2, 3, 5)[n - 1])
                ffn_second(n)
                ffn_loop(n, 0, TURNS - (n == 3))
                if n == 3:
                    ffn_turn(n, TURNS - 1)
                else:
                    norm(n + 2, n)
                split_after(FFN_BASE[n] + FFN_UNITS - 2)
                split_after(FFN_BASE[n] + FFN_UNITS - 1)
                if n == 2:
                    attention()
            for bank in range(4):
                ffn_update(3, bank)
            for d in range(KB):
                dve.wait_ge(x_ready, 5 * KB + d + 1)
                dve.tensor_scalar(g_out[:, d, :], x[:, d, :], gain[:, 6, d:d + 1], None, ALU.mult).then_inc(xg_ready, 1)
            root(6)
            dve.wait_ge(xg_ready, KB)
            for d in range(0, KB, 2):
                two = g_out[:, d:d + 2, :]
                dve.tensor_tensor(two, two, rstd[:, :].unsqueeze(1).broadcast_to([P, 2, SEQ]),
                                  ALU.mult).then_inc(y_ready, 1)

        @block.tensor
        def _(pe):
            def three(dst, unit_slot, cols, hi, lo, start, stop, check=False):
                a, b_ = w_hi[:, unit_slot, cols], w_lo[:, unit_slot, cols]
                pe.matmul(dst, a, hi, start=start, stop=False, skip_group_check=check)
                pe.matmul(dst, a, lo, start=False, stop=False, skip_group_check=check)
                return pe.matmul(dst, b_, hi, start=False, stop=stop, skip_group_check=check)

            def column_unit(dst, s):
                for kb in range(KB):
                    last = three(dst, s, slice(P * kb, P * kb + P), g_hi[:, kb, :], g_lo[:, kb, :],
                                 kb == 0, kb == KB - 1)
                last.then_inc(unit_done, 1)

            def two_units(bank, n, ready, first, hi, lo, kbs=range(KB)):
                for kb in kbs:
                    if kb == 0:
                        pe.wait_ge(lo_ready, n + 2)
                    pe.wait_ge(ready, first + kb + 1)
                    for r in range(2):
                        mm = three(bank[:, SEQ * r:SEQ * (r + 1)], (n + r) % RING, slice(P * kb, P * kb + P),
                                   hi[:, kb, :], lo[:, kb, :], kb == 0 and r == 0, kb == KB - 1, check=True)
                        if kb == KB - 1:
                            mm.then_inc(unit_done, 1)

            def down_unit(s, m, first=False, last_block=False):
                for d in range(KB):
                    mm = three(acc[:, d // 2, SEQ * (d % 2):SEQ * (d % 2 + 1)], s, slice(P * d, P * d + P),
                               h_hi[:, m, :], h_lo[:, m, :], first and d % 2 == 0, last_block, check=True)
                    if last_block and d % 2 and d < KB - 1:
                        mm.then_inc(acc_ready, 1)
                mm.then_inc(unit_done, 1)

            def squares(n):
                pe.wait_ge(sq_added, 3 * (n + 1))
                if n == 0:
                    pe.wait_ge(const_ready, 1)
                pe.matmul(mx[:, 1, 0:SEQ], ones[:, :], ssq[:, 0:SEQ], start=True, stop=False)
                mm = pe.matmul(mx[:, 1, 0:SEQ], ones[:, :], ssq[:, SEQ:2 * SEQ], start=False, stop=True)
                mm.then_inc(sum_ready, 1)

            def ffn_first(n, norm_index):
                if n:
                    pe.wait_ge(gu_scaled, NF * n - 1)
                if n == 1:
                    pe.wait_ge(mix_read, KB - 1)
                if n == 3:
                    pe.wait_ge(x_ready, 5 * KB - 1)
                if n:
                    two_units(gu[:, 0, :], FFN_BASE[n], g_ready, KB * norm_index, g_hi, g_lo)
                    squares(norm_index)
                else:
                    pe.wait_ge(half_lo, 1)
                    for kb in range(KB):
                        if kb == KB // 2:
                            pe.wait_ge(lo_ready, 1)
                        pe.wait_ge(g_ready, kb + 1)
                        mm = three(gu[:, 0, 0:SEQ], 0, slice(P * kb, P * kb + P), g_hi[:, kb, :], g_lo[:, kb, :],
                                   kb == 0, kb == KB - 1)
                    mm.then_inc(unit_done, 1)
                    pe.wait_ge(lo_ready, 2)
                    for kb in range(KB):
                        mm = three(gu[:, 0, SEQ:2 * SEQ], 1, slice(P * kb, P * kb + P), g_hi[:, kb, :], g_lo[:, kb, :],
                                   kb == 0, kb == KB - 1)
                        if kb == 3:
                            squares(0)
                    mm.then_inc(unit_done, 1)

            def ffn_second(n):
                g = gate_unit(FFN_BASE[n], 1)
                if n:
                    pe.wait_ge(gu_scaled, NF * n)
                if n == 1:
                    pe.wait_ge(mix_read, KB)
                if n == 3:
                    pe.wait_ge(x_ready, 5 * KB)
                pe.wait_ge(lo_ready, g + 1)
                column_unit(gu[:, 1, 0:SEQ], g % RING)
                pe.wait_ge(lo_ready, g + 2)
                column_unit(gu[:, 1, SEQ:2 * SEQ], (g + 1) % RING)
                pe.wait_ge(lo_ready, g + 3)
                pe.wait_ge(hlo_ready, NF * n + 1)
                down_unit((g + 2) % RING, 0, first=True)

            def ffn_loop(n, first, last):
                base = FFN_BASE[n]
                with pe.Fori(first, last) as i:
                    for m in range(BODY):
                        g0 = gate_unit(base, 2 + m)
                        f0 = NF * n + 2 + m
                        pe.wait_ge(gu_scaled, BODY * i + (f0 - 1))
                        pe.wait_ge(lo_ready, 3 * BODY * i + (g0 + 1))
                        column_unit(gu[:, m % 2, 0:SEQ], g0 % RING)
                        pe.wait_ge(lo_ready, 3 * BODY * i + (g0 + 2))
                        column_unit(gu[:, m % 2, SEQ:2 * SEQ], (g0 + 1) % RING)
                        pe.wait_ge(lo_ready, 3 * BODY * i + (g0 + 3))
                        pe.wait_ge(hlo_ready, BODY * i + f0)
                        down_unit((g0 + 2) % RING, (m + 1) % 2)

            def ffn_tail(n):
                g = gate_unit(FFN_BASE[n], NF - 1)
                pe.wait_ge(lo_ready, g + 4)
                pe.wait_ge(hlo_ready, NF * n + NF)
                down_unit((g + 3) % RING, (NF - 1) % 2, last_block=True)

            def s5_prepare():
                pe.wait_ge(matrices_ready, 1)
                pe.wait_ge(const_ready, 1)

                def turn(k):
                    for a in range(4):
                        mm = pe.transpose(mx[:, k % 2, P * a:P * (a + 1)], b_pow[:, k // 8, 4 * (k % 8) + a, :],
                                          ident[:, :])
                    mm.then_inc(turned, 1)

                for k in range(8):
                    if k >= 2:
                        pe.wait_ge((prep_dve, prep_act)[k % 2], k // 2)
                    turn(k)
                for k in range(8):
                    if k == 1:
                        pe.wait_ge(prep_act, 4)
                    else:
                        pe.wait_ge(prep_dve, 4 + max(k - 1, 0))
                    for a in range(4):
                        pair = 4 * k + a
                        for r in range(2):
                            pe.matmul(mx[0:CH, k % 2, P * a:P * a + CH], b_pow[:, r, pair, 3 * CH:4 * CH],
                                      c_zero[:, r, pair, :], start=a == 0 and r == 0, stop=False,
                                      skip_group_check=True)
                        for r in range(2):
                            pe.matmul(mx[0:CH, k % 2, P * a + CH:P * (a + 1)], b_pow[:, r, pair, 3 * CH:4 * CH],
                                      state_out[:, r, pair, 0:3 * CH], start=False, stop=False, skip_group_check=True)
                    mm = pe.matmul(mx[0:CH, k % 2, :].rearrange("p (a s) -> p a s", a=4)[:, :, 0:CH],
                                   ident[0:CH, 0:CH], skip_diag[:, 4 * k:4 * k + 4, :], start=False, stop=True,
                                   skip_group_check=True)
                    mm.then_inc(kernels_done, 1)
                for k in range(8, 16):
                    if k == 8:
                        pe.wait_ge(prep_dve, 11)
                    elif k % 2 == 0:
                        pe.wait_ge(prep_dve, 8 + k // 2)
                    elif k == 9:
                        pe.wait_ge(prep_dve, 12)
                    else:
                        pe.wait_ge(prep_act, k // 2)
                    turn(k)

            def s5_inflow(q):
                pe.wait_ge(u_ready, 2 * q + 2)
                if q >= 2:
                    pe.wait_ge(inflow_read, q - 1)
                bank = (gu, mx)[q % 2]
                for a in range(QP):
                    for r in range(2):
                        mm = pe.matmul(bank[:, r, CHUNKS * a:CHUNKS * (a + 1)], state_in[r][:, QP * q + a, :],
                                       u[:, QP * q + a, :], start=True, stop=True)
                mm.then_inc(inflow_done, 1)
                for a in range(QP):
                    mm = pe.matmul(y_of(q, a), u[:, QP * q + a, :], toep[:, QP * q + a, :],
                                   start=a % 4 == 0, stop=False, skip_group_check=True)
                mm.then_inc(own_done, 1)

            def y_of(q, a):
                rows = slice(CHUNKS * (a // 4), CHUNKS * (a // 4 + 1))
                return acc[rows, q, P * (a % 4):P * (a % 4 + 1)]

            def s5_outflow(q):
                pe.wait_ge(real_ready, q + 1)
                pe.wait_ge(imag_ready, q + 1)
                for a in range(QP):
                    for r in range(2):
                        state = (u[:, QP * q + a, :], state_im[:, q % 2, a, :])[r]
                        mm = pe.matmul(y_of(q, a), state, state_out[:, r, QP * q + a, :],
                                       start=False, stop=r == 1, skip_group_check=True)
                mm.then_inc(y_done, 1)

            def s5_turn(q):
                pe.wait_ge(z_ready, q + 1)
                zq = u[:, QP * q:QP * (q + 1), :].rearrange("p a c -> p (a c)")
                for j in range(STEPS):
                    mm = pe.transpose(acc[:, q, P * j:P * (j + 1)], zq[:, P * j:P * (j + 1)], ident[:, :])
                mm.then_inc(z_turned, 1)

            PASSES = ("hi*hi", "hi*lo", "lo*hi")

            def value_gate(cb, kbs, passes, first=False, last=False):
                n = S5_BASE + KB + 2 * cb
                for kb in kbs:
                    pe.wait_ge(m_hi_ready, kb + 1)
                    if "hi*lo" in passes:
                        pe.wait_ge(m_ready, kb + 1)
                    if kb == kbs[0]:
                        pe.wait_ge(lo_ready if "lo*hi" in passes else hi_ready, n + 2)
                    for r in range(2):
                        for p in passes:
                            w_, m_ = (w_lo if p[:2] == "lo" else w_hi), (m_lo if p[3:] == "lo" else m_hi)
                            w = w_[:, (n + r) % RING, P * kb:P * kb + P]
                            mm = pe.matmul(gu[:, cb % 2, SEQ * r:SEQ * (r + 1)], w, m_[:, kb, :],
                                           start=first and kb == kbs[0] and r == 0 and p == passes[0],
                                           stop=last and kb == kbs[-1] and p == passes[-1], skip_group_check=True)
                        if last and kb == kbs[-1]:
                            mm.then_inc(unit_done, 1)

            def s5_mixer():
                b = S5_BASE

                def project(k):
                    pe.wait_ge(lo_ready, b + k + 1)
                    column_unit(acc[:, k // 2, SEQ * (k % 2):SEQ * (k % 2 + 1)], (b + k) % RING)

                two_units(acc[:, 0, :], b, g_ready, KB, g_hi, g_lo)
                project(2)
                squares(1)
                project(3)
                project(4)
                project(5)
                project(6)
                s5_inflow(0)
                s5_inflow(1)
                project(7)
                s5_outflow(0)
                s5_inflow(2)
                s5_outflow(1)
                s5_inflow(3)
                s5_turn(0)
                s5_turn(1)
                s5_outflow(2)
                pe.wait_ge(inflow_read, 3)
                early, late = range(4), range(4, KB)
                value_gate(0, early, ("hi*hi", "lo*hi"), first=True)
                value_gate(1, early, ("hi*hi",), first=True)
                value_gate(0, early, ("hi*lo",))
                value_gate(1, early, ("hi*lo",))
                s5_turn(2)
                s5_outflow(3)
                s5_turn(3)
                value_gate(0, late, PASSES, last=True)
                value_gate(1, early, ("lo*hi",))
                value_gate(1, late, PASSES, last=True)
                for cb in range(2, KB):
                    n = b + KB + 2 * cb
                    pe.wait_ge(mix_read, cb - 1)
                    for r in range(2):
                        pe.wait_ge(lo_ready, n + r + 1)
                        output_unit(gu[:, cb % 2, SEQ * r:SEQ * (r + 1)], (n + r) % RING)

            def output_unit(dst, s):
                for kb in range(KB):
                    mm = three(dst, s, slice(P * kb, P * kb + P), m_hi[:, kb, :], m_lo[:, kb, :],
                               kb == 0, kb == KB - 1)
                mm.then_inc(unit_done, 1)

            def attention():
                b = ATT_BASE
                for kb in range(KB):
                    pe.wait_ge(lo_ready, b + kb + 1)
                    pe.wait_ge(g_ready, 4 * KB + kb + 1)
                    s = (b + kb) % RING
                    for t in range(2):
                        gh, gl = g_hi[:, kb, P * t:P * (t + 1)], g_lo[:, kb, P * t:P * (t + 1)]
                        for half in range(2):
                            if kb == 0:
                                pe.wait_ge(x_ready, 3 * KB + 2 * (2 * t + half) + 2)
                            cols = slice(512 * half, 512 * half + 512)
                            dst = acc[:, 2 * t + half, :]
                            pe.matmul(dst, gh, w_hi[:, s, cols], start=kb == 0, stop=False)
                            pe.matmul(dst, gh, w_lo[:, s, cols], start=False, stop=False)
                            mm = pe.matmul(dst, gl, w_hi[:, s, cols], start=False, stop=kb == KB - 1)
                    mm.then_inc(unit_done, 1)
                    if kb == 2:
                        squares(4)
                pe.wait_ge(rstd_ready, 5)
                for t in range(2):
                    mm = pe.matmul(mx[:, 0, t:t + 1], rstd[0:1, P * t:P * (t + 1)], ones[0:1, 0:1],
                                   start=True, stop=True)
                mm.then_inc(rcol_done, 1)

                def project(cb, r):
                    n = b + KB + 2 * cb + r
                    pe.wait_ge(lo_ready, n + 1)
                    if cb >= 2:
                        pe.wait_ge(qk_ready, cb - 1)
                    column_unit(gu[:, cb % 2, SEQ * r:SEQ * (r + 1)], n % RING)

                def logits(cb):
                    pe.wait_ge(qk_ready, cb + 1)
                    if cb == 0:
                        pe.wait_ge(rcol_ready, 1)
                    elif cb == 1:
                        pe.wait_ge(v_ready, 4)
                    else:
                        pe.wait_ge(wts_ready, cb - 1)
                    z = z_banks(cb)
                    for hh in range(2):
                        rows = slice(HEAD * hh, HEAD * (hh + 1))
                        q_, k_ = qk[rows, cb % 2, 0, :], qk[rows, cb % 2, 1, :]
                        pe.matmul(z[:, hh, 0:SEQ], k_[:, 0:P], q_, start=True, stop=False, skip_group_check=True)
                        mm = pe.matmul(z[:, hh, SEQ:384], k_[:, P:SEQ], q_[:, P:SEQ], start=False, stop=False,
                                       skip_group_check=True)
                    mm.then_inc(logits_done, 1)

                def arguments(cb):
                    pe.wait_ge(sp_ready, cb + 1)
                    z = z_banks(cb)
                    for hh in range(2):
                        args = [(z[:, hh, 0:P], ident_b[:, :], big_b[:, :]),
                                (z[:, hh, SEQ:384], ident_b[:, :], big_b[:, :])]
                        for s_ in (sp_hi[:, hh, :], sp_lo[:, hh, :]):
                            args += [(z[:, hh, 0:SEQ], ntri, s_[:, 0:SEQ]), (z[:, hh, P:SEQ], nones, s_[:, SEQ:384]),
                                     (z[:, hh, SEQ:384], ntri, s_[:, SEQ:384])]
                        for k, (dst, a, m_) in enumerate(args):
                            mm = pe.matmul(dst, a, m_, start=False, stop=k == len(args) - 1, skip_group_check=True)
                    mm.then_inc(arg_done, 1)

                def outputs(cb):
                    pe.wait_ge(wts_ready, cb + 1)
                    if cb >= 2:
                        pe.wait_ge(m_ready, KB + cb - 1)
                    for hh in range(2):
                        c0 = P * cb + HEAD * hh
                        dst = acc[HEAD * hh:HEAD * (hh + 1), cb % 2, 0:SEQ]
                        pe.matmul(dst, v[:, 0, c0:c0 + HEAD], wts[:, hh, 0:SEQ], start=True, stop=False,
                                  skip_group_check=True)
                        mm = pe.matmul(dst[:, P:SEQ], v[:, 1, c0:c0 + HEAD], wts[:, hh, SEQ:384], start=False,
                                       stop=True, skip_group_check=True)
                    mm.then_inc(o_done, 1)

                def first_outputs(pair, kbs):
                    n = b + 3 * KB + 2 * pair
                    pe.wait_ge(lo_ready, n + 2)
                    pe.wait_ge(qk_ready, KB)
                    if pair:
                        pe.wait_ge(wts_ready, KB - 1)
                    for kb in kbs:
                        pe.wait_ge(m_ready, KB + kb + 1)
                        for r in range(2):
                            mm = three(out_bank(2 * pair + r), (n + r) % RING, slice(P * kb, P * kb + P),
                                       m_hi[:, kb, :], m_lo[:, kb, :], kb == 0, kb == KB - 1, check=True)
                            if kb == KB - 1:
                                mm.then_inc(unit_done, 1)

                project(0, 0)
                project(0, 1)
                project(1, 0)
                logits(0)
                project(1, 1)
                project(2, 0)
                for cb in range(KB):
                    if cb + 1 < KB:
                        logits(cb + 1)
                    if cb + 2 < KB:
                        project(cb + 2, 1)
                    elif cb + 1 < KB:
                        first_outputs(0, range(2, 5))
                    else:
                        first_outputs(1, range(0, 6))
                    arguments(cb)
                    if cb + 3 < KB:
                        project(cb + 3, 0)
                    elif cb + 2 < KB:
                        first_outputs(0, range(0, 2))
                    elif cb + 1 < KB:
                        first_outputs(0, range(5, 6))
                    else:
                        first_outputs(0, range(6, 7))
                    outputs(cb)
                first_outputs(0, range(7, KB))
                first_outputs(1, range(6, KB))
                for cb in range(4, KB):
                    n = b + 3 * KB + cb
                    pe.wait_ge(lo_ready, n + 1)
                    pe.wait_ge(x_ready, 4 * KB + cb - 3)
                    output_unit(out_bank(cb), n % RING)

            def last_sum():
                for d in range(KB):
                    pe.wait_ge(sq_ready, 24 + d + 1)
                    mm = pe.matmul(mx[:, 1, 0:SEQ], ones[:, :], squares_out[:, d, :], start=d == 0, stop=d == KB - 1)
                mm.then_inc(sum_ready, 1)

            ffn_first(0, 0)
            ffn_second(0)
            ffn_loop(0, 0, PREP_TURN)
            s5_prepare()
            ffn_loop(0, PREP_TURN, TURNS)
            ffn_tail(0)
            s5_mixer()
            for n in (1, 2, 3):
                ffn_first(n, (2, 3, 5)[n - 1])
                ffn_second(n)
                ffn_loop(n, 0, TURNS)
                ffn_tail(n)
                if n == 2:
                    attention()
            last_sum()

        @block.gpsimd
        def _(pool):
            count = [0]

            def step(ins):
                count[0] += 1
                ins.then_inc(pool_step, 1)
                pool.wait_ge(pool_step, count[0])

            def norm(n):
                for p in range(1, KB // 2):
                    pool.wait_ge(sq_ready, 4 * n + p + 1)
                    if p > 1:
                        pool.wait_ge(sq_added, 3 * n + p - 1)
                    pool.tensor_tensor(ssq[:, :], ssq[:, :], two_squares(p), ALU.add).then_inc(sq_added, 1)

            def halves(fn):
                for g2 in range(2):
                    fn(slice(STATE * g2, STATE * (g2 + 1)), slice(GROUP * g2, GROUP * (g2 + 1)))

            def times(dst_re, dst_im, re, im, l_re, l_im, t, conj):
                tt = pool.tensor_tensor
                step(tt(t[0], re, l_re, ALU.mult))
                step(tt(t[1], im, l_im, ALU.mult))
                step(tt(dst_re, t[0], t[1], ALU.add if conj else ALU.subtract))
                step(tt(t[0], im, l_re, ALU.mult))
                step(tt(t[1], re, l_im, ALU.mult))
                step(tt(dst_im, t[0], t[1], ALU.subtract if conj else ALU.add))

            def s5_parameters():
                pr = lambda k: par[:, k, :]
                tt_ = lambda a, b_, c, op: pool.tensor_tensor(pr(a), pr(b_), pr(c), op)
                tt = lambda *o: step(tt_(*o))
                pool.wait_ge(s5_loaded, 16 * S5_ARRAYS)
                tt(18, 0, 0, ALU.mult)
                tt(19, 1, 1, ALU.mult)
                tt_(18, 18, 19, ALU.add).then_inc(par_ready, 1)
                pool.wait_ge(par_act, 1)
                tt(4, 0, 3, ALU.mult)
                tt_(5, 1, 3, ALU.mult).then_inc(par_ready, 1)
                pool.wait_ge(par_ready, 2)
                step(pool.tensor_scalar(par_i[:, :], pr(5), 1 / TWO_PI, None, ALU.mult))
                step(pool.tensor_copy(pr(10), par_i[:, :]))
                for c in (C1, C2, C3):
                    step(pool.tensor_scalar(pr(7), pr(10), c, None, ALU.mult))
                    tt(5, 5, 7, ALU.subtract)
                step(pool.tensor_scalar(pr(7), pr(5), 0.5, None, ALU.mult))
                step(pool.tensor_scalar(pr(8), pr(7), 0.0, 2.0, ALU.max, ALU.mult))
                tt(8, 8, 7, ALU.subtract)
                pool.tensor_scalar(pr(8), pr(8), -1.0, math.pi / 2, ALU.mult, ALU.add).then_inc(par_ready, 1)
                step(pool.memset(b_pow[:, 0], 0.0))
                step(pool.memset(c_zero, 0.0))
                pool.wait_ge(par_act, 4)
                tt(13, 9, 10, ALU.mult)
                step(pool.tensor_scalar(pr(13), pr(13), 2.0, None, ALU.mult))
                tt(12, 9, 9, ALU.mult)
                step(pool.tensor_scalar(pr(12), pr(12), -2.0, 1.0, ALU.mult, ALU.add))
                tt(14, 6, 12, ALU.mult)
                tt(15, 6, 13, ALU.mult)
                step(pool.tensor_scalar(pr(5), pr(14), -1.0, None, ALU.add))
                t = [pr(7), pr(8)]
                times(pr(16), pr(17), pr(5), pr(15), pr(0), pr(1), t, True)
                pool.wait_ge(par_dve, 1)
                tt(16, 16, 11, ALU.mult)
                tt(17, 17, 11, ALU.mult)
                for w, k, at, first in ((0, 16, STEPS - 1, -1), (1, 14, 0, 1)):
                    for r in range(2):
                        step(pool.tensor_copy(powers[:, w, r, :, at], pr(k + r)))
                    for _ in range(STEPS - 1):
                        src, dst = ([powers[:, w, r, :, j] for r in range(2)] for j in (at, at + first))
                        times(*dst, *src, pr(14), pr(15), t, False)
                        at += first
                tt(18, 6, 6, ALU.mult)
                tt(19, 18, 18, ALU.mult)
                src = (12, 13)
                for dst in [(12, 13)] + ROTATIONS:
                    tt(14, src[0], src[0], ALU.mult)
                    tt(15, src[1], src[1], ALU.mult)
                    tt(16, src[0], src[1], ALU.mult)
                    tt(dst[0], 14, 15, ALU.subtract)
                    step(pool.tensor_scalar(pr(dst[1]), pr(16), 2.0, None, ALU.mult))
                    src = dst

            def s5_matrices():
                tt = pool.tensor_tensor
                each = lambda raw_: raw_.unsqueeze(2).broadcast_to([P, PAIRS, STEPS, GROUP])
                power = lambda w, r: powers[:, w, r].unsqueeze(3).broadcast_to([P, PAIRS, STEPS, GROUP])
                step(pool.tensor_scalar(c_raw[:, 1], c_raw[:, 1], -1.0, None, ALU.mult))
                for r in range(2):
                    halves(lambda rows, cols: step(pool.tensor_copy(c_zero[rows, r, :, cols], c_raw[rows, r])))
                for w, src, dst in ((0, b_raw, b_pow), (1, c_raw, state_out)):
                    dst = dst.rearrange("p r a (j c) -> p r a j c", j=STEPS)
                    for r in range(2):
                        step(tt(prep_tmp[0], each(src[:, r]), power(w, 0), ALU.mult))
                        step(tt(prep_tmp[1], each(src[:, 1 - r]), power(w, 1), ALU.mult))
                        op = (ALU.subtract, ALU.add)[(r + w) % 2]
                        halves(lambda rows, cols: step(tt(dst[rows, r, :, :, cols], prep_tmp[0][rows],
                                                          prep_tmp[1][rows], op)))
                step(pool.tensor_tensor(skip_diag, ident[0:CH, 0:CH].unsqueeze(1).broadcast_to([CH, PAIRS, CH]),
                                        skip_col[0:CH, :].unsqueeze(2).broadcast_to([CH, PAIRS, CH]), ALU.mult))

            def s5_tables():
                pool.wait_ge(prep_dve, 16)
                pool.wait_ge(prep_act, 8)
                wide = lambda k, n: par[:, k, :].unsqueeze(2).broadcast_to([P, PAIRS, n])
                step(pool.memset(rot[:, 0, :, 0:1], 1.0))
                step(pool.memset(rot[:, 1, :, 0:1], 0.0))
                step(pool.tensor_scalar(rho, par[:, 19, :].unsqueeze(2).broadcast_to([P, PAIRS, CHUNKS]), 1.0, None,
                                        ALU.mult))
                step(pool.memset(rho[:, :, 0:1], 0.0))
                for k, step_ in enumerate(ROTATIONS):
                    n = 2 ** k
                    t = [rot_tmp[:, r, :, 0:n] for r in range(2)]
                    times(rot[:, 0, :, n:2 * n], rot[:, 1, :, n:2 * n], rot[:, 0, :, 0:n], rot[:, 1, :, 0:n],
                          wide(step_[0], n), wide(step_[1], n), t, False)

            def s5_imaginary(q):
                cos, sin = (rot[:, r, QP * q:QP * (q + 1), :] for r in range(2))
                vr, vi = (mod[:, k, :].rearrange("p (a c) -> p a c", a=QP) for k in (1, 3))
                pool.wait_ge(v_scanned, 2 * q + 1)
                pool.tensor_tensor(pool_tmp[:, 0], vr, sin, ALU.mult)
                pool.wait_ge(v_scanned, 2 * q + 2)
                step(pool.tensor_tensor(pool_tmp[:, 1], vi, cos, ALU.mult))
                pool.sem_inc(scan_read, 1)
                if q >= 2:
                    pool.wait_ge(y_done, q - 1)
                pool.tensor_tensor(state_im[:, q % 2, :, 1:CHUNKS], pool_tmp[:, 0, :, 0:CHUNKS - 1],
                                   pool_tmp[:, 1, :, 0:CHUNKS - 1], ALU.add).then_inc(imag_ready, 1)
                pool.wait_ge(imag_ready, q + 1)

            def attention_masks():
                pool.wait_ge(x_ready, 2 * KB)
                step(pool.memset(neg[:, 1, :], -1.0))
                step(pool.memset(keep[:, :], 1.0))
                step(pool.memset(big[:, :], 0.0))
                step(pool.affine_select(out=neg[:, 0, :], in_=neg[:, 1, :], compare_op=ALU.is_ge, fill=0.0, base=0,
                                        pattern=[[-1, P]], channel_multiplier=1))
                step(pool.tensor_copy(neg_r[:, :, :], neg[:, :, :]))
                step(pool.affine_select(out=keep[:, :], in_=keep[:, :], compare_op=ALU.is_gt, fill=0.0, base=0,
                                        pattern=[[1, P]], channel_multiplier=-1))
                step(pool.affine_select(out=big[:, :], in_=big[:, :], compare_op=ALU.is_gt, fill=NEG, base=0,
                                        pattern=[[1, P]], channel_multiplier=-1))
                step(pool.tensor_copy(ident_b[:, :], ident[:, :]))
                pool.tensor_copy(big_b[:, :], big[:, :]).then_inc(att_const, 1)

            step(pool.memset(ident[:, :], 0.0))
            step(pool.affine_select(out=ident[:, :], in_=ident[:, :], compare_op=ALU.not_equal, fill=1.0, base=0,
                                    pattern=[[-1, P]], channel_multiplier=1))
            pool.memset(ones[:, :], 1.0).then_inc(const_ready, 1)
            norm(0)
            s5_parameters()
            step(pool.memset(b_pow[:, 1], 0.0))
            step(pool.memset(state_out, 0.0))
            s5_matrices()
            pool.sem_inc(matrices_ready, 1)
            pool.memset(toep, 0.0).then_inc(zeroed, 1)
            s5_tables()
            step(pool.memset(state_im[:, :, :, 0:1], 0.0))
            pool.sem_inc(rot_ready, 1)
            norm(1)
            for q in range(QUARTERS):
                s5_imaginary(q)
            norm(2)
            attention_masks()
            for n in (3, 4, 5):
                norm(n)


PREP_TURN = 4


def lay_out(a):
    import numpy as np

    stream = np.empty((UNITS, P, D), np.float32)
    at = [0]

    def put(block):
        stream[at[0]] = block
        at[0] += 1

    def columns(w, c):
        put(w[:, P * c:P * (c + 1)].reshape(KB, P, P).transpose(1, 0, 2).reshape(P, D))

    def ffn(w_in, w_out):
        for f in range(NF):
            columns(w_in, f)
            columns(w_in, NF + f)
            if f:
                put(w_out[P * (f - 1):P * f])
        put(w_out[P * (NF - 1):])

    ffn(a["ffn1_w_in"][0], a["ffn1_w_out"][0])
    for c in range(KB):
        columns(a["s5_w_in"][0], c)
    for c in range(KB):
        columns(a["s5_w_out"][0], c)
        columns(a["s5_w_out"][0], KB + c)
    ffn(a["ffn2_w_in"][0], a["ffn2_w_out"][0])
    ffn(a["ffn1_w_in"][1], a["ffn1_w_out"][1])
    qkv = a["sb_w_qkv"][0]
    for k in range(KB):
        put(qkv[P * k:P * (k + 1), 2 * D:])
    for c in range(KB):
        columns(qkv, c)
        columns(qkv, KB + c)
    for c in range(KB):
        columns(a["sb_w_out"][0], c)
    ffn(a["ffn2_w_in"][1], a["ffn2_w_out"][1])

    def block_vector(g):
        return g.reshape(KB, P).T

    def states(m):
        m = m.reshape(PAIRS, 2, STATE, *m.shape[2:])
        return m.transpose(1, 2, 0, *range(3, m.ndim)).reshape(P, PAIRS, *m.shape[3:])

    gains = np.stack([block_vector(g) for g in (
        a["ffn1_norm"][0], a["mix_norm"][0], a["ffn2_norm"][0], a["ffn1_norm"][1], a["mix_norm"][1],
        a["ffn2_norm"][1], a["final_norm"])], axis=1)
    return {
        "x_in": a["x"][0].T.reshape(KB, P, SEQ).transpose(1, 0, 2),
        "gains": gains,
        "wstream": stream,
        "lam_re": states(a["s5_lam_re"][0]),
        "lam_im": states(a["s5_lam_im"][0]),
        "log_dt": a["s5_log_dt"][0].reshape(PAIRS, 2).T,
        "b_re": states(a["s5_b_re"][0]),
        "b_im": states(a["s5_b_im"][0]),
        "c_re": states(a["s5_c_re"][0].transpose(0, 2, 1)),
        "c_im": states(a["s5_c_im"][0].transpose(0, 2, 1)),
        "skip": np.concatenate([a["s5_d"][0].reshape(PAIRS, CH).T] * STEPS),
    }


def kernel(**inputs):
    import numpy as np
    import concourse.bacc as bacc
    from concourse.bass_utils import run_bass_kernel_spmd as run

    nc = bacc.Bacc("TRN2", target_bir_lowering=False, num_devices=1)
    arrays, args = {}, []
    for name, a in lay_out({k: np.asarray(v) for k, v in inputs.items()}).items():
        a = np.ascontiguousarray(a)
        arrays[f"{name}_dram"] = a
        args.append(nc.dram_tensor(f"{name}_dram", a.shape, mybir.dt.from_np(a.dtype), kind="ExternalInput").ap())
    out = nc.dram_tensor("out_dram", (P, KB, SEQ), F32, kind="ExternalOutput").ap()
    trunk(nc, *args, out)
    result = run(nc, [arrays], core_ids=[0]).results[0]["out_dram"]
    return result.transpose(1, 0, 2).reshape(1, D, SEQ).transpose(0, 2, 1)
```
